# Optimizing a Trainium2 kernel written in Bass

```python
import jax, jax.numpy as jnp
from jax import lax
import numpy as np

D_MODEL = 1024
BATCH = 1
SEQ = 512
DEPTH = 1
DEC_BATCH = 8
DEC_SEQ = 8
PAST_LEN = 2048
PAGE_SIZE = 128

D_MIX = D_MODEL
D_ATTN = D_MIX // 2
D_SSM = D_MIX - D_ATTN
V_HEAD = 64
MLA_HEADS = D_ATTN // V_HEAD
QK_NOPE = 64
QK_ROPE = 32
KV_LORA = D_MODEL // 4
Q_LORA = (3 * D_MODEL) // 8
ROPE_THETA = 10000.0
SSM_HEADDIM = 64
SSM_HEADS = D_SSM // SSM_HEADDIM
SSM_GROUPS = 2
D_STATE = 128
CONV_K = 4
CHUNK = 256
CONV_DIM = D_SSM + 2 * SSM_GROUPS * D_STATE
D_FF = 4 * D_MODEL
N_IN = Q_LORA + KV_LORA + QK_ROPE + D_SSM + CONV_DIM + SSM_HEADS
EPS = 1e-6
QBLOCK = 128

kernel_name = 'hymba_mla_ssd_decode_step'

def rmsnorm(x, g):
    xf = x.astype(jnp.float32)
    xf = xf * lax.rsqrt(jnp.mean(xf * xf, axis=-1, keepdims=True) + EPS)
    return (xf * g.astype(jnp.float32)).astype(x.dtype)

def rope_tables(pos):
    inv = ROPE_THETA ** (-(jnp.arange(0, QK_ROPE, 2, dtype=jnp.float32) / QK_ROPE))
    ang = pos.astype(jnp.float32)[:, None] * inv[None, :]
    return jnp.cos(ang), jnp.sin(ang)

def apply_rope(x, cos, sin):
    half = QK_ROPE // 2
    xf = x.astype(jnp.float32)
    x1, x2 = xf[..., :half], xf[..., half:]
    return jnp.concatenate([x1 * cos - x2 * sin, x2 * cos + x1 * sin], axis=-1).astype(x.dtype)

def mla_attend(q_abs, q_pe, c_kv, k_pe, q_pos, k_pos):
    b, lq, h, r = q_abs.shape
    qb = QBLOCK if lq % QBLOCK == 0 else lq
    nb = lq // qb
    scale = (QK_NOPE + QK_ROPE) ** -0.5
    qa = jnp.moveaxis(q_abs.reshape(b, nb, qb, h, r), 1, 0)
    qp = jnp.moveaxis(q_pe.reshape(b, nb, qb, h, QK_ROPE), 1, 0)
    qpos = q_pos.reshape(nb, qb)

    def block(args):
        qa_b, qp_b, pos_b = args
        s = (jnp.einsum('bqhr,bkr->bhqk', qa_b, c_kv) + jnp.einsum('bqhd,bkd->bhqk', qp_b, k_pe)).astype(jnp.float32) * scale
        mask = k_pos[None, :] <= pos_b[:, None]
        s = jnp.where(mask[None, None], s, -jnp.inf)
        p = jax.nn.softmax(s, axis=-1).astype(c_kv.dtype)
        return jnp.einsum('bhqk,bkr->bqhr', p, c_kv)

    out = lax.map(block, (qa, qp, qpos))
    return jnp.moveaxis(out, 0, 1).reshape(b, lq, h, r)

def ssd_chunked(x, dt, A, Bm, Cm, h0):
    b, L, H, P = x.shape
    G, N = Bm.shape[2], Bm.shape[3]
    E = H // G
    Q = min(CHUNK, L)
    pad = (-L) % Q
    x = x.astype(jnp.float32)
    dt = dt.astype(jnp.float32)
    Bm = Bm.astype(jnp.float32)
    Cm = Cm.astype(jnp.float32)
    if pad:
        x = jnp.pad(x, ((0, 0), (0, pad), (0, 0), (0, 0)))
        dt = jnp.pad(dt, ((0, 0), (0, pad), (0, 0)))
        Bm = jnp.pad(Bm, ((0, 0), (0, pad), (0, 0), (0, 0)))
        Cm = jnp.pad(Cm, ((0, 0), (0, pad), (0, 0), (0, 0)))
    nc = (L + pad) // Q
    xc = x.reshape(b, nc, Q, G, E, P)
    dtc = dt.reshape(b, nc, Q, G, E)
    Bc = Bm.reshape(b, nc, Q, G, N)
    Cc = Cm.reshape(b, nc, Q, G, N)
    acs = jnp.cumsum(dtc * A.astype(jnp.float32).reshape(G, E), axis=2)
    causal = jnp.tril(jnp.ones((Q, Q), dtype=bool))
    seg = acs[:, :, :, None] - acs[:, :, None, :]
    lmat = jnp.exp(jnp.where(causal[:, :, None, None], seg, -jnp.inf))
    x_dt = xc * dtc[..., None]
    cb = jnp.einsum('bcqgn,bcsgn->bcqsg', Cc, Bc)
    y_diag = jnp.einsum('bcqsge,bcsgep->bcqgep', cb[..., None] * lmat, x_dt)
    decay_to_end = jnp.exp(acs[:, :, -1:] - acs)
    chunk_states = jnp.einsum('bcsgn,bcsgep->bcgepn', Bc, x_dt * decay_to_end[..., None])
    chunk_decay = jnp.exp(acs[:, :, -1])

    def step(h, inp):
        dec, st = inp
        return dec[..., None, None] * h + st, h

    h_init = h0.astype(jnp.float32).reshape(b, G, E, P, N)
    h_final, h_prev = lax.scan(step, h_init, (jnp.moveaxis(chunk_decay, 1, 0), jnp.moveaxis(chunk_states, 1, 0)))
    h_prev = jnp.moveaxis(h_prev, 0, 1)
    y_off = jnp.einsum('bcqgn,bcgepn->bcqgep', Cc, h_prev) * jnp.exp(acs)[..., None]
    y = (y_diag + y_off).reshape(b, nc * Q, H, P)[:, :L]
    return y, h_final.reshape(b, H, P, N)

def mixer_block(x, c_past, kr_past, h0, conv_buf, norm_attn, w_in, q_norm, kv_norm, w_uq, w_uk, w_uv,
                conv_w, conv_b, dt_bias, a_log, d_skip, ssm_norm, w_out):
    b, L, _ = x.shape
    past_len = c_past.shape[1]
    h = rmsnorm(x, norm_attn)
    proj = jnp.einsum('bld,dn->bln', h, w_in)
    o1 = Q_LORA
    o2 = o1 + KV_LORA
    o3 = o2 + QK_ROPE
    o4 = o3 + D_SSM
    o5 = o4 + CONV_DIM
    q_lat, kv_lat, k_pe, z, xbc, dt_raw = jnp.split(proj, [o1, o2, o3, o4, o5], axis=-1)
    q_pos = past_len + jnp.arange(L, dtype=jnp.int32)
    cos, sin = rope_tables(q_pos)
    q = jnp.einsum('blr,rn->bln', rmsnorm(q_lat, q_norm), w_uq).reshape(b, L, MLA_HEADS, QK_NOPE + QK_ROPE)
    q_nope, q_pe = q[..., :QK_NOPE], q[..., QK_NOPE:]
    q_pe = apply_rope(q_pe, cos[:, None, :], sin[:, None, :])
    c_new = rmsnorm(kv_lat, kv_norm)
    kr_new = apply_rope(k_pe, cos, sin)
    q_abs = jnp.einsum('blhd,hdr->blhr', q_nope, w_uk)
    c_all = jnp.concatenate([c_past.astype(c_new.dtype), c_new], axis=1)
    kr_all = jnp.concatenate([kr_past.astype(kr_new.dtype), kr_new], axis=1)
    k_pos = jnp.arange(past_len + L, dtype=jnp.int32)
    o_lat = mla_attend(q_abs, q_pe, c_all, kr_all, q_pos, k_pos)
    o_attn = jnp.einsum('blhr,hrv->blhv', o_lat, w_uv).reshape(b, L, D_ATTN)
    xpad = jnp.concatenate([conv_buf.astype(xbc.dtype), xbc], axis=1)
    conv = conv_b
    for k in range(CONV_K):
        conv = conv + xpad[:, k:k + L] * conv_w[k]
    conv = jax.nn.silu(conv)
    conv_new = xpad[:, L:]
    xs, Bm, Cm = jnp.split(conv, [D_SSM, D_SSM + SSM_GROUPS * D_STATE], axis=-1)
    xs = xs.reshape(b, L, SSM_HEADS, SSM_HEADDIM)
    dt = jax.nn.softplus(dt_raw.astype(jnp.float32) + dt_bias.astype(jnp.float32))
    A = -jnp.exp(a_log.astype(jnp.float32))
    y, h_new = ssd_chunked(xs, dt, A, Bm.reshape(b, L, SSM_GROUPS, D_STATE), Cm.reshape(b, L, SSM_GROUPS, D_STATE), h0)
    y = y + d_skip.astype(jnp.float32)[:, None] * xs.astype(jnp.float32)
    g = y.reshape(b, L, D_SSM) * jax.nn.silu(z.astype(jnp.float32))
    g = g.reshape(b, L, SSM_GROUPS, D_SSM // SSM_GROUPS)
    g = g * lax.rsqrt(jnp.mean(g * g, axis=-1, keepdims=True) + EPS)
    o_ssm = (g.reshape(b, L, D_SSM) * ssm_norm.astype(jnp.float32)).astype(x.dtype)
    out = jnp.einsum('blm,md->bld', jnp.concatenate([o_attn, o_ssm], axis=-1), w_out)
    return out, c_new, kr_new, h_new.astype(h0.dtype), conv_new

def sq_relu_mlp(x, g, w_up, w_down):
    u = jax.nn.relu(jnp.einsum('bld,df->blf', rmsnorm(x, g), w_up))
    return jnp.einsum('blf,fd->bld', u * u, w_down)

def setup_inputs(seed: int = 0) -> dict:
    key = jax.random.key(seed)
    ks = jax.random.split(key, 32)
    n_pages = PAST_LEN // PAGE_SIZE
    used = DEC_BATCH * n_pages
    n_pool = used + used // 4
    f32 = jnp.float32

    def nrm(k, shape, scale):
        return jax.random.normal(k, shape, f32) * scale

    dt0 = jnp.exp(jax.random.uniform(ks[14], (DEPTH, SSM_HEADS), f32, np.log(1e-3), np.log(1e-1)))
    return {
        'x_prompt': nrm(ks[0], (BATCH, SEQ, D_MODEL), 1.0),
        'x_sample': nrm(ks[1], (DEC_BATCH, DEC_SEQ, D_MODEL), 1.0),
        'cache_kv_latent': nrm(ks[2], (DEPTH, n_pool, PAGE_SIZE, KV_LORA), 1.0),
        'cache_k_rope': nrm(ks[3], (DEPTH, n_pool, PAGE_SIZE, QK_ROPE), 1.0),
        'state_ssm': nrm(ks[4], (DEPTH, DEC_BATCH, SSM_HEADS, SSM_HEADDIM, D_STATE), 0.1),
        'state_conv': nrm(ks[5], (DEPTH, DEC_BATCH, CONV_K - 1, CONV_DIM), 1.0),
        'page_table': jax.random.permutation(ks[6], n_pool)[:used].reshape(DEC_BATCH, n_pages).astype(jnp.int32),
        'norm_attn': 1.0 + nrm(ks[7], (DEPTH, D_MODEL), 0.02),
        'w_in': nrm(ks[8], (DEPTH, D_MODEL, N_IN), D_MODEL ** -0.5),
        'q_norm': 1.0 + nrm(ks[9], (DEPTH, Q_LORA), 0.02),
        'kv_norm': 1.0 + nrm(ks[10], (DEPTH, KV_LORA), 0.02),
        'w_uq': nrm(ks[11], (DEPTH, Q_LORA, MLA_HEADS * (QK_NOPE + QK_ROPE)), Q_LORA ** -0.5),
        'w_uk': nrm(ks[12], (DEPTH, MLA_HEADS, QK_NOPE, KV_LORA), KV_LORA ** -0.5),
        'w_uv': nrm(ks[13], (DEPTH, MLA_HEADS, KV_LORA, V_HEAD), KV_LORA ** -0.5),
        'conv_w': nrm(ks[15], (DEPTH, CONV_K, CONV_DIM), CONV_K ** -0.5),
        'conv_b': nrm(ks[16], (DEPTH, CONV_DIM), 0.02),
        'dt_bias': dt0 + jnp.log(-jnp.expm1(-dt0)),
        'a_log': jnp.log(jax.random.uniform(ks[17], (DEPTH, SSM_HEADS), f32, 1.0, 16.0)),
        'd_skip': 1.0 + nrm(ks[18], (DEPTH, SSM_HEADS), 0.1),
        'ssm_norm': 1.0 + nrm(ks[19], (DEPTH, D_SSM), 0.02),
        'w_out': nrm(ks[20], (DEPTH, D_MIX, D_MODEL), D_MIX ** -0.5),
        'norm_mlp': 1.0 + nrm(ks[21], (DEPTH, D_MODEL), 0.02),
        'w_up': nrm(ks[22], (DEPTH, D_MODEL, D_FF), D_MODEL ** -0.5),
        'w_down': nrm(ks[23], (DEPTH, D_FF, D_MODEL), D_FF ** -0.5),
        'norm_final': 1.0 + nrm(ks[24], (D_MODEL,), 0.02),
    }

def reference(x_prompt, x_sample, cache_kv_latent, cache_k_rope, state_ssm, state_conv, page_table,
              norm_attn, w_in, q_norm, kv_norm, w_uq, w_uk, w_uv, conv_w, conv_b, dt_bias, a_log, d_skip,
              ssm_norm, w_out, norm_mlp, w_up, w_down, norm_final):
    bp = x_prompt.shape[0]
    bs, n_pages = page_table.shape
    page = cache_kv_latent.shape[2]
    xp, xs = x_prompt, x_sample
    ckv_p, ckr_p, ssm_p, conv_p = [], [], [], []
    ckv_s, ckr_s, ssm_s, conv_s = [], [], [], []
    for l in range(DEPTH):
        lw = (norm_attn[l], w_in[l], q_norm[l], kv_norm[l], w_uq[l], w_uk[l], w_uv[l], conv_w[l], conv_b[l],
              dt_bias[l], a_log[l], d_skip[l], ssm_norm[l], w_out[l])
        att, c_new, kr_new, h_new, cv_new = mixer_block(
            xp, jnp.zeros((bp, 0, KV_LORA), xp.dtype), jnp.zeros((bp, 0, QK_ROPE), xp.dtype),
            jnp.zeros((bp, SSM_HEADS, SSM_HEADDIM, D_STATE), xp.dtype), jnp.zeros((bp, CONV_K - 1, CONV_DIM), xp.dtype), *lw)
        xp = xp + att
        xp = xp + sq_relu_mlp(xp, norm_mlp[l], w_up[l], w_down[l])
        ckv_p.append(c_new); ckr_p.append(kr_new); ssm_p.append(h_new); conv_p.append(cv_new)
        c_past = cache_kv_latent[l][page_table].reshape(bs, n_pages * page, KV_LORA)
        kr_past = cache_k_rope[l][page_table].reshape(bs, n_pages * page, QK_ROPE)
        att, c_new, kr_new, h_new, cv_new = mixer_block(xs, c_past, kr_past, state_ssm[l], state_conv[l], *lw)
        xs = xs + att
        xs = xs + sq_relu_mlp(xs, norm_mlp[l], w_up[l], w_down[l])
        ckv_s.append(c_new); ckr_s.append(kr_new); ssm_s.append(h_new); conv_s.append(cv_new)
    y_prompt = rmsnorm(xp, norm_final)
    y_sample = rmsnorm(xs, norm_final)
    return (y_prompt, y_sample,
            jnp.stack(ckv_p), jnp.stack(ckr_p), jnp.stack(ssm_p), jnp.stack(conv_p),
            jnp.stack(ckv_s), jnp.stack(ckr_s), jnp.stack(ssm_s), jnp.stack(conv_s))


_drawn_inputs = setup_inputs


def setup_inputs(seed=0):
    import zlib

    import numpy as np

    out = dict(_drawn_inputs(seed))
    spreads = {}
    factors = {'cache_k_rope': 4.61,
     'q_norm': 8.0,
     'kv_norm': 2.73,
     'ssm_norm': 4.857,
     'norm_mlp': 3.357,
     'norm_final': 2.865}
    for name, (base, spread) in spreads.items():
        noise = np.random.default_rng([zlib.crc32(name.encode()), seed]).standard_normal(out[name].shape)
        drawn = base * np.exp(spread * noise) if base else spread * noise
        out[name] = __import__('jax').numpy.asarray(drawn.astype(out[name].dtype))
    for name, factor in factors.items():
        out[name] = (out[name] * factor).astype(out[name].dtype)
    return out
```

```python
import concourse.bass as bass
from concourse import mybir
from contextlib import ExitStack

P = 128
D = 1024
KT = D // P
TP, NB, TS = 512, 8, 8
SA = NB * TS
T = TP + SA
HALF = T // 2
QL, CL, RP = 384, 256, 32
H, DH = 8, 64
NST = 128
PAST, PAGE = 2048, 128
NPG = PAST // PAGE
POOL = 160
QT_N = TP // P
CONV_K = 4
EPS = 1e-6
SCALE = float(64 + RP) ** -0.5
NEG = -1e30

B_Q, B_KV, B_SP, B_X, B_Z, N_IN = 0, 3, 5, 6, 14, 18
B_OUT = N_IN
B_MLP = B_OUT + 8
N_BLK = B_MLP + 64
QUARTERS = 4

V_GATT, V_GQ, V_GKV, V_CW, V_CB, V_GS, V_GM, V_GF, V_D, V_DTB, V_AL, V_EPS, V_BM, V_QM = (
    0, 8, 11, 13, 45, 53, 57, 65, 73, 77, 78, 79, 80, 88)
NV = 92
C_ID, C_ONE, C_ROT, C_AM, C_TRI, C_NEG, C_SNEG, C_COS, C_SIN, C_SM, C_RST, C_REP, C_RREP = (
    0, 128, 256, 384, 512, 640, 768, 832, 1408, 1984, 2496, 3072, 3584)
NC_ = 3712

PADW = 3 + TP + NB * (3 + TS)
CW = PADW - 3
SB0 = 3 + TP
GOFF = [0, 512, 896, 1152, 1280]


def build(nc, wst, x_d, kv_d, kr_d, h0_d, sc_d, wuq_d, wukT_d, wuk_d, wuv_d, vec_d, con_d, pt_d,
          y_o, c_o, kr_o, sp_o, ss_o, cn_o):
    f32, f32r, i32 = mybir.dt.float32, mybir.dt.float32r, mybir.dt.int32
    ALU, ACT, AX = mybir.AluOpType, mybir.ActivationFunctionType, mybir.AxisListType
    ctx = ExitStack()
    with ctx:
        base = (nc.sbuf_base + 31) // 32 * 32
        room = nc.sbuf_usable_end - base

        def at(name, shape, off, dt=f32):
            size = 4
            for s in shape[1:]:
                size *= s
            assert off + size <= room, (name, off + size, room)
            return nc.alloc_sbuf_tensor_at(name, shape, dt, offset=base + off)

        made = {}

        def sem(name):
            if name not in made:
                made[name] = ctx.enter_context(nc.semaphore(name))
            return made[name]

        xT = at("xT", [P, KT, T], 0)
        h0T = at("h0T", [P, NB, 512], 0)
        catH = at("catH", [P, KT, T], 18432, f32r)
        catL = at("catL", [P, KT, T], 36864, f32r)
        wraw = [at(f"wraw{i}", [P, KT, P], 55296 + 4096 * i) for i in range(2)]
        whi = [at(f"whi{i}", [P, KT, P], 63488 + 4096 * i, f32r) for i in range(2)]
        wlo = [at(f"wlo{i}", [P, KT, P], 71680 + 4096 * i, f32r) for i in range(2)]
        con = at("con", [P, NC_], 79872)
        vec = at("vec", [P, NV], 94720)
        o = 95104
        qlat = at("qlat", [P, 3, T], o)
        cT = at("cT", [P, 2, T], o + 6912)
        wuq = at("wuq", [P, 3, 768], o + 11520)
        wukT = at("wukT", [P, 2, 512], o + 20736)
        wuk = at("wuk", [64, H, CL], o + 24832)
        wuv = at("wuv", [P, 2, 512], o + 33024)
        rx_o = o + 37120
        rx = at("rx", [P, T], rx_o)
        rq = at("rq", [P, T], o + 39424)
        rk = at("rk", [P, T], o + 41728)
        krR = at("krR", [P, T], o + 44032)
        pack = at("pack", [P, T], o + 46336)
        acs = at("acs", [P, T], o + 48640)
        pn = at("pn", [P, 5, 72], o + 50944)
        ptb = at("ptb", [1, NB * NPG], o + 52384, i32)
        r = o + 52896
        xc = at("xc", [P, KT, T], r)
        sqx = at("sqx", [P, KT, T], r)
        z = at("z", [P, 4, T], r + 18432)
        xnat = at("xnat", [P, 5, 512], r + 27648)
        bnat = at("bnat", [P, 5, 256], r + 37888)
        cbm = at("cbm", [P, 2, 1280], r + 43008)
        sqq = at("sqq", [P, 5, T], r + 37888)
        cbs = at("cbs", [64, 2, SA], r + 53248)
        pad = [at(f"pad{i}", [P, PADW], r + 53760 + 2432 * i) for i in range(2)]
        cacc = [at(f"cacc{i}", [P, PADW], r + 53760 + 4864 + 2432 * i) for i in range(2)]
        krw = at("krw", [P, T], r + 27648)
        t1 = at("t1", [P, T], r + 27648 + 2304)
        dw = [at(f"dw{i}", [P, T], r + 27648 + 4608 + 2304 * 0 + 2304 * i) for i in range(2)]
        cn = at("cn", [P, KT, 27], r + 63488)
        scv = at("scv", [P, KT, NB, 3], 0 + 16384)
        assert r + 64352 <= room, (r + 64352, room)
        ex = [at("ex0", [P, 1280], 18432), at("ex1", [P, 1280], 36864), at("ex2", [P, 1280], r + 53760)]
        dgn = [at(f"dgn{i}", [P, 4, P], 18432 + 5120 + 2048 * i) for i in range(2)]
        gs = at("gs", [64, H, SA], 36864 + 5120)
        se = at("se", [P, 320], r + 53760 + 5120)
        ysm = at("ysm", [P, 4, SA], r + 53760 + 6400)
        bms = at("bms", [64, NB, 256], 18432)
        spo = at("spo", [P, 512], 36864)
        rg = at("rg", [P, 2, T], r + 43008)
        QT = at("QT", [96, H, TP], r)
        KTt = at("KTt", [96, H, TP], r + 16384)
        V = at("V", [P, QT_N, 512], r + 32768)
        Pm = [at(f"Pm{i}", [P, 1280], r + 40960 + 5120 * i) for i in range(2)]
        PTm = [at(f"PTm{i}", [P, 1280], r + 51200 + 5120 * i) for i in range(2)]
        qp = at("qp", [P, 2, T], r + 40960)
        tq = [at(f"tq{i}", [P, 2, T], r + 51200 + 4608 * i) for i in range(2)]
        qs = at("qs", [64, H, SA], r + 61440)
        qrs = at("qrs", [P, 2, SA], r + 63488)
        mx = at("mx", [P, 24], rx_o)
        qabs = at("qabs", [P, 2, 512], o)
        qps = at("qps", [P, 512], o + 4096)
        snew = at("snew", [64, 512], o + 46336)
        c64 = at("c64", [64, 256], o + 50944)
        ckv = [at("ckv0", [P, NPG, CL], 0), at("ckv1", [P, NPG, CL], r)]
        ckr = [at("ckr0", [P, NPG, RP], 16384), at("ckr1", [P, NPG, RP], r + 16384)]
        CTr = at("CTr", [P, 2, PAST], r + 18432)
        KRr = at("KRr", [P, 4, P], r + 34816)
        sS = at("sS", [P, 1088], r + 36864)
        pS = at("pS", [P, 1088], r + 41216)
        mxs = at("mxs", [P, P], r + 48160)
        rm = at("rm", [SA, 1], r + 45824)
        dgm = at("dgm", [SA, SA], r + 45856)
        psm = at("psm", [P, SA], r + 46112)
        rsm = at("rsm", [P, SA], r + 46368)
        qab = at("qab", [P, 2, SA], r + 46624)
        qpb = at("qpb", [P, 4, SA], r + 47136)
        olat = at("olat", [P, 2, 512], o + 6912)
        x2H = at("x2H", [P, KT, T], o, f32r)
        x2L = at("x2L", [P, KT, T], o + 18432, f32r)
        uH = at("uH", [P, KT, T], o + 36864, f32r)
        uL = at("uL", [P, KT, T], o + 55296, f32r)
        ru = [at(f"ru{i}", [P, T], o + 73728 + 2304 * i) for i in range(2)]
        us = [at(f"us{i}", [P, T], o + 78336 + 2304 * i) for i in range(2)]
        r2 = at("r2", [P, T], o + 82944)
        r3 = at("r3", [P, T], o + 85248)
        sq2 = at("sq2", [P, KT, T], o + 87552)

        B = [ctx.enter_context(nc.psum_tensor(f"bank{i}", [P, 2, 512], f32)) for i in range(2)] + \
            [ctx.enter_context(nc.psum_tensor(f"bank{i}", [P, 512], f32)) for i in range(4, 8)]
        acc = [B[0], B[1]]
        b4, b5, b6, b7 = B[2:]

        ident = con[:, C_ID:C_ID + P]
        ones = con[:, C_ONE:C_ONE + P]
        rot = con[:, C_ROT:C_ROT + P]
        tri = con[:, C_TRI:C_TRI + P]
        neg = con[:, C_NEG:C_NEG + P]
        cosT = con[:, C_COS:C_COS + T]
        sinT = con[:, C_SIN:C_SIN + T]

        def halves(ap):
            return ap.rearrange("p (a n) -> p a n", a=2)

        def samp(ap, w=TS):
            return ap[:, SB0:SB0 + NB * (3 + TS)].rearrange("p (b w) -> p b w", w=3 + TS)

        block = ctx.enter_context(nc.Block())

        @block.sync
        def _(sp):
            def ring(g):
                if g >= 2:
                    sp.wait_ge(sem("w_split"), g - 1)
                sp.dma_start(wraw[g % 2][:], wst[g, :, :].rearrange("p (k n) -> p k n", k=KT)
                             ).then_inc(sem(f"w_arrived{g % 2}"), 16)

            for c in range(4):
                sp.dma_start(xT[:, 2 * c:2 * c + 2, :], x_d[:, 2 * c:2 * c + 2, :]).then_inc(sem(f"x_arrived{c}"), 16)
            for g in range(N_IN + 2):
                ring(g)

            def pages(b, u):
                for j in range(NPG):
                    page = sp.value_load(ptb[0:1, b * NPG + j:b * NPG + j + 1] if isinstance(b, int)
                                         else ptb[0:1, bass.ds(b * NPG + j, 1)], min_val=0, max_val=POOL - 1)
                    sp.dma_start(ckv[u][:, j, :], kv_d[bass.ds(page, 1), :, :].rearrange("a p n -> (a p) n")
                                 ).then_inc(sem(f"cache_arrived{u}"), 16)
                    sp.dma_start(ckr[u][:, j, :], kr_d[bass.ds(page, 1), :, :].rearrange("a p n -> (a p) n")
                                 ).then_inc(sem(f"cache_arrived{u}"), 16)

            sp.wait_ge(sem("pt_arrived"), 16)
            sp.wait_ge(sem("out_ss"), 16)
            pages(0, 0)
            sp.wait_ge(sem("o_mm"), H)
            pages(1, 1)
            with sp.Fori(1, 4) as i:
                for u in range(2):
                    sp.wait_ge(sem("pv_mm"), i * 2 + u - 1)
                    pages(i * 2 + u, u)
            sp.wait_ge(sem("pv_mm"), 7)
            sp.dma_start(xT[:], x_d).then_inc(sem("x_again"), 16)
            with sp.Fori((N_IN + 2) // 2, N_BLK // 2) as i:
                for u in range(2):
                    sp.wait_ge(sem("w_split"), i * 2 + u - 1)
                    sp.dma_start(wraw[u][:], wst[bass.ds(i * 2 + u, 1), :, :].rearrange("a p (k n) -> (a p) k n", k=KT)
                                 ).then_inc(sem(f"w_arrived{u}"), 16)
            for c in range(4):
                sp.wait_ge(sem("y_ready"), 2 * c + 2)
                sp.dma_start(y_o[:, 2 * c:2 * c + 2, :], sq2[:, 2 * c:2 * c + 2, :]).then_inc(sem("out_y"), 16)
            for name in ("out_c", "out_kr", "out_cn", "out_sp", "out_ss"):
                sp.wait_ge(sem(name), 16)
            sp.wait_ge(sem("out_y"), 64)

        @block.gpsimd
        def _(pool):
            def low(g):
                pool.wait_ge(sem("w_high"), g + 1)
                pool.tensor_tensor(wlo[g % 2][:], wraw[g % 2][:], whi[g % 2][:].bitcast(f32),
                                   ALU.subtract).then_inc(sem("w_split"), 1)

            pool.memset(pack[:], 0.0).then_inc(sem("pack_zero"), 1)
            for i in range(2):
                pool.memset(pad[i][:], 0.0).then_inc(sem("pad_zero"), 1)
            for g in range(N_IN + 2):
                low(g)
                if B_X <= g + 0 < B_X + KT:
                    c = g - B_X
                    if c == 0:
                        pool.wait_ge(sem("sc_arrived"), 16)
                        pool.wait_ge(sem("pad_zero"), 2)
                    if c >= 2:
                        pool.wait_ge(sem("conv_done"), c - 1)
                        pool.wait_ge(sem("cn_copied"), 2 * (c - 1))
                    pool.tensor_copy(samp(pad[c % 2])[:, :, 0:3], scv[:, c, :, :]).then_inc(sem("pad_state"), 1)
                if B_X <= g - 1 < B_X + KT:
                    c = g - 1 - B_X
                    pool.wait_ge(sem("pad_filled"), c + 1)
                    pool.tensor_copy(cn[:, c, 0:3], pad[c % 2][:, TP:TP + 3]).then_inc(sem("cn_copied"), 1)
                    pool.tensor_copy(cn[:, c, 3:27].rearrange("p (b w) -> p b w", w=3),
                                     samp(pad[c % 2])[:, :, TS:TS + 3]).then_inc(sem("cn_copied"), 1)

            pool.wait_ge(sem("xnat_ready"), 6)
            pool.wait_ge(sem("y_mm"), H)
            pool.wait_ge(sem("vec_arrived"), 16)
            for b in range(NB):
                pool.tensor_scalar(bms[:, b, :], bnat[0:SA, 4, :], vec[0:SA, V_BM + b:V_BM + b + 1], 1.0,
                                   ALU.mult, ALU.mult).then_inc(sem("bms_ready"), 1)
            for j in range(4):
                pool.wait_ge(sem("oh_ready"), j + 1)
                pool.tensor_tensor(catL[:, 4 + j, :], xc[:, j, :], catH[:, 4 + j, :].bitcast(f32), ALU.subtract
                                   ).then_inc(sem("ol_ready"), 1)
            pool.wait_ge(sem("kr_ready"), 1)
            pool.wait_ge(sem("q_evac"), 1)
            for h in range(H):
                m = pool.tensor_copy(KTt[64:96, h, :], krR[64:96, 0:TP])
            m.then_inc(sem("krope_ready"), 1)
            def spread(q):
                return pool.tensor_tensor(qpb[:], q.rearrange("p (a n) -> p a n", a=1).to_broadcast([P, 4, SA]),
                                          vec[:, V_QM:V_QM + 4].rearrange("p (a n) -> p a n", n=1)
                                          .to_broadcast([P, 4, SA]), ALU.mult)

            pool.wait_ge(sem("qabs_ready"), 2)
            pool.wait_ge(sem("qps_ready"), 1)
            pool.wait_ge(sem("attn_low"), 4)
            pool.tensor_copy(qab[:], qabs[:, :, 0:SA])
            spread(qps[:, 0:SA]).then_inc(sem("qb_ready"), 1)
            with pool.Fori(1, NB) as b:
                pool.wait_ge(sem("s_mm"), b)
                pool.tensor_copy(qab[:], qabs[:, :, bass.ds(b * SA, SA)])
                spread(qps[:, bass.ds(b * SA, SA)]).then_inc(sem("qb_ready"), 1)
            for d in range(KT):
                low(B_OUT + 2 + d)
                pool.wait_ge(sem("x2_squared"), d + 1)
                if d == 1:
                    pool.tensor_tensor(r2[:], sq2[:, 0, :], sq2[:, 1, :], ALU.add).then_inc(sem("pool_sum"), 1)
                elif d > 1:
                    pool.wait_ge(sem("pool_sum"), d - 1)
                    pool.tensor_tensor(r2[:], r2[:], sq2[:, d, :], ALU.add
                                       ).then_inc(sem("pool_sum" if d < KT - 1 else "x2_summed"), 1)
            pool.wait_ge(sem("x2_root"), 1)
            pool.tensor_copy(us[0][:, 0:1], vec[:, V_EPS:V_EPS + 1]).then_inc(sem("ul_ready"), 2)

            def low_at(g, u):
                pool.wait_ge(sem("w_high"), g + 1)
                pool.tensor_tensor(wlo[u][:], wraw[u][:], whi[u][:].bitcast(f32), ALU.subtract
                                   ).then_inc(sem("w_split"), 1)

            def low_hidden(n, u, slot):
                dst = uL[:, bass.ds(slot, 1), :].rearrange("p a n -> p (a n)")
                hi_ = uH[:, bass.ds(slot, 1), :].rearrange("p a n -> p (a n)").bitcast(f32)
                pool.wait_ge(sem("ru_free"), n + 3)
                pool.wait_ge(sem("uh_ready"), n + 1)
                pool.tensor_tensor(dst, us[u][:], hi_, ALU.subtract).then_inc(sem("ul_ready"), 1)

            def pool_quarter(q, last):
                g0 = q * 16 + B_MLP
                with pool.Fori(0, 4) as j:
                    for u in range(2):
                        low_at(g0 + 2 * j + 2 + u, u)
                        low_hidden(q * 8 + 2 * j + u, u, 2 * j + u)
                with pool.Fori(0, 3 if last else 4) as j:
                    for u in range(2):
                        low_at(g0 + 2 * j + 10 + u, u)

            with pool.Fori(0, QUARTERS - 1) as q:
                pool_quarter(q, False)
            pool_quarter(QUARTERS - 1, True)
            for d in range(KT):
                pool.wait_ge(sem("x3_squared"), d + 1)
                if d == 1:
                    pool.tensor_tensor(r2[:], sq2[:, 0, :], sq2[:, 1, :], ALU.add).then_inc(sem("pool_sum3"), 1)
                elif d > 1:
                    pool.wait_ge(sem("pool_sum3"), d - 1)
                    pool.tensor_tensor(r2[:], r2[:], sq2[:, d, :], ALU.add
                                       ).then_inc(sem("pool_sum3" if d < KT - 1 else "x3_summed"), 1)

        @block.scalar
        def _(act):
            chain = [0]

            def link(ins):
                chain[0] += 1
                ins.then_inc(sem("act_chain"), 1)
                act.wait_ge(sem("act_chain"), chain[0])

            def high(g):
                act.wait_ge(sem(f"w_arrived{g % 2}"), 16 * (g // 2 + 1))
                if g >= 2:
                    act.wait_ge(sem("gemm_done"), g - 1)
                act.activation(whi[g % 2][:], wraw[g % 2][:], ACT.Copy).then_inc(sem("w_high"), 1)

            act.dma_start(vec[:], vec_d).then_inc(sem("vec_arrived"), 16)
            act.dma_start(con[:], con_d).then_inc(sem("con_arrived"), 16)
            act.dma_start(wuq[:], wuq_d).then_inc(sem("wuq_arrived"), 16)
            act.dma_start(wukT[:], wukT_d).then_inc(sem("wukT_arrived"), 16)
            act.dma_start(wuk[:], wuk_d).then_inc(sem("wuk_arrived"), 16)
            act.dma_start(wuv[:], wuv_d).then_inc(sem("wuv_arrived"), 16)
            act.dma_start(ptb[:], pt_d).then_inc(sem("pt_arrived"), 16)
            for k in range(KT):
                if k % 2 == 0:
                    act.wait_ge(sem(f"x_arrived{k // 2}"), 16)
                act.activation(sqx[:, k, :], xT[:, k, :], ACT.Square).then_inc(sem("x_squared"), 1)
            high(0)
            high(1)
            act.wait_ge(sem("x_summed"), 1)
            act.wait_ge(sem("vec_arrived"), 16)
            act.activation(rx[:, 0:HALF], b4[:, 0:HALF], ACT.Sqrt, scale=1.0 / D, bias=vec[:, V_EPS:V_EPS + 1])
            act.activation(rx[:, HALF:T], b5[:, 0:HALF], ACT.Sqrt, scale=1.0 / D,
                           bias=vec[:, V_EPS:V_EPS + 1]).then_inc(sem("x_root"), 1)
            act.wait_ge(sem("x_split"), 2 * KT)
            act.wait_ge(sem("x_squared"), KT)
            act.dma_start(h0T[:], h0_d).then_inc(sem("h0_arrived"), 16)
            act.dma_start(scv[:], sc_d).then_inc(sem("sc_arrived"), 16)
            for g in range(2, N_IN + 2):
                high(g)
                if g == 4:
                    act.wait_ge(sem("evac"), 3)
                    act.wait_ge(sem("x_summed"), 1)
                    for i in range(3):
                        act.activation(sqq[:, i, :], qlat[:, i, :], ACT.Square).then_inc(sem("q_squared"), 1)
                if g == 6:
                    act.wait_ge(sem("evac"), 5)
                    for i in range(2):
                        act.activation(sqq[:, 3 + i, :], cT[:, i, :], ACT.Square).then_inc(sem("q_squared"), 1)
                if g == 7:
                    act.wait_ge(sem("q_summed"), 1)
                    act.activation(rq[:, 0:HALF], b4[:, 0:HALF], ACT.Sqrt, scale=1.0 / QL,
                                   bias=vec[:, V_EPS:V_EPS + 1])
                    act.activation(rq[:, HALF:T], b5[:, 0:HALF], ACT.Sqrt, scale=1.0 / QL,
                                   bias=vec[:, V_EPS:V_EPS + 1]).then_inc(sem("q_root"), 1)
                    act.wait_ge(sem("q_summed"), 2)
                    act.activation(rk[:, 0:HALF], b6[:, 0:HALF], ACT.Sqrt, scale=1.0 / CL,
                                   bias=vec[:, V_EPS:V_EPS + 1])
                    act.activation(rk[:, HALF:T], b7[:, 0:HALF], ACT.Sqrt, scale=1.0 / CL,
                                   bias=vec[:, V_EPS:V_EPS + 1]).then_inc(sem("q_root"), 1)
                    act.wait_ge(sem("evac"), B_SP + 1)
                    link(act.activation(dw[0][32:40, :], krw[32:40, :], ACT.Abs, bias=vec[32:40, V_DTB:V_DTB + 1]))
                    link(act.activation(dw[1][32:40, :], dw[0][32:40, :], ACT.Exp, scale=-1.0))
                    act.activation(dw[1][32:40, :], dw[1][32:40, :], ACT.Ln, bias=1.0).then_inc(sem("dt_ln"), 1)
                    act.activation(vec[32:40, V_AL:V_AL + 1], vec[32:40, V_AL:V_AL + 1], ACT.Exp
                                   ).then_inc(sem("dt_ln"), 1)
                if g == 9:
                    act.wait_ge(sem("dt_end"), 2)
                    act.activation(dw[1][32:40, :], dw[0][32:40, :], ACT.Exp).then_inc(sem("dt_decay"), 1)
                    act.wait_ge(sem("acs_ready"), 1)
                    act.activation(pack[96:104, :], acs[32:40, :], ACT.Exp).then_inc(sem("dt_decay"), 1)
                if g >= 9 and g - 9 < KT:
                    c = g - 9
                    act.wait_ge(sem("conv_done"), c + 1)
                    act.activation(xc[:, c, 0:TP], cacc[c % 2][:, 0:TP], ACT.Silu)
                    act.activation(xc[:, c, TP:T].rearrange("p (b w) -> p b w", w=TS),
                                   samp(cacc[c % 2])[:, :, 0:TS], ACT.Silu).then_inc(sem("silu_done"), 1)
            act.wait_ge(sem("c_ready"), 2)
            act.wait_ge(sem("kr_ready"), 1)
            act.wait_ge(sem("evac"), N_IN)
            act.activation(z[:], z[:], ACT.Silu).then_inc(sem("z_silu"), 1)
            act.wait_ge(sem("pn_ready"), 1)
            act.wait_ge(sem("conv_done"), KT)
            for h in range(H):
                act.wait_ge(sem("diag_ready"), h + 1)
                if h >= 3:
                    act.wait_ge(sem("y_mm"), h - 2)
                e = ex[h % 3]
                for i in range(4):
                    m = act.activation(e[:, GOFF[i]:GOFF[i] + P], dgn[h % 2][:, i, :], ACT.Exp,
                                       bias=pn[:, i, h:h + 1])
                    if i < 3:
                        m = act.activation(e[:, GOFF[i] + P:GOFF[i + 1]], acc[0][:, h % 2, P * i + P:TP], ACT.Exp,
                                           bias=pn[:, i, h:h + 1])
                m.then_inc(sem("ex_done"), 1)
            act.wait_ge(sem("sdiag_ready"), 1)
            act.activation(gs[:], gs[:], ACT.Exp).then_inc(sem("sex_done"), 1)
            for j in range(4):
                act.wait_ge(sem("gated"), j + 1)
                act.activation(z[:, j, :], xc[:, j, :], ACT.Square).then_inc(sem("g_squared"), 1)
            for c in range(2):
                act.wait_ge(sem("g_summed"), c + 1)
                for h in range(2):
                    bk = ((b4, b5), (b6, b7))[c][h]
                    m = act.activation(rg[:, c, h * HALF:(h + 1) * HALF], bk[:, 0:HALF], ACT.Sqrt,
                                       scale=1.0 / 256, bias=vec[:, V_EPS:V_EPS + 1])
                m.then_inc(sem("g_root"), 1)
            for j in range(4):
                act.wait_ge(sem("o_ready"), j + 1)
                act.activation(catH[:, 4 + j, :], xc[:, j, :], ACT.Copy).then_inc(sem("oh_ready"), 1)
            act.dma_start(c_o, cT[:]).then_inc(sem("out_c"), 16)
            act.dma_start(kr_o, krR[0:RP, :]).then_inc(sem("out_kr"), 16)
            act.wait_ge(sem("cn_copied"), 2 * KT)
            act.dma_start(cn_o, cn[:]).then_inc(sem("out_cn"), 16)
            act.wait_ge(sem("spo_ready"), 1)
            act.dma_start(sp_o, spo[:]).then_inc(sem("out_sp"), 16)
            act.wait_ge(sem("hn_ready"), NB)
            act.dma_start(ss_o, h0T[:]).then_inc(sem("out_ss"), 16)
            act.wait_ge(sem("q_evac"), 1)
            for u in range(8):
                act.wait_ge(sem("kv_mm"), u + 1)
                src = acc[u % 2][:, 0, :]
                if u < 4:
                    act.activation(KTt[0:64, 2 * u, :], src[0:64], ACT.Copy)
                    m = act.activation(KTt[0:64, 2 * u + 1, :], src[64:128], ACT.Copy)
                else:
                    m = act.activation(V[:, u - 4, :], src, ACT.Copy)
                m.then_inc(sem("kv_evac"), 1)

            def by_sequence(ap):
                return ap.rearrange("p (b h t) -> p h b t", b=NB, h=H)

            def by_head(ap):
                return ap.rearrange("p (h b t) -> p h b t", b=NB, h=H)

            act.wait_ge(sem("qps_mm"), 1)
            act.activation(by_sequence(qps[:]), by_head(b7[:]), ACT.Copy).then_inc(sem("qps_ready"), 1)
            act.wait_ge(sem("qabs_mm"), 1)
            for k in range(2):
                act.activation(by_sequence(qabs[:, k, :]), by_head(acc[0][:, k, :]), ACT.Copy
                               ).then_inc(sem("qabs_ready"), 1)
            act.wait_ge(sem("c64_mm"), 1)
            act.activation(c64[:], b4[0:SA, 0:256], ACT.Copy).then_inc(sem("c64_ready"), 1)

            sbank = [acc[0][:, 0, :], acc[0][:, 1, :], acc[1][:, 0, :], acc[1][:, 1, :]]
            off = [0, 128, 384, 768, 1280]

            def exps(h):
                c = 4 * (h % 2)
                act.wait_ge(sem("nm_ready"), h + 1)
                if h >= 2:
                    act.wait_ge(sem("pt_mm"), h - 1)
                for i in range(QT_N):
                    m = act.activation(Pm[h % 2][:, off[i]:off[i + 1]], sbank[i][:, 0:P * (i + 1)], ACT.Exp,
                                       bias=mx[:, 8 + c + i:9 + c + i], scale=SCALE,
                                       accum_out=mx[:, 16 + c + i:17 + c + i])
                m.then_inc(sem("p_exp"), 1)

            exps(0)
            for h in range(H):
                act.wait_ge(sem("pt_mm"), h + 1)
                if h >= 2:
                    act.wait_ge(sem("o_mm"), h - 1)
                act.activation(PTm[h % 2][:, 0:512], b4[:], ACT.Copy)
                act.activation(PTm[h % 2][:, 1024:1280], b6[:, 0:256], ACT.Copy).then_inc(sem("pt_act"), 1)
                if h + 1 < H:
                    exps(h + 1)
                if h % 2 == 1:
                    act.wait_ge(sem("o_mm"), h + 1)
                    act.activation(catH[:, h // 2, 0:TP], b7[:], ACT.Copy).then_inc(sem("attn_high"), 1)

            def ct_out(b, u, qs_, free):
                for q in qs_:
                    if q == 0 and free:
                        act.wait_ge(sem("s_mm"), b)
                    act.wait_ge(sem("ct_mm"), b * 9 + q + 1)
                    bk = (b4, b5)[(u + q) % 2]
                    if q < 8:
                        act.activation(CTr[:, :, 256 * q:256 * q + 256].rearrange("p k (t n) -> p t k n", n=P),
                                       bk[:].rearrange("p (t k n) -> p t k n", k=2, n=P), ACT.Copy
                                       ).then_inc(sem("ct_evac"), 1)
                    else:
                        act.activation(KRr[:].rearrange("p a n -> p (a n)"), bk[:], ACT.Copy
                                       ).then_inc(sem("ct_evac"), 1)

            def probs(b, u, nxt):
                if nxt:
                    ct_out(b + 1, 1 - u, range(9), True)
                act.wait_ge(sem("shift_ready"), b + 1)
                act.activation(pS[:, 0:1024], sS[:, 0:1024], ACT.Exp, scale=SCALE)
                act.activation(pS[0:SA, 1024:1088], sS[0:SA, 1024:1088], ACT.Exp, scale=SCALE
                               ).then_inc(sem("sp_exp"), 1)

            ct_out(0, 0, range(9), False)
            with act.Fori(0, 3) as i:
                for u in range(2):
                    probs(i * 2 + u, u, True)
            probs(6, 0, True)
            probs(7, 1, False)
            act.wait_ge(sem("os_mm"), 1)
            act.activation(catH[:, 0:4, TP:T], b5[:, 0:256].rearrange("p (a n) -> p a n", a=4), ACT.Copy
                           ).then_inc(sem("osh_ready"), 1)

            for d in range(KT):
                high(B_OUT + 2 + d)
                act.wait_ge(sem("evac"), B_OUT + d + 1)
                act.activation(sq2[:, d, :], xT[:, d, :], ACT.Square).then_inc(sem("x2_squared"), 1)
            act.wait_ge(sem("x2_sum_mm"), 1)
            act.activation(r3[:, 0:HALF], b4[:, 0:HALF], ACT.Sqrt, scale=1.0 / D, bias=vec[:, V_EPS:V_EPS + 1])
            act.activation(r3[:, HALF:T], b5[:, 0:HALF], ACT.Sqrt, scale=1.0 / D,
                           bias=vec[:, V_EPS:V_EPS + 1]).then_inc(sem("x2_root"), 1)
            act.activation(ru[0][:, 0:1], vec[:, V_EPS:V_EPS + 1], ACT.Copy).then_inc(sem("ru_free"), 2)

            def high_at(g, u, pair):
                act.wait_ge(sem(f"w_arrived{u}"), pair * 16 + 16)
                act.wait_ge(sem("gemm_done"), g - 1)
                act.activation(whi[u][:], wraw[u][:], ACT.Copy).then_inc(sem("w_high"), 1)

            def square(n, u, g):
                act.wait_ge(sem("evac"), g + 1)
                act.wait_ge(sem("ul_ready"), n + 1)
                act.activation(us[u][:], ru[u][:], ACT.Square).then_inc(sem("ru_free"), 1)

            def act_quarter(q, last):
                g0 = q * 16 + B_MLP
                with act.Fori(0, 4) as j:
                    for u in range(2):
                        high_at(g0 + 2 * j + 2 + u, u, q * 8 + j + B_MLP // 2 + 1)
                        square(q * 8 + 2 * j + u, u, g0 + 2 * j + u)
                with act.Fori(0, 3 if last else 4) as j:
                    for u in range(2):
                        high_at(g0 + 2 * j + 10 + u, u, q * 8 + j + B_MLP // 2 + 5)

            with act.Fori(0, QUARTERS - 1) as q:
                act_quarter(q, False)
            act_quarter(QUARTERS - 1, True)
            for d in range(KT):
                act.wait_ge(sem("evac"), N_BLK - 8 + d + 1)
                act.activation(sq2[:, d, :], xT[:, d, :], ACT.Square).then_inc(sem("x3_squared"), 1)
            act.wait_ge(sem("x3_sum_mm"), 1)
            act.activation(r3[:, 0:HALF], b4[:, 0:HALF], ACT.Sqrt, scale=1.0 / D, bias=vec[:, V_EPS:V_EPS + 1])
            act.activation(r3[:, HALF:T], b5[:, 0:HALF], ACT.Sqrt, scale=1.0 / D,
                           bias=vec[:, V_EPS:V_EPS + 1]).then_inc(sem("x3_root"), 1)

        @block.vector
        def _(dve):
            chain = [0]

            def link(ins):
                chain[0] += 1
                ins.then_inc(sem("dve_chain"), 1)
                dve.wait_ge(sem("dve_chain"), chain[0])

            dve.wait_ge(sem("vec_arrived"), 16)
            for k in range(KT):
                if k % 2 == 0:
                    dve.wait_ge(sem(f"x_arrived{k // 2}"), 16)
                g = vec[:, V_GATT + k:V_GATT + k + 1]
                dve.tensor_scalar(catH[:, k, :], xT[:, k, :], g, None, ALU.mult).then_inc(sem("x_split"), 1)
                dve.wait_ge(sem("x_split"), 2 * k + 1)
                dve.scalar_tensor_tensor(catL[:, k, :], xT[:, k, :], g, catH[:, k, :].bitcast(f32),
                                         ALU.mult, ALU.subtract).then_inc(sem("x_split"), 1)
            dve.wait_ge(sem("x_root"), 1)
            dve.reciprocal(rx[:], rx[:]).then_inc(sem("rx_ready"), 1)
            dve.wait_ge(sem("rx_ready"), 1)

            def evac(g, out):
                dve.wait_ge(sem("gemm_done"), g + 1)
                return dve.tensor_tensor(out, acc[g % 2][:, :, 0:HALF], halves(rx[:]), ALU.mult)

            for g in range(N_IN):
                if g < B_KV:
                    evac(g, halves(qlat[:, g, :])).then_inc(sem("evac"), 1)
                elif g < B_SP:
                    evac(g, halves(cT[:, g - B_KV, :])).then_inc(sem("evac"), 1)
                elif g == B_SP:
                    dve.wait_ge(sem("gemm_done"), g + 1)
                    dve.tensor_tensor(halves(krw[0:64, :]), acc[g % 2][0:64, :, 0:HALF], halves(rx[0:64, :]),
                                      ALU.mult).then_inc(sem("evac"), 1)
                    dve.wait_ge(sem("evac"), g + 1)
                    dve.wait_ge(sem("vec_arrived"), 16)
                    b = vec[32:40, V_DTB:V_DTB + 1]
                    dve.tensor_scalar(acs[32:40, :], krw[32:40, :], b, 0.0, ALU.add, ALU.max
                                      ).then_inc(sem("dt_pos"), 1)
                elif g < B_Z:
                    c = g - B_X
                    p_, q_ = pad[c % 2], cacc[c % 2]
                    dve.wait_ge(sem("gemm_done"), g + 1)
                    if c >= 2:
                        dve.wait_ge(sem("cn_copied"), 2 * (c - 1))
                        dve.wait_ge(sem("silu_done"), c - 1)
                    else:
                        dve.wait_ge(sem("pad_zero"), 2)
                    A = acc[g % 2]
                    dve.tensor_tensor(p_[:, 3:3 + HALF], A[:, 0, 0:HALF], rx[:, 0:HALF], ALU.mult)
                    dve.tensor_tensor(p_[:, 3 + HALF:3 + TP], A[:, 1, 0:TP - HALF], rx[:, HALF:TP], ALU.mult)
                    dve.tensor_tensor(samp(p_)[:, :, 3:3 + TS],
                                      A[:, 1, TP - HALF:HALF].rearrange("p (b w) -> p b w", w=TS),
                                      rx[:, TP:T].rearrange("p (b w) -> p b w", w=TS),
                                      ALU.mult).then_inc(sem("pad_filled"), 1)
                    dve.wait_ge(sem("pad_filled"), c + 1)
                    dve.wait_ge(sem("pad_state"), c + 1)
                    w = [vec[:, V_CW + CONV_K * c + k:V_CW + CONV_K * c + k + 1] for k in range(CONV_K)]
                    ins = dve.tensor_scalar(q_[:, 0:CW], p_[:, 0:CW], w[0], vec[:, V_CB + c:V_CB + c + 1],
                                            ALU.mult, ALU.add)
                    ins.then_inc(sem("evac"), 1)
                    dve.wait_ge(sem("evac"), g + 1)
                    for k in (1, 2):
                        link(dve.scalar_tensor_tensor(q_[:, 0:CW], p_[:, k:k + CW], w[k], q_[:, 0:CW],
                                                      ALU.mult, ALU.add))
                    dve.scalar_tensor_tensor(q_[:, 0:CW], p_[:, 3:3 + CW], w[3], q_[:, 0:CW],
                                             ALU.mult, ALU.add).then_inc(sem("conv_done"), 1)
                else:
                    evac(g, halves(z[:, g - B_Z, :])).then_inc(sem("evac"), 1)
                if g == 6:
                    dve.wait_ge(sem("q_squared"), 3)
                    for i in range(3):
                        dve.tensor_scalar(qlat[:, i, :], qlat[:, i, :], vec[:, V_GQ + i:V_GQ + i + 1], None,
                                          ALU.mult).then_inc(sem("qg_ready"), 1)
                    dve.wait_ge(sem("q_root"), 1)
                    dve.reciprocal(rq[:], rq[:]).then_inc(sem("rq_ready"), 1)
                    dve.wait_ge(sem("dt_ln"), 2)
                    dve.wait_ge(sem("dt_pos"), 1)
                    dve.wait_ge(sem("pack_zero"), 1)
                    link(dve.tensor_tensor(pack[32:40, :], acs[32:40, :], dw[1][32:40, :], ALU.add))
                    link(dve.tensor_scalar(dw[0][32:40, :], pack[32:40, :], vec[32:40, V_AL:V_AL + 1], -1.0,
                                           ALU.mult, ALU.mult))
                    dve.wait_ge(sem("con_arrived"), 16)
                    dve.tensor_tensor_scan(acs[32:40, :], con[32:40, C_RST:C_RST + T], dw[0][32:40, :], 0.0,
                                           ALU.mult, ALU.add).then_inc(sem("acs_ready"), 1)
                    dve.wait_ge(sem("acs_ready"), 1)
                    dve.tensor_scalar(pack[0:8, :], acs[32:40, :], -1.0, None, ALU.mult)
                    dve.tensor_scalar(dw[0][32:40, 0:TP], acs[32:40, 0:TP], -1.0, acs[32:40, TP - 1:TP],
                                      ALU.mult, ALU.add).then_inc(sem("dt_end"), 1)
                    sa = acs[32:40, TP:T].rearrange("p (b w) -> p b w", w=TS)
                    dve.tensor_tensor(dw[0][32:40, TP:T].rearrange("p (b w) -> p b w", w=TS),
                                      sa[:, :, TS - 1:TS].to_broadcast([8, NB, TS]), sa,
                                      ALU.subtract).then_inc(sem("dt_end"), 1)
                if g == 7:
                    dve.wait_ge(sem("q_root"), 2)
                    dve.wait_ge(sem("q_squared"), 5)
                    link(dve.reciprocal(rk[:], rk[:]))
                    for i in range(2):
                        dve.scalar_tensor_tensor(cT[:, i, :], cT[:, i, :], vec[:, V_GKV + i:V_GKV + i + 1],
                                                 rk[:], ALU.mult, ALU.mult).then_inc(sem("c_ready"), 1)
                if g == 8:
                    dve.wait_ge(sem("dt_decay"), 1)
                    dve.tensor_tensor(pack[64:72, :], pack[32:40, :], dw[1][32:40, :], ALU.mult
                                      ).then_inc(sem("pack_ready"), 1)
                    dve.wait_ge(sem("kr_mm"), 1)
                    dve.tensor_tensor(t1[:, 0:HALF], b4[:, 0:HALF], cosT[:, 0:HALF], ALU.mult)
                    link(dve.tensor_tensor(t1[:, HALF:T], b5[:, 0:HALF], cosT[:, HALF:T], ALU.mult))
                    dve.tensor_tensor(krR[:, 0:HALF], b6[:, 0:HALF], sinT[:, 0:HALF], ALU.mult)
                    link(dve.tensor_tensor(krR[:, HALF:T], b7[:, 0:HALF], sinT[:, HALF:T], ALU.mult))
                    dve.tensor_tensor(krR[:], krR[:], t1[:], ALU.add).then_inc(sem("kr_ready"), 1)
                if g == 10:
                    dve.wait_ge(sem("pack_tr"), 1)
                    dve.tensor_copy(pn[:, 0:4, :].rearrange("p a b -> p (a b)"), b4[:, 0:288])
                    dve.tensor_copy(pn[0:SA, 4, :], b4[0:SA, 288:360]).then_inc(sem("pn_ready"), 1)
                if g >= 11 and g - 11 < 6:
                    c = g - 11
                    dve.wait_ge(sem("x_tr"), c + 1)
                    dst = xnat[:, :, c * P:(c + 1) * P] if c < 4 else bnat[:, :, (c - 4) * P:(c - 3) * P]
                    bk = b5 if c % 2 == 0 else b6
                    dve.tensor_copy(dst[:, 0:4, :], bk[:].rearrange("p (a n) -> p a n", a=4))
                    dve.tensor_copy(dst[0:SA, 4, :], b7[0:SA, 0:P]).then_inc(sem("xnat_ready"), 1)
            for c in range(2):
                dve.wait_ge(sem("cb_mm"), c + 1)
                for i, (bk, off) in enumerate(((b4, 0), (b5, 0), (b6, 0), (b5, 384))):
                    dve.tensor_tensor(cbm[:, c, GOFF[i]:GOFF[i] + P], bk[:, off:off + P], tri, ALU.mult)
                    if i < 3:
                        dve.tensor_copy(cbm[:, c, GOFF[i] + P:GOFF[i + 1]], bk[:, off + P:off + TP - P * i])
                dve.tensor_copy(cbs[:, c, :], b6[0:SA, 256:256 + SA]).then_inc(sem("cb_ready"), 1)

            def diag_rows(h):
                dve.wait_ge(sem("rows_done"), h + 1)
                if h >= 2:
                    dve.wait_ge(sem("ex_done"), h - 1)
                dve.tensor_tensor(dgn[h % 2][:], acc[0][:, h % 2, :].rearrange("p (a n) -> p a n", a=4),
                                  neg.rearrange("p (a n) -> p a n", a=1).to_broadcast([P, 4, P]),
                                  ALU.add).then_inc(sem("diag_ready"), 1)

            def take_y(j):
                dve.wait_ge(sem("y_mm"), 2 * j + 2)
                dve.scalar_tensor_tensor(xc[:, j, 0:TP], xc[:, j, 0:TP], vec[:, V_D + j:V_D + j + 1],
                                         acc[1][:, j % 2, :], ALU.mult, ALU.add).then_inc(sem("y_taken"), 1)

            dve.wait_ge(sem("cb_ready"), 2)
            dve.wait_ge(sem("pn_ready"), 1)
            diag_rows(0)
            for h in range(H):
                if h + 1 < H:
                    diag_rows(h + 1)
                dve.wait_ge(sem("ex_done"), h + 1)
                e = ex[h % 3]
                for i in range(4):
                    sl = slice(GOFF[i], GOFF[i + 1])
                    m = dve.scalar_tensor_tensor(e[:, sl], e[:, sl], pn[:, i, 32 + h:33 + h],
                                                 cbm[:, h // 4, sl], ALU.mult, ALU.mult)
                m.then_inc(sem("mix_ready"), 1)
                if h >= 3 and h % 2 == 1:
                    take_y(h // 2 - 1)
            dve.wait_ge(sem("srows_done"), 1)

            def heads(ap):
                return ap.rearrange("p (h n) -> p h n", n=1).to_broadcast([SA, H, SA])

            link(dve.tensor_tensor(gs[:], b4[0:SA, :].rearrange("p (h n) -> p h n", h=H),
                                   con[0:SA, C_SNEG:C_SNEG + SA].rearrange("p (a n) -> p a n", a=1)
                                   .to_broadcast([SA, H, SA]), ALU.add))
            dve.tensor_tensor(gs[:], gs[:], heads(pn[0:SA, 4, 0:8]), ALU.add).then_inc(sem("sdiag_ready"), 1)
            take_y(3)
            dve.wait_ge(sem("se_mm"), 1)
            dve.wait_ge(sem("mix_ready"), H)
            link(dve.tensor_copy(se[:], b7[:, 0:320]))
            dve.wait_ge(sem("sex_done"), 1)
            link(dve.tensor_tensor(gs[:], gs[:], heads(pn[0:SA, 4, 32:40]), ALU.mult))
            dve.tensor_tensor(gs[:].rearrange("p (g e) n -> p g e n", g=2),
                              gs[:].rearrange("p (g e) n -> p g e n", g=2),
                              cbs[:].rearrange("p g (a n) -> p g a n", a=1).to_broadcast([SA, 2, 4, SA]),
                              ALU.mult).then_inc(sem("smix_ready"), 1)
            dve.wait_ge(sem("yo_mm"), 1)
            link(dve.tensor_tensor(ysm[:].rearrange("p a n -> p (a n)"), b6[:, 0:256], se[:, 0:256], ALU.mult))
            dve.wait_ge(sem("ys_mm"), 1)
            dve.tensor_tensor(xnat[:, 0:4, :].rearrange("p a (h n) -> p a h n", h=H),
                              xnat[:, 0:4, :].rearrange("p a (h n) -> p a h n", h=H),
                              pn[:, 0:4, 64:72].rearrange("p a (h n) -> p a h n", n=1)
                              .to_broadcast([P, 4, H, DH]), ALU.mult).then_inc(sem("xdd_ready"), 1)
            dve.tensor_tensor(xnat[0:SA, 4, :].rearrange("p (h n) -> p h n", h=H),
                              xnat[0:SA, 4, :].rearrange("p (h n) -> p h n", h=H),
                              pn[0:SA, 4, 64:72].rearrange("p (h n) -> p h n", n=1)
                              .to_broadcast([SA, H, DH]), ALU.mult).then_inc(sem("xdd_ready"), 1)
            link(dve.tensor_tensor(ysm[:].rearrange("p a n -> p (a n)"), b5[:, 0:256],
                                   ysm[:].rearrange("p a n -> p (a n)"), ALU.add))
            for j in range(4):
                m = dve.scalar_tensor_tensor(xc[:, j, TP:T], xc[:, j, TP:T], vec[:, V_D + j:V_D + j + 1],
                                             ysm[:, j, :], ALU.mult, ALU.add)
            m.then_inc(sem("ys_taken"), 1)
            dve.wait_ge(sem("ys_taken"), 1)
            dve.wait_ge(sem("y_taken"), 4)
            dve.wait_ge(sem("z_silu"), 1)
            for j in range(4):
                dve.tensor_tensor(xc[:, j, :], xc[:, j, :], z[:, j, :], ALU.mult).then_inc(sem("gated"), 1)
            for b in range(NB):
                hb = h0T[:, b, :].rearrange("p (h n) -> p h n", h=H)
                if b == 0:
                    dve.wait_ge(sem("h0_arrived"), 16)
                link(dve.tensor_tensor(hb, hb, se[:, 256 + b:320:NB].rearrange("p (h n) -> p h n", n=1)
                                       .to_broadcast([P, H, DH]), ALU.mult))
                dve.wait_ge(sem("hn_mm"), b + 1)
                dve.tensor_tensor(h0T[:, b, :], h0T[:, b, :], acc[1][:, b % 2, :], ALU.add
                                  ).then_inc(sem("hn_ready"), 1)
                if b == 0:
                    dve.wait_ge(sem("sp_mm"), 1)
                    dve.tensor_copy(spo[:], acc[0][:, 0, :]).then_inc(sem("spo_ready"), 1)
            for c in range(2):
                dve.wait_ge(sem("g_root"), c + 1)
                link(dve.reciprocal(rg[:, c, :], rg[:, c, :]))
                for i in range(2):
                    j = 2 * c + i
                    dve.scalar_tensor_tensor(xc[:, j, :], xc[:, j, :], vec[:, V_GS + j:V_GS + j + 1],
                                             rg[:, c, :], ALU.mult, ALU.mult).then_inc(sem("o_ready"), 1)
            dve.wait_ge(sem("oh_ready"), 4)
            dve.wait_ge(sem("ol_ready"), 4)
            dve.wait_ge(sem("rq_ready"), 1)
            for u in range(6):
                dve.wait_ge(sem("q_mm"), u + 1)
                pr, sa = acc[u % 2][:, 0, :], acc[u % 2][:, 1, 0:SA]
                if u < 4:
                    for e in range(2):
                        rows = slice(64 * e, 64 * e + 64)
                        dve.tensor_tensor(QT[0:64, 2 * u + e, :], pr[rows], rq[rows, 0:TP], ALU.mult)
                        m = dve.tensor_tensor(qs[:, 2 * u + e, :], sa[rows], rq[rows, TP:T], ALU.mult)
                else:
                    dve.tensor_tensor(qp[:, u - 4, 0:TP], pr, rq[:, 0:TP], ALU.mult)
                    m = dve.tensor_tensor(qp[:, u - 4, TP:T], sa, rq[:, TP:T], ALU.mult)
                m.then_inc(sem("q_evac"), 1)
            dve.wait_ge(sem("q_evac"), 6)

            def both(ap):
                return ap.rearrange("p (a n) -> p a n", a=1).to_broadcast([P, 2, ap.shape[1]])

            dve.tensor_tensor(tq[0][:], qp[:], both(cosT), ALU.mult)
            dve.wait_ge(sem("rot_mm"), 1)
            for i in range(2):
                dve.tensor_tensor(tq[1][:, i, 0:TP], (b4, b5)[i][:], sinT[:, 0:TP], ALU.mult)
            link(dve.tensor_tensor(tq[1][:, :, TP:T], b6[:, 0:2 * SA].rearrange("p (a n) -> p a n", a=2),
                                   both(sinT[:, TP:T]), ALU.mult))
            dve.wait_ge(sem("out_cn"), 16)
            dve.tensor_tensor(qrs[:], tq[0][:, :, TP:T], tq[1][:, :, TP:T], ALU.add).then_inc(sem("qrs_ready"), 1)
            for h in range(H):
                rows = slice(RP * (h % 4), RP * (h % 4) + RP)
                dve.tensor_tensor(QT[64:96, h, :], tq[0][rows, h // 4, 0:TP], tq[1][rows, h // 4, 0:TP],
                                  ALU.add).then_inc(sem("qrope_ready"), 1)
            dve.wait_ge(sem("snew_mm"), 1)
            dve.tensor_tensor(snew[:], b5[0:SA, :], con[0:SA, C_SM:C_SM + 512], ALU.add
                              ).then_inc(sem("snew_ready"), 1)

            sbank = [acc[0][:, 0, :], acc[0][:, 1, :], acc[1][:, 0, :], acc[1][:, 1, :]]
            am = con[:, C_AM:C_AM + P]

            def maxima(h):
                c = 4 * (h % 2)
                for i in range(QT_N):
                    dve.wait_ge(sem("score_mm"), 4 * h + i + 1)
                    dve.tensor_tensor(sbank[i][:, P * i:P * i + P], sbank[i][:, P * i:P * i + P], am, ALU.add
                                      ).then_inc(sem("score_masked"), 1)
                for i in range(QT_N):
                    dve.wait_ge(sem("score_masked"), 4 * h + i + 1)
                    m = dve.reduce_max(mx[:, c + i:c + i + 1], sbank[i][:, 0:P * (i + 1)], AX.X, negate=True)
                link(m)
                dve.tensor_scalar(mx[:, 8 + c:12 + c], mx[:, c:c + 4], SCALE, None, ALU.mult
                                  ).then_inc(sem("nm_ready"), 1)

            maxima(0)
            off = [0, 128, 384, 768, 1280]
            for h in range(H):
                c = 16 + 4 * (h % 2)
                dve.wait_ge(sem("p_exp"), h + 1)
                link(dve.reciprocal(mx[:, c:c + 4], mx[:, c:c + 4]))
                for i in range(QT_N):
                    sl = Pm[h % 2][:, off[i]:off[i + 1]]
                    m = dve.tensor_scalar(sl, sl, mx[:, c + i:c + i + 1], None, ALU.mult)
                m.then_inc(sem("p_norm"), 1)
                dve.wait_ge(sem("pt_mm"), h + 1)
                if h >= 2:
                    dve.wait_ge(sem("o_mm"), h - 1)
                dve.tensor_copy(PTm[h % 2][:, 512:1024], b5[:]).then_inc(sem("pt_dve"), 1)
                if h + 1 < H:
                    maxima(h + 1)
                if h % 2 == 1:
                    j = h // 2
                    dve.wait_ge(sem("attn_high"), j + 1)
                    if j == 0:
                        dve.wait_ge(sem("out_sp"), 16)
                    dve.tensor_tensor(catL[:, j, 0:TP], b7[:], catH[:, j, 0:TP].bitcast(f32), ALU.subtract
                                      ).then_inc(sem("attn_low"), 1)

            dve.memset(mxs[:, SA:P], 0.0)
            dve.wait_ge(sem("out_c"), 16)
            with dve.Fori(0, NB) as b:
                sn = snew[:, bass.ds(b * SA, SA)]
                dve.wait_ge(sem("s_mm"), b + 1)
                sc_ = acc[0][:].rearrange("p a (t q) -> p (a t) q", q=SA)
                dve.reduce_max(mxs[:, 0:SA], sc_.rearrange("p t q -> p q t"), AX.X).then_inc(sem("smax_part"), 1)
                dve.wait_ge(sem("smax_part"), b + 1)
                dve.tensor_tensor(mxs[0:SA, 0:SA], mxs[0:SA, 0:SA], sn, ALU.max).then_inc(sem("smax_ready"), 1)
                dve.wait_ge(sem("smax_tr"), b + 1)
                dve.reduce_max(rm[:], b7[0:SA, 0:P], AX.X).then_inc(sem("rm_ready"), 1)
                dve.wait_ge(sem("rm_ready"), b + 1)
                dve.tensor_scalar(dgm[:], ident[0:SA, 0:SA], rm[:], None, ALU.mult).then_inc(sem("sdiag2_ready"), 1)
                dve.wait_ge(sem("smax_mm"), b + 1)
                dve.tensor_copy(mxs[:, 0:SA], b7[:, P:P + SA]).then_inc(sem("mb_ready"), 1)
                dve.wait_ge(sem("mb_ready"), b + 1)
                dve.tensor_tensor(sS[:, 0:1024].rearrange("p (t q) -> p t q", q=SA), sc_,
                                  mxs[:, 0:SA].rearrange("p (a q) -> p a q", a=1).to_broadcast([P, NPG, SA]),
                                  ALU.subtract)
                dve.tensor_tensor(sS[0:SA, 1024:1088], sn, mxs[0:SA, 0:SA], ALU.subtract).then_inc(sem("shift_ready"), 1)
                dve.wait_ge(sem("sp_exp"), b + 1)
                dve.reduce_sum(psm[:], pS[:, 0:1024].rearrange("p (t q) -> p q t", q=SA), AX.X
                               ).then_inc(sem("psum_part"), 1)
                dve.wait_ge(sem("psum_part"), b + 1)
                dve.tensor_tensor(psm[0:SA, :], psm[0:SA, :], pS[0:SA, 1024:1088], ALU.add
                                  ).then_inc(sem("psum_ready"), 1)
                dve.wait_ge(sem("den_mm"), b + 1)
                dve.reciprocal(rsm[:], b7[:, P:P + SA]).then_inc(sem("rsm_ready"), 1)
                dve.wait_ge(sem("rsm_ready"), b + 1)
                dve.wait_ge(sem("pv_mm"), b + 1)
                dve.tensor_tensor(olat[:, :, bass.ds(b * SA, SA)],
                                  b6[:, 0:2 * SA].rearrange("p (a n) -> p a n", a=2), both(rsm[:]), ALU.mult
                                  ).then_inc(sem("olat_ready"), 1)
            dve.wait_ge(sem("osh_ready"), 1)
            dve.tensor_tensor(catL[:, 0:4, TP:T], b5[:, 0:256].rearrange("p (a n) -> p a n", a=4),
                              catH[:, 0:4, TP:T].bitcast(f32), ALU.subtract).then_inc(sem("osl_ready"), 1)

            dve.wait_ge(sem("out_kr"), 16)
            dve.wait_ge(sem("x_again"), 16)
            for d in range(KT):
                g = B_OUT + d
                dve.wait_ge(sem("gemm_done"), g + 1)
                dve.tensor_tensor(halves(xT[:, d, :]), acc[g % 2][:, :, 0:HALF], halves(xT[:, d, :]), ALU.add
                                  ).then_inc(sem("evac"), 1)
                dve.wait_ge(sem("evac"), g + 1)
                gm = vec[:, V_GM + d:V_GM + d + 1]
                dve.tensor_scalar(x2H[:, d, :], xT[:, d, :], gm, None, ALU.mult).then_inc(sem("x2_split"), 1)
                dve.wait_ge(sem("x2_split"), 2 * d + 1)
                dve.scalar_tensor_tensor(x2L[:, d, :], xT[:, d, :], gm, x2H[:, d, :].bitcast(f32),
                                         ALU.mult, ALU.subtract).then_inc(sem("x2_split"), 1)

            def up_out(n, g, u):
                dve.wait_ge(sem("gemm_done"), g + 1)
                dve.wait_ge(sem("ru_free"), n + 1)
                dve.scalar_tensor_tensor(halves(ru[u][:]), acc[u][:, :, 0:HALF], 0.0, halves(r3[:]),
                                         ALU.max, ALU.mult).then_inc(sem("evac"), 1)
                dve.wait_ge(sem("evac"), g + 1)

            def up_high(n, u, slot):
                dve.tensor_tensor(uH[:, slot, :] if isinstance(slot, int) else
                                  uH[:, bass.ds(slot, 1), :].rearrange("p a n -> p (a n)"),
                                  ru[u][:], ru[u][:], ALU.mult).then_inc(sem("uh_ready"), 1)

            def down_out(g, u, d):
                x_ = xT[:, bass.ds(d, 1), :].rearrange("p a (h n) -> p (a h) n", h=2)
                dve.wait_ge(sem("gemm_done"), g + 1)
                dve.tensor_tensor(x_, acc[u][:, :, 0:HALF], x_, ALU.add).then_inc(sem("evac"), 1)

            dve.wait_ge(sem("x2_root"), 1)
            dve.reciprocal(r3[:], r3[:]).then_inc(sem("r3_ready"), 1)
            dve.wait_ge(sem("r3_ready"), 1)
            with dve.Fori(0, QUARTERS) as q:
                with dve.Fori(0, 4) as j:
                    for u in range(2):
                        up_out(q * 8 + 2 * j + u, q * 16 + 2 * j + B_MLP + u, u)
                        up_high(None, u, 2 * j + u)
                with dve.Fori(0, 4) as j:
                    for u in range(2):
                        down_out(q * 16 + 2 * j + B_MLP + 8 + u, u, 2 * j + u)
            dve.wait_ge(sem("x3_root"), 1)
            link(dve.reciprocal(r3[:], r3[:]))
            for d in range(KT):
                dve.scalar_tensor_tensor(sq2[:, d, :], xT[:, d, :], vec[:, V_GF + d:V_GF + d + 1], r3[:],
                                         ALU.mult, ALU.mult).then_inc(sem("y_ready"), 1)

        @block.tensor
        def _(pe):
            def gemm(u, xh, xl, order=range(KT), before=None):
                n = 0
                for k in order:
                    if before:
                        before(k)
                    for h in range(2):
                        cols = slice(h * HALF, (h + 1) * HALF)
                        for q, (a, b) in enumerate(((whi, xh), (whi, xl), (wlo, xh))):
                            m = pe.matmul(acc[u][:, h, 0:HALF], a[u][:, k, :], b[:, k, cols],
                                          start=n == 0 and q == 0, stop=n == KT - 1 and q == 2)
                    n += 1
                m.then_inc(sem("gemm_done"), 1)

            def block_ready(g):
                pe.wait_ge(sem("w_split"), g + 1)
                if isinstance(g, int) and g < 2:
                    return
                pe.wait_ge(sem("evac"), g - 1)

            pe.wait_ge(sem("con_arrived"), 16)
            for g in range(N_IN):
                block_ready(g)
                gemm(g % 2, catH, catL,
                     before=(lambda k: pe.wait_ge(sem("x_split"), 2 * k + 2)) if g == 0 else None)
                if g == 0:
                    for k in range(KT):
                        pe.wait_ge(sem("x_squared"), k + 1)
                        for h in range(2):
                            m = pe.matmul((b4, b5)[h][:, 0:HALF], ones, sqx[:, k, h * HALF:(h + 1) * HALF],
                                          start=k == 0, stop=k == KT - 1)
                    m.then_inc(sem("x_summed"), 1)
                if g == 5:
                    pe.wait_ge(sem("x_root"), 1)
                    pe.wait_ge(sem("q_squared"), 3)
                    for h, bk in ((0, b4), (1, b5)):
                        for i in range(3):
                            m = pe.matmul(bk[:, 0:HALF], ones, sqq[:, i, h * HALF:(h + 1) * HALF],
                                          start=i == 0, stop=i == 2)
                    m.then_inc(sem("q_summed"), 1)
                    pe.wait_ge(sem("q_squared"), 5)
                    for h, bk in ((0, b6), (1, b7)):
                        for i in range(2):
                            m = pe.matmul(bk[:, 0:HALF], ones, sqq[:, 3 + i, h * HALF:(h + 1) * HALF],
                                          start=i == 0, stop=i == 1)
                    m.then_inc(sem("q_summed"), 1)
                if g == 7:
                    pe.wait_ge(sem("q_root"), 2)
                    for lhs, (ba, bb) in ((con[0:RP, C_REP:C_REP + P], (b4, b5)),
                                          (con[0:RP, C_RREP:C_RREP + P], (b6, b7))):
                        for h, bk in ((0, ba), (1, bb)):
                            m = pe.matmul(bk[:, 0:HALF], lhs, krw[0:RP, h * HALF:(h + 1) * HALF],
                                          start=True, stop=True)
                    m.then_inc(sem("kr_mm"), 1)
                if g == 9:
                    pe.wait_ge(sem("pack_ready"), 1)
                    pe.wait_ge(sem("kr_ready"), 1)
                    for i in range(5):
                        n = P if i < 4 else SA
                        m = pe.transpose(b4[0:n, 72 * i:72 * i + 72], pack[0:72, P * i:P * i + n],
                                         ident[0:72, 0:72])
                    m.then_inc(sem("pack_tr"), 1)
                if g >= 10 and g - 10 < 6:
                    c = g - 10
                    pe.wait_ge(sem("silu_done"), c + 1)
                    if c >= 1:
                        pe.wait_ge(sem("xnat_ready"), c)
                    bk = b5 if c % 2 == 0 else b6
                    for i in range(5):
                        n = P if i < 4 else SA
                        m = pe.transpose(bk[:, P * i:P * i + P] if i < 4 else b7[0:SA, 0:P],
                                         xc[:, c, P * i:P * i + n], ident)
                    m.then_inc(sem("x_tr"), 1)
                if g >= 16:
                    c = g - 16
                    pe.wait_ge(sem("silu_done"), KT)
                    pe.wait_ge(sem("xnat_ready"), 6)
                    if c:
                        pe.wait_ge(sem("cb_ready"), 1)
                    for i, (bk, off) in enumerate(((b4, 0), (b5, 0), (b6, 0), (b5, 384))):
                        m = pe.matmul(bk[:, off:off + TP - P * i], xc[:, 4 + c, P * i:P * i + P],
                                      xc[:, 6 + c, P * i:TP], start=True, stop=True)
                    m = pe.matmul(b6[0:SA, 256:256 + SA], xc[:, 4 + c, TP:T], xc[:, 6 + c, TP:T],
                                  start=True, stop=True)
                    m.then_inc(sem("cb_mm"), 1)

            def decay_rows(h):
                if h >= 2:
                    pe.wait_ge(sem("ex_done"), h - 1)
                else:
                    pe.wait_ge(sem("evac"), N_IN)
                pe.matmul(acc[0][:, h % 2, :], ident[32:40, 32 + h:33 + h].to_broadcast([8, P]),
                          acs[32:40, 0:TP], start=True, stop=True).then_inc(sem("rows_done"), 1)

            decay_rows(0)
            for h in range(H):
                if h + 1 < H:
                    decay_rows(h + 1)
                j = h // 2
                pe.wait_ge(sem("mix_ready"), h + 1)
                if j >= 2:
                    pe.wait_ge(sem("y_taken"), j - 1)
                for i in range(4):
                    m = pe.matmul(acc[1][64 * (h % 2):64 * (h % 2) + 64, j % 2, P * i:TP],
                                  xnat[:, i, 64 * h:64 * h + 64], ex[h % 3][:, GOFF[i]:GOFF[i + 1]],
                                  start=i == 0, stop=i == 3)
                m.then_inc(sem("y_mm"), 1)
            pe.wait_ge(sem("cb_ready"), 2)
            for h in range(H):
                m = pe.matmul(b4[0:SA, SA * h:SA * h + SA], ident[32:40, 32 + h:33 + h].to_broadcast([8, SA]),
                              acs[32:40, TP:T], start=True, stop=True)
            m.then_inc(sem("srows_done"), 1)
            e8 = pack[96:104, :]
            for h in range(H):
                sel = ident[96:104, 96 + h:97 + h]
                pe.matmul(b7[64 * (h % 2):64 * (h % 2) + 64, SA * (h // 2):SA * (h // 2) + SA],
                          sel.to_broadcast([8, 64]), e8[:, TP:T], start=True, stop=True)
            for h in range(H):
                sel = ident[96:104, 96 + h:97 + h]
                m = pe.matmul(b7[:, 256 + NB * h:256 + NB * h + NB], sel.to_broadcast([8, P]),
                              e8[:, TP + TS - 1:T:TS], start=True, stop=True)
            m.then_inc(sem("se_mm"), 1)
            pe.wait_ge(sem("h0_arrived"), 16)
            for b in range(NB):
                for j in range(4):
                    m = pe.matmul(b6[:, SA * j + TS * b:SA * j + TS * b + TS], h0T[:, b, P * j:P * j + P],
                                  xc[:, 6 + j // 2, TP + TS * b:TP + TS * b + TS], start=True, stop=True)
            m.then_inc(sem("yo_mm"), 1)
            pe.wait_ge(sem("smix_ready"), 1)
            for h in range(H):
                m = pe.matmul(b5[64 * (h % 2):64 * (h % 2) + 64, SA * (h // 2):SA * (h // 2) + SA],
                              xnat[0:SA, 4, 64 * h:64 * h + 64], gs[:, h, :], start=True, stop=True)
            m.then_inc(sem("ys_mm"), 1)
            pe.wait_ge(sem("xdd_ready"), 1)
            for c in range(2):
                for i in range(4):
                    m = pe.matmul(acc[0][:, 0, 256 * c:256 * c + 256], bnat[:, i, P * c:P * c + P],
                                  xnat[:, i, 256 * c:256 * c + 256], start=i == 0, stop=i == 3)
            m.then_inc(sem("sp_mm"), 1)
            pe.wait_ge(sem("bms_ready"), NB)
            pe.wait_ge(sem("xdd_ready"), 2)
            pe.wait_ge(sem("y_taken"), 4)
            for b in range(NB):
                if b >= 2:
                    pe.wait_ge(sem("hn_ready"), b - 1)
                for c in range(2):
                    m = pe.matmul(acc[1][:, b % 2, 256 * c:256 * c + 256], bms[:, b, P * c:P * c + P],
                                  xnat[0:SA, 4, 256 * c:256 * c + 256], start=True, stop=True)
                m.then_inc(sem("hn_mm"), 1)
            pe.wait_ge(sem("ys_taken"), 1)
            for c in range(2):
                for h, bk in ((0, (b4, b6)[c]), (1, (b5, b7)[c])):
                    for i in range(2):
                        if h == 0:
                            pe.wait_ge(sem("g_squared"), 2 * c + i + 1)
                        m = pe.matmul(bk[:, 0:HALF], ones, z[:, 2 * c + i, h * HALF:(h + 1) * HALF],
                                      start=i == 0, stop=i == 1)
                m.then_inc(sem("g_summed"), 1)
            pe.wait_ge(sem("hn_ready"), NB)
            pe.wait_ge(sem("spo_ready"), 1)
            pe.wait_ge(sem("wuq_arrived"), 16)
            pe.wait_ge(sem("qg_ready"), 3)
            for u in range(6):
                if u >= 2:
                    pe.wait_ge(sem("q_evac"), u - 1)
                for k in range(3):
                    w = wuq[:, k, P * u:P * u + P]
                    pe.matmul(acc[u % 2][:, 0, :], w, qlat[:, k, 0:TP], start=k == 0, stop=k == 2)
                    m = pe.matmul(acc[u % 2][:, 1, 0:SA], w, qlat[:, k, TP:T], start=k == 0, stop=k == 2)
                m.then_inc(sem("q_mm"), 1)
            pe.wait_ge(sem("wukT_arrived"), 16)
            pe.wait_ge(sem("wuv_arrived"), 16)
            pe.wait_ge(sem("c_ready"), 2)
            for u in range(8):
                if u < 2:
                    pe.wait_ge(sem("q_evac"), 5 + u)
                else:
                    pe.wait_ge(sem("kv_evac"), u - 1)
                for k in range(2):
                    if u < 4:
                        lhs, rhs = wukT[:, k, P * u:P * u + P], cT[:, k, 0:TP]
                    else:
                        lhs, rhs = cT[:, k, P * (u - 4):P * (u - 3)], wuv[:, k, :]
                    m = pe.matmul(acc[u % 2][:, 0, :], lhs, rhs, start=k == 0, stop=k == 1)
                m.then_inc(sem("kv_mm"), 1)
            pe.wait_ge(sem("g_root"), 2)
            for i in range(2):
                pe.matmul((b4, b5)[i][:], rot, qp[:, i, 0:TP], start=True, stop=True)
                m = pe.matmul(b6[:, SA * i:SA * i + SA], rot, qp[:, i, TP:T], start=True, stop=True)
            m.then_inc(sem("rot_mm"), 1)
            pe.wait_ge(sem("qrs_ready"), 1)
            for h in range(H):
                m = pe.matmul(b7[:, SA * h:SA * h + SA], con[:, C_REP + P * (h % 4):C_REP + P * (h % 4) + P],
                              qrs[:, h // 4, :], start=True, stop=True)
            m.then_inc(sem("qps_mm"), 1)
            pe.wait_ge(sem("kv_evac"), 8)
            pe.wait_ge(sem("wuk_arrived"), 16)
            for h in range(H):
                for k in range(2):
                    m = pe.matmul(acc[0][:, k, SA * h:SA * h + SA], wuk[:, h, P * k:P * k + P], qs[:, h, :],
                                  start=True, stop=True)
            m.then_inc(sem("qabs_mm"), 1)
            for k in range(2):
                m = pe.transpose(b4[0:SA, P * k:P * k + P], cT[:, k, TP:T], ident)
            m.then_inc(sem("c64_mm"), 1)
            pe.wait_ge(sem("qabs_ready"), 2)
            pe.wait_ge(sem("qps_ready"), 1)
            for k in range(2):
                pe.matmul(b5[0:SA, :], cT[:, k, TP:T], qabs[:, k, :], start=k == 0, stop=False)
            pe.matmul(b5[0:SA, :], krR[0:RP, TP:T], qps[0:RP, :], start=False, stop=True
                      ).then_inc(sem("snew_mm"), 1)

            sbank = [acc[0][:, 0, :], acc[0][:, 1, :], acc[1][:, 0, :], acc[1][:, 1, :]]

            def scores(h):
                if h == 0:
                    pe.wait_ge(sem("qrope_ready"), H)
                    pe.wait_ge(sem("krope_ready"), 1)
                else:
                    pe.wait_ge(sem("p_exp"), h)
                for i in range(QT_N):
                    pe.matmul(sbank[i][:, 0:P * (i + 1)], QT[:, h, P * i:P * i + P], KTt[:, h, 0:P * (i + 1)],
                              start=True, stop=True).then_inc(sem("score_mm"), 1)

            scores(0)
            pe.wait_ge(sem("c64_ready"), 1)
            pe.wait_ge(sem("snew_ready"), 1)
            for h in range(H):
                pe.wait_ge(sem("p_norm"), h + 1)
                if h:
                    pe.wait_ge(sem("pt_act"), h)
                    pe.wait_ge(sem("pt_dve"), h)
                off = [0, 128, 384, 768]
                for k in range(QT_N):
                    for i in range(k, QT_N):
                        c = GOFF[k] + P * (i - k)
                        m = pe.transpose((b4, b5, b6)[c // 512][:, c % 512:c % 512 + P],
                                         Pm[h % 2][:, off[i] + P * k:off[i] + P * k + P], ident)
                m.then_inc(sem("pt_mm"), 1)
                if h + 1 < H:
                    scores(h + 1)
                pe.wait_ge(sem("pt_act"), h + 1)
                pe.wait_ge(sem("pt_dve"), h + 1)
                if h and h % 2 == 0:
                    pe.wait_ge(sem("attn_low"), h // 2)
                for k in range(QT_N):
                    m = pe.matmul(b7[64 * (h % 2):64 * (h % 2) + 64, P * k:TP], V[:, k, 64 * h:64 * h + 64],
                                  PTm[h % 2][:, GOFF[k]:GOFF[k + 1]], start=k == 0, stop=k == 3)
                m.then_inc(sem("o_mm"), 1)

            def turn(u, q):
                bk = (b4, b5)[(u + q) % 2]
                for j in range(4):
                    if q < 8:
                        src = ckv[u][:, 2 * q + j // 2, P * (j % 2):P * (j % 2) + P]
                    else:
                        src = ckr[u][:, 4 * j:4 * j + 4, :].rearrange("p a n -> p (a n)")
                    m = pe.transpose(bk[:, P * j:P * j + P], src, ident)
                m.then_inc(sem("ct_mm"), 1)

            def turns(b, u, qs_, first=False):
                for q in qs_:
                    if q == 0:
                        pe.wait_ge(sem(f"cache_arrived{u}"), 512 * (b // 2 + 1) if isinstance(b, int) else b * 256 + 512 - 256 * u)
                    if not (first and q < 2):
                        pe.wait_ge(sem("ct_evac"), b * 9 + q - 1)
                    turn(u, q)

            def sequence(b, u, nxt):
                pe.wait_ge(sem("ct_evac"), b * 9 + 9)
                pe.wait_ge(sem("qb_ready"), b + 1)
                for a in range(NPG // 4):
                    pe.matmul(acc[0][:, a // 2, 256 * (a % 2):256 * (a % 2) + 256], KRr[:, a, :],
                              qpb[:].rearrange("p a n -> p (a n)"), start=True, stop=False)
                    for t in range(4 * a, 4 * a + 4):
                        for k in range(2):
                            m = pe.matmul(acc[0][:, t // 8, SA * (t % 8):SA * (t % 8) + SA],
                                          CTr[:, k, P * t:P * t + P], qab[:, k, :], start=False, stop=k == 1 and t % 4 == 3)
                m.then_inc(sem("s_mm"), 1)
                if nxt:
                    turns(b + 1, 1 - u, range(0, 3))
                pe.wait_ge(sem("smax_ready"), b + 1)
                pe.transpose(b7[:, 0:P], mxs[:], ident).then_inc(sem("smax_tr"), 1)
                if nxt:
                    turns(b + 1, 1 - u, range(3, 6))
                pe.wait_ge(sem("sdiag2_ready"), b + 1)
                pe.matmul(b7[:, P:P + SA], ones[0:SA, :], dgm[:], start=True, stop=True
                          ).then_inc(sem("smax_mm"), 1)
                if nxt:
                    turns(b + 1, 1 - u, range(6, 9))
                pe.wait_ge(sem("sp_exp"), b + 1)
                for k in range(2):
                    for t in range(NPG):
                        pe.matmul(b6[:, SA * k:SA * k + SA], ckv[u][:, t, P * k:P * k + P],
                                  pS[:, SA * t:SA * t + SA], start=t == 0, stop=False)
                    m = pe.matmul(b6[:, SA * k:SA * k + SA], c64[:, P * k:P * k + P], pS[0:SA, 1024:1088],
                                  start=False, stop=True)
                m.then_inc(sem("pv_mm"), 1)
                pe.wait_ge(sem("psum_ready"), b + 1)
                pe.matmul(b7[:, P:P + SA], ones, psm[:], start=True, stop=True).then_inc(sem("den_mm"), 1)

            pe.wait_ge(sem("attn_low"), 4)
            turns(0, 0, range(9), first=True)
            with pe.Fori(0, 3) as i:
                for u in range(2):
                    sequence(i * 2 + u, u, True)
            sequence(6, 0, True)
            sequence(7, 1, False)
            pe.wait_ge(sem("olat_ready"), NB)
            for h in range(H):
                for k in range(2):
                    rhs = olat[:, k, :].rearrange("p (b h t) -> p h b t", b=NB, h=H)[:, h, :, :]
                    m = pe.matmul(b5[64 * (h % 2):64 * (h % 2) + 64, SA * (h // 2):SA * (h // 2) + SA],
                                  wuv[:, k, 64 * h:64 * h + 64], rhs, start=k == 0, stop=k == 1)
            m.then_inc(sem("os_mm"), 1)

            pe.wait_ge(sem("oh_ready"), 4)
            pe.wait_ge(sem("ol_ready"), 4)

            def heads_ready(k):
                if k < 4:
                    pe.wait_ge(sem("osl_ready"), 1)

            for g in range(B_OUT, B_MLP):
                block_ready(g)
                gemm(g % 2, catH, catL, order=[4, 5, 6, 7, 0, 1, 2, 3], before=heads_ready if g == B_OUT else None)

            def up(g, u, before=None):
                block_ready(g)
                gemm(u, x2H, x2L, before=before)

            def down(g, u, q, first):
                block_ready(g)
                gemm(u, uH, uL, before=(lambda k: pe.wait_ge(sem("ul_ready"), q * 8 + k + 3)) if first else None)

            def quarter(q, peel):
                g0 = q * 16 + B_MLP
                if peel:
                    up(g0, 0, before=lambda k: pe.wait_ge(sem("x2_split"), 2 * k + 2))
                    pe.wait_ge(sem("x2_summed"), 1)
                    for h in range(2):
                        m = pe.matmul((b4, b5)[h][:, 0:HALF], ones, r2[:, h * HALF:(h + 1) * HALF],
                                      start=True, stop=True)
                    m.then_inc(sem("x2_sum_mm"), 1)
                    up(g0 + 1, 1)
                else:
                    up(g0, 0)
                    up(g0 + 1, 1)
                with pe.Fori(1, 4) as j:
                    up(g0 + 2 * j, 0)
                    up(g0 + 2 * j + 1, 1)
                down(g0 + 8, 0, q, True)
                down(g0 + 9, 1, q, False)
                with pe.Fori(1, 4) as j:
                    down(g0 + 2 * j + 8, 0, q, False)
                    down(g0 + 2 * j + 9, 1, q, False)

            quarter(0, True)
            with pe.Fori(1, QUARTERS) as q:
                quarter(q, False)
            pe.wait_ge(sem("x3_summed"), 1)
            for h in range(2):
                m = pe.matmul((b4, b5)[h][:, 0:HALF], ones, r2[:, h * HALF:(h + 1) * HALF], start=True, stop=True)
            m.then_inc(sem("x3_sum_mm"), 1)


_SHAPES = [((P, KT, T), "y"), ((P, 2, T), "c"), ((RP, T), "kr"), ((P, 512), "ssm_p"),
           ((P, NB, 512), "ssm_s"), ((P, KT, 27), "conv")]


def layouts(i):
    import numpy as np
    c = np.ascontiguousarray

    def blocks(w):
        k, n = w.shape[0] // P, w.shape[1] // P
        return w.reshape(k, P, n, P).transpose(2, 1, 0, 3).reshape(n, P, k * P)

    def columns(v):
        return v.reshape(-1, P).T

    w_in, w_up, w_down = i["w_in"][0], i["w_up"][0], i["w_down"][0]
    e = np.cumsum([QL, CL, RP, 512, 1024, 8])
    q, kv, kpe, zz, xbc, dt = np.split(w_in, e[:-1], axis=1)
    special = np.concatenate([kpe, dt, np.zeros((D, P - RP - 8), w_in.dtype)], axis=1)
    parts = [blocks(a) for a in (q, kv, special, xbc, zz)] + [blocks(i["w_out"][0])]
    fq = w_up.shape[1] // QUARTERS
    for n in range(QUARTERS):
        parts += [blocks(w_up[:, n * fq:(n + 1) * fq]), blocks(w_down[n * fq:(n + 1) * fq])]
    x = np.concatenate([i["x_prompt"].reshape(TP, D), i["x_sample"].reshape(SA, D)], axis=0)
    wuq = i["w_uq"][0].reshape(QL, H, 96)
    wuq = np.concatenate([wuq[:, :, :64].reshape(QL, 512), wuq[:, :, 64:].reshape(QL, 256)], axis=1)
    vec = np.zeros((P, NV), np.float32)
    vec[:, V_GATT:V_GATT + 8] = columns(i["norm_attn"][0])
    vec[:, V_GQ:V_GQ + 3] = columns(i["q_norm"][0])
    vec[:, V_GKV:V_GKV + 2] = columns(i["kv_norm"][0])
    vec[:, V_CW:V_CW + 32] = i["conv_w"][0].reshape(CONV_K, KT, P).transpose(2, 1, 0).reshape(P, 32)
    vec[:, V_CB:V_CB + 8] = columns(i["conv_b"][0])
    vec[:, V_GS:V_GS + 4] = columns(i["ssm_norm"][0])
    vec[:, V_GM:V_GM + 8] = columns(i["norm_mlp"][0])
    vec[:, V_GF:V_GF + 8] = columns(i["norm_final"])
    vec[:, V_D:V_D + 4] = columns(np.repeat(i["d_skip"][0], DH))
    vec[32:40, V_DTB] = i["dt_bias"][0]
    vec[32:40, V_AL] = i["a_log"][0]
    vec[:, V_EPS] = EPS
    s = np.arange(P)
    for b in range(NB):
        vec[:SA, V_BM + b] = (s[:SA] // TS == b)
    for a in range(4):
        vec[:, V_QM + a] = (s // RP == a)
    return {
        "wst": c(np.concatenate(parts, axis=0)),
        "x": c(x.T.reshape(KT, P, T).transpose(1, 0, 2)),
        "kv": c(i["cache_kv_latent"][0]), "kr": c(i["cache_k_rope"][0]),
        "h0": c(i["state_ssm"][0].reshape(NB, 512, NST).transpose(2, 0, 1)),
        "sc": c(i["state_conv"][0].reshape(NB, 3, KT, P).transpose(3, 2, 0, 1)),
        "wuq": c(wuq.reshape(3, P, 768).transpose(1, 0, 2)),
        "wukT": c(i["w_uk"][0].transpose(2, 0, 1).reshape(2, P, 512).transpose(1, 0, 2)),
        "wuk": c(i["w_uk"][0].transpose(1, 0, 2)),
        "wuv": c(i["w_uv"][0].transpose(1, 0, 2).reshape(2, P, 512).transpose(1, 0, 2)),
        "vec": vec, "con": constants(), "pt": c(i["page_table"].reshape(1, NB * NPG)),
    }


def constants():
    import numpy as np
    con = np.zeros((P, NC_), np.float32)
    p = np.arange(P)
    con[:, C_ID:C_ID + P] = np.eye(P)
    con[:, C_ONE:C_ONE + P] = 1.0
    swap = (p // RP) * RP + (p % RP + RP // 2) % RP
    con[p, C_ROT + swap] = 1.0
    for a in range(4):
        con[RP * a + p % RP, C_REP + P * a + p] = 1.0
    con[(p % RP + RP // 2) % RP, C_RREP + p] = 1.0
    con[:, C_AM:C_AM + P] = np.where(p[None, :] <= p[:, None], 0, NEG)
    con[:, C_TRI:C_TRI + P] = p[None, :] >= p[:, None]
    con[:, C_NEG:C_NEG + P] = np.where(p[None, :] >= p[:, None], 0, NEG)
    s = np.arange(SA)
    same = (s[:, None] // TS == s[None, :] // TS) & (s[None, :] >= s[:, None])
    con[:SA, C_SNEG:C_SNEG + SA] = np.where(same, 0, NEG)
    pos = np.concatenate([np.arange(TP), np.tile(PAST + np.arange(TS), NB)]).astype(np.float32)
    inv = (np.float32(10000.0) ** (-(np.arange(0, RP, 2, dtype=np.float32) / RP))).astype(np.float32)
    ang = (pos[:, None] * inv[None, :]).astype(np.float32)
    con[:, C_COS:C_COS + T] = np.cos(ang)[:, p % 16].T
    con[:, C_SIN:C_SIN + T] = np.sin(ang)[:, p % 16].T * np.where(p % RP < 16, -1, 1)[:, None]
    m = same.reshape(SA, NB, 1, TS)
    con[:SA, C_SM:C_SM + 512] = np.broadcast_to(np.where(m, 0, NEG), (SA, NB, H, TS)).reshape(SA, 512)
    rst = np.ones(T)
    rst[0] = 0
    rst[TP::TS] = 0
    con[:, C_RST:C_RST + T] = rst
    return con


def kernel(**inputs):
    import numpy as np
    import concourse.bacc as bacc
    from concourse.bass_utils import run_bass_kernel_spmd as run

    nc = bacc.Bacc("TRN2", target_bir_lowering=False, num_devices=1)
    arrays, args = {}, []
    for name, a in layouts({k: np.asarray(v) for k, v in inputs.items()}).items():
        arrays["in_" + name] = a
        args.append(nc.dram_tensor("in_" + name, a.shape, mybir.dt.from_np(a.dtype), kind="ExternalInput").ap())
    for shape, name in _SHAPES:
        args.append(nc.dram_tensor("out_" + name, shape, mybir.dt.float32, kind="ExternalOutput").ap())
    build(nc, *args)
    r = run(nc, [arrays], core_ids=[0]).results[0]
    y = r["out_y"].transpose(2, 1, 0).reshape(T, D)
    c = r["out_c"].transpose(2, 1, 0).reshape(T, CL)
    kr = r["out_kr"].T
    sp = r["out_ssm_p"].T
    ss = r["out_ssm_s"].transpose(1, 2, 0)
    cn = r["out_conv"].transpose(2, 1, 0).reshape(27, D)
    return (y[:TP].reshape(1, TP, D), y[TP:].reshape(NB, TS, D),
            c[:TP].reshape(1, 1, TP, CL), kr[:TP].reshape(1, 1, TP, RP),
            sp.reshape(1, 1, H, DH, NST), cn[:3].reshape(1, 1, 3, D),
            c[TP:].reshape(1, NB, TS, CL), kr[TP:].reshape(1, NB, TS, RP),
            ss.reshape(1, NB, H, DH, NST), cn[3:].reshape(1, NB, 3, D))
```

```python
import concourse.bass as bass
from concourse import mybir
from contextlib import ExitStack

P = 128
D = 1024
KT = D // P
TP, NB, TS = 512, 8, 8
SA = NB * TS
T = TP + SA
HALF = T // 2
QL, CL, RP = 384, 256, 32
H, DH = 8, 64
NST = 128
PAST, PAGE = 2048, 128
NPG = PAST // PAGE
POOL = 160
QT_N = TP // P
CONV_K = 4
EPS = 1e-6
SCALE = float(64 + RP) ** -0.5
NEG = -1e30

B_Q, B_KV, B_SP, B_X, B_Z, N_IN = 0, 3, 5, 6, 14, 18
B_OUT = N_IN
B_MLP = B_OUT + 8
N_BLK = B_MLP + 64
QUARTERS = 4
Q_ORDER = (4, 5, 0, 1, 2, 3)

V_GATT, V_GQ, V_GKV, V_CW, V_CB, V_GS, V_GM, V_GF, V_D, V_DTB, V_AL, V_EPS, V_BM, V_QM = (
    0, 8, 11, 13, 45, 53, 57, 65, 73, 77, 78, 79, 80, 88)
NV = 92
C_ONE, C_ID, C_ROT, C_AM, C_TRI, C_NEG, C_SNEG, C_COS, C_SIN, C_SM, C_RST, C_REP, C_RREP = (
    0, 128, 256, 384, 512, 640, 768, 832, 1408, 1984, 2496, 3072, 3584)
NC_ = 3712

PADW = 3 + TP + NB * (3 + TS)
CW = PADW - 3
SB0 = 3 + TP
GOFF = [0, 512, 896, 1152, 1280]


def build(nc, wst, x_d, kv_d, kr_d, h0_d, sc_d, wuq_d, wukT_d, wuk_d, wuv_d, vec_d, con_d, pt_d,
          y_o, c_o, kr_o, sp_o, ss_o, cn_o):
    f32, f32r, i32 = mybir.dt.float32, mybir.dt.float32r, mybir.dt.int32
    ALU, ACT, AX = mybir.AluOpType, mybir.ActivationFunctionType, mybir.AxisListType
    ctx = ExitStack()
    with ctx:
        base = (nc.sbuf_base + 31) // 32 * 32
        room = nc.sbuf_usable_end - base

        def at(name, shape, off, dt=f32):
            size = 4
            for s in shape[1:]:
                size *= s
            assert off + size <= room, (name, off + size, room)
            return nc.alloc_sbuf_tensor_at(name, shape, dt, offset=base + off)

        made = {}

        def sem(name):
            if name not in made:
                made[name] = ctx.enter_context(nc.semaphore(name))
            return made[name]

        xT = at("xT", [P, KT, T], 0)
        h0T = at("h0T", [P, NB, 512], 0)
        catH = at("catH", [P, KT, T], 18432, f32r)
        catL = at("catL", [P, KT, T], 36864, f32r)
        wraw = [at(f"wraw{i}", [P, KT, P], 55296 + 4096 * i) for i in range(2)]
        whi = [at(f"whi{i}", [P, KT, P], 63488 + 4096 * i, f32r) for i in range(2)]
        wlo = [at(f"wlo{i}", [P, KT, P], 71680 + 4096 * i, f32r) for i in range(2)]
        con = at("con", [P, NC_], 79872)
        vec = at("vec", [P, NV], 94720)
        o = 95104
        qlat = at("qlat", [P, 3, T], o)
        cT = at("cT", [P, 2, T], o + 6912)
        wuq = at("wuq", [P, 3, 768], o + 11520)
        wukT = at("wukT", [P, 2, 512], o + 20736)
        wuk = at("wuk", [64, H, CL], o + 24832)
        wuv = at("wuv", [P, 2, 512], o + 33024)
        rx_o = o + 37120
        rx = at("rx", [P, T], rx_o)
        rq = at("rq", [P, T], o + 39424)
        rk = at("rk", [P, T], o + 41728)
        krR = at("krR", [P, T], o + 44032)
        pack = at("pack", [P, T], o + 46336)
        acs = at("acs", [P, T], o + 48640)
        pn = at("pn", [P, 5, 72], o + 50944)
        ptb = at("ptb", [1, NB * NPG], o + 52384, i32)
        r = o + 52896
        xc = at("xc", [P, KT, T], r)
        sqx = at("sqx", [P, KT, T], r)
        z = at("z", [P, 4, T], r + 18432)
        xnat = at("xnat", [P, 5, 512], r + 27648)
        bnat = at("bnat", [P, 5, 256], r + 37888)
        cbm = at("cbm", [P, 2, 1280], r + 43008)
        sqq = at("sqq", [P, 5, T], r + 37888)
        cbs = at("cbs", [64, 2, SA], r + 53248)
        pad = [at(f"pad{i}", [P, PADW], r + 53760 + 2432 * i) for i in range(2)]
        cacc = [at(f"cacc{i}", [P, PADW], r + 53760 + 4864 + 2432 * i) for i in range(2)]
        krw = at("krw", [P, T], r + 27648)
        t1 = at("t1", [P, T], r + 27648 + 2304)
        dw = [at(f"dw{i}", [P, T], r + 27648 + 4608 + 2304 * 0 + 2304 * i) for i in range(2)]
        cn = at("cn", [P, KT, 27], r + 63488)
        scv = at("scv", [P, KT, NB, 3], 0 + 16384)
        assert r + 64352 <= room, (r + 64352, room)
        ex = [at("ex0", [P, 1280], 18432), at("ex1", [P, 1280], 36864), at("ex2", [P, 1280], r + 53760)]
        dgn = [at(f"dgn{i}", [P, 4, P], 18432 + 5120 + 2048 * i) for i in range(2)]
        gs = at("gs", [64, H, SA], 36864 + 5120)
        se = at("se", [P, 320], r + 53760 + 5120)
        ysm = at("ysm", [P, 4, SA], r + 53760 + 6400)
        bms = at("bms", [64, NB, 256], 18432)
        spo = at("spo", [P, 512], 36864)
        rg = at("rg", [P, 2, T], r + 43008)
        QT = at("QT", [96, H, TP], r)
        KTt = at("KTt", [96, H, TP], r + 16384)
        V = at("V", [P, QT_N, 512], r + 32768)
        Pm = at("Pm", [P, 1280], r + 40960)
        PTm = at("PTm", [P, 1280], r + 46080)
        qp = at("qp", [P, 2, T], r + 40960)
        tq = [at(f"tq{i}", [P, 2, T], r + 51200 + 4608 * i) for i in range(2)]
        qs = at("qs", [64, H, SA], r + 61440)
        qrs = at("qrs", [P, 2, SA], r + 63488)
        mx = at("mx", [P, 12], rx_o)
        qabs = at("qabs", [P, 2, 512], o)
        qps = at("qps", [P, 512], o + 4096)
        snew = at("snew", [64, 512], o + 46336)
        c64 = at("c64", [64, 256], o + 50944)
        ckv = [at("ckv0", [P, NPG, CL], 0), at("ckv1", [P, NPG, CL], o + 11520)]
        ckr = [at("ckr0", [P, NPG, RP], 16384), at("ckr1", [P, NPG, RP], o + 27904)]
        CTr = at("CTr", [P, 2, PAST], 63488)
        KRr = at("KRr", [P, 4, P], o + 39424)
        sS = at("sS", [P, 1088], r + 51200)
        pS = at("pS", [P, 1088], r + 55552)
        rm = at("rm", [SA, 1], r + 59904)
        dgm = at("dgm", [SA, SA], r + 59936)
        psm = at("psm", [P, SA], r + 60192)
        rsm = at("rsm", [P, SA], r + 60448)
        mxs = at("mxs", [P, P], r + 60704)
        qpb = at("qpb", [P, 4, SA], r + 61216)
        olat = at("olat", [P, 2, 512], o + 6912)
        x2H = at("x2H", [P, KT, T], o, f32r)
        x2L = at("x2L", [P, KT, T], o + 18432, f32r)
        uH = at("uH", [P, KT, T], o + 36864, f32r)
        uL = at("uL", [P, KT, T], o + 55296, f32r)
        ru = [at(f"ru{i}", [P, T], o + 73728 + 2304 * i) for i in range(2)]
        us = [at(f"us{i}", [P, T], o + 78336 + 2304 * i) for i in range(2)]
        r2 = at("r2", [P, T], o + 82944)
        r3 = at("r3", [P, T], o + 85248)
        sq2 = at("sq2", [P, KT, T], o + 87552)

        B = [ctx.enter_context(nc.psum_tensor(f"bank{i}", [P, 2, 512], f32)) for i in range(2)] + \
            [ctx.enter_context(nc.psum_tensor(f"bank{i}", [P, 512], f32)) for i in range(4, 8)]
        acc = [B[0], B[1]]
        b4, b5, b6, b7 = B[2:]

        ident = con[:, C_ID:C_ID + P]
        ones = con[:, C_ONE:C_ONE + P]
        rot = con[:, C_ROT:C_ROT + P]
        tri = con[:, C_TRI:C_TRI + P]
        neg = con[:, C_NEG:C_NEG + P]
        cosT = con[:, C_COS:C_COS + T]
        sinT = con[:, C_SIN:C_SIN + T]

        rows_bank = [acc[0][:, 0, :], acc[0][:, 1, :], b4[:], b5[:]]

        def halves(ap):
            return ap.rearrange("p (a n) -> p a n", a=2)

        def samp(ap, w=TS):
            return ap[:, SB0:SB0 + NB * (3 + TS)].rearrange("p (b w) -> p b w", w=3 + TS)

        block = ctx.enter_context(nc.Block())

        @block.sync
        def _(sp):
            def ring(g):
                if g >= 2:
                    sp.wait_ge(sem("w_split"), g - 1)
                sp.dma_start(wraw[g % 2][:], wst[g, :, :].rearrange("p (k n) -> p k n", k=KT)
                             ).then_inc(sem(f"w_arrived{g % 2}"), 16)

            for k in range(KT):
                if k % 2 == 0:
                    sp.dma_start(xT[:, k:k + 2, :], x_d[:, k:k + 2, :]).then_inc(sem(f"x_arrived{k // 2}"), 16)
                if k == 0:
                    ring(0)
            for g in range(1, N_IN + 2):
                ring(g)

            def pages(b, u, free, count):
                numbers = [sp.value_load(ptb[0:1, b * NPG + j:b * NPG + j + 1] if isinstance(b, int)
                                         else ptb[0:1, bass.ds(b * NPG + j, 1)], min_val=0, max_val=POOL - 1)
                           for j in range(NPG)]
                sp.wait_ge(sem(free), count)
                for j, page in enumerate(numbers):
                    sp.dma_start(ckv[u][:, j, :], kv_d[bass.ds(page, 1), :, :].rearrange("a p n -> (a p) n")
                                 ).then_inc(sem(f"cache{u}_half{j // (NPG // 2)}"), 16)
                for j, page in enumerate(numbers):
                    sp.dma_start(ckr[u][:, j, :], kr_d[bass.ds(page, 1), :, :].rearrange("a p n -> (a p) n")
                                 ).then_inc(sem(f"cache{u}_rotary"), 16)

            sp.wait_ge(sem("pt_arrived"), 16)
            pages(0, 0, "out_ss", 16)
            pages(1, 1, "qabs_mm", 1)
            with sp.Fori(1, NB // 2) as i:
                for u in range(2):
                    pages(i * 2 + u, u, "pv_mm", i * 2 + u - 1)
            sp.wait_ge(sem("pv_mm"), 7)
            sp.dma_start(xT[:], x_d).then_inc(sem("x_again"), 16)
            with sp.Fori((N_IN + 2) // 2, N_BLK // 2) as i:
                for u in range(2):
                    sp.wait_ge(sem("w_split"), i * 2 + u - 1)
                    sp.dma_start(wraw[u][:], wst[bass.ds(i * 2 + u, 1), :, :].rearrange("a p (k n) -> (a p) k n", k=KT)
                                 ).then_inc(sem(f"w_arrived{u}"), 16)
            for c in range(4):
                sp.wait_ge(sem("y_ready"), 2 * c + 2)
                sp.dma_start(y_o[:, 2 * c:2 * c + 2, :], sq2[:, 2 * c:2 * c + 2, :]).then_inc(sem("out_y"), 16)
            for name in ("out_c", "out_kr", "out_cn", "out_sp", "out_ss"):
                sp.wait_ge(sem(name), 16)
            sp.wait_ge(sem("out_y"), 64)

        @block.gpsimd
        def _(pool):
            def low(g):
                pool.wait_ge(sem("w_high"), g + 1)
                pool.tensor_tensor(wlo[g % 2][:], wraw[g % 2][:], whi[g % 2][:].bitcast(f32),
                                   ALU.subtract).then_inc(sem("w_split"), 1)

            pool.memset(ones, 1.0).then_inc(sem("ones_ready"), 1)
            pool.memset(pack[:], 0.0).then_inc(sem("pack_zero"), 1)
            for i in range(2):
                pool.memset(pad[i][:], 0.0).then_inc(sem("pad_zero"), 1)
            def sum_squares(src, dst, squared, link_, done):
                for k in range(1, KT):
                    pool.wait_ge(sem(squared), k + 1)
                    if k > 1:
                        pool.wait_ge(sem(link_), k - 1)
                    pool.tensor_tensor(dst, src[:, 0, :] if k == 1 else dst, src[:, k, :], ALU.add
                                       ).then_inc(sem(link_ if k < KT - 1 else done), 1)

            for g in range(N_IN):
                low(g)
                if g == 0:
                    sum_squares(sqx, rk[:], "x_squared", "pool_sum1", "x_added")
                if B_X <= g + 0 < B_X + KT:
                    c = g - B_X
                    if c == 0:
                        pool.wait_ge(sem("sc_arrived"), 16)
                        pool.wait_ge(sem("pad_zero"), 2)
                    if c >= 2:
                        pool.wait_ge(sem("conv_done"), c - 1)
                        pool.wait_ge(sem("cn_copied"), 2 * (c - 1))
                    pool.tensor_copy(samp(pad[c % 2])[:, :, 0:3], scv[:, c, :, :]).then_inc(sem("pad_state"), 1)
                if B_X <= g - 1 < B_X + KT:
                    c = g - 1 - B_X
                    pool.wait_ge(sem("pad_filled"), c + 1)
                    pool.tensor_copy(cn[:, c, 0:3], pad[c % 2][:, TP:TP + 3]).then_inc(sem("cn_copied"), 1)
                    pool.tensor_copy(cn[:, c, 3:27].rearrange("p (b w) -> p b w", w=3),
                                     samp(pad[c % 2])[:, :, TS:TS + 3]).then_inc(sem("cn_copied"), 1)

            pool.wait_ge(sem("xnat_ready"), 6)
            pool.wait_ge(sem("y_mm"), H)
            pool.wait_ge(sem("vec_arrived"), 16)
            for b in range(NB):
                pool.tensor_scalar(bms[:, b, :], bnat[0:SA, 4, :], vec[0:SA, V_BM + b:V_BM + b + 1], 1.0,
                                   ALU.mult, ALU.mult).then_inc(sem("bms_ready"), 1)
            for j in range(4):
                pool.wait_ge(sem("oh_ready"), j + 1)
                pool.tensor_tensor(catL[:, 4 + j, :], xc[:, j, :], catH[:, 4 + j, :].bitcast(f32), ALU.subtract
                                   ).then_inc(sem("ol_ready"), 1)
            pool.wait_ge(sem("kr_ready"), 1)
            pool.wait_ge(sem("hn_mm"), NB)
            pool.wait_ge(sem("g_summed"), 2)
            pool.wait_ge(sem("ol_ready"), 4)
            for h in range(H):
                m = pool.tensor_copy(KTt[64:96, h, :], krR[64:96, 0:TP])
            m.then_inc(sem("krope_ready"), 1)
            def spread(q):
                return pool.tensor_tensor(qpb[:], q.rearrange("p (a n) -> p a n", a=1).to_broadcast([P, 4, SA]),
                                          vec[:, V_QM:V_QM + 4].rearrange("p (a n) -> p a n", n=1)
                                          .to_broadcast([P, 4, SA]), ALU.mult)

            pool.wait_ge(sem("qabs_ready"), 2)
            pool.wait_ge(sem("qps_ready"), 1)
            pool.wait_ge(sem("qabs_mm"), 1)
            pool.wait_ge(sem("qrope_ready"), H)
            pool.wait_ge(sem("krope_ready"), 1)
            spread(qps[:, 0:SA]).then_inc(sem("qb_ready"), 1)
            with pool.Fori(1, NB) as b:
                pool.wait_ge(sem("s_mm"), b)
                spread(qps[:, bass.ds(b * SA, SA)]).then_inc(sem("qb_ready"), 1)
            pool.wait_ge(sem("s_mm"), NB)
            for g in range(B_OUT, B_OUT + 2):
                low(g)
            for d in range(KT):
                low(B_OUT + 2 + d)
                pool.wait_ge(sem("x2_squared"), d + 1)
                if d == 1:
                    pool.tensor_tensor(r2[:], sq2[:, 0, :], sq2[:, 1, :], ALU.add).then_inc(sem("pool_sum"), 1)
                elif d > 1:
                    pool.wait_ge(sem("pool_sum"), d - 1)
                    pool.tensor_tensor(r2[:], r2[:], sq2[:, d, :], ALU.add
                                       ).then_inc(sem("pool_sum" if d < KT - 1 else "x2_summed"), 1)
            pool.wait_ge(sem("x2_root"), 1)
            pool.tensor_copy(us[0][:, 0:1], vec[:, V_EPS:V_EPS + 1]).then_inc(sem("ul_ready"), 2)

            def low_at(g, u):
                pool.wait_ge(sem("w_high"), g + 1)
                pool.tensor_tensor(wlo[u][:], wraw[u][:], whi[u][:].bitcast(f32), ALU.subtract
                                   ).then_inc(sem("w_split"), 1)

            def low_hidden(n, u, slot):
                dst = uL[:, bass.ds(slot, 1), :].rearrange("p a n -> p (a n)")
                hi_ = uH[:, bass.ds(slot, 1), :].rearrange("p a n -> p (a n)").bitcast(f32)
                pool.wait_ge(sem("ru_free"), n + 3)
                pool.wait_ge(sem("uh_ready"), n + 1)
                pool.tensor_tensor(dst, us[u][:], hi_, ALU.subtract).then_inc(sem("ul_ready"), 1)

            def pool_quarter(q, last):
                g0 = q * 16 + B_MLP
                with pool.Fori(0, 4) as j:
                    for u in range(2):
                        low_at(g0 + 2 * j + 2 + u, u)
                        low_hidden(q * 8 + 2 * j + u, u, 2 * j + u)
                with pool.Fori(0, 3 if last else 4) as j:
                    for u in range(2):
                        low_at(g0 + 2 * j + 10 + u, u)

            with pool.Fori(0, QUARTERS - 1) as q:
                pool_quarter(q, False)
            pool_quarter(QUARTERS - 1, True)
            for d in range(KT):
                pool.wait_ge(sem("x3_squared"), d + 1)
                if d == 1:
                    pool.tensor_tensor(r2[:], sq2[:, 0, :], sq2[:, 1, :], ALU.add).then_inc(sem("pool_sum3"), 1)
                elif d > 1:
                    pool.wait_ge(sem("pool_sum3"), d - 1)
                    pool.tensor_tensor(r2[:], r2[:], sq2[:, d, :], ALU.add
                                       ).then_inc(sem("pool_sum3" if d < KT - 1 else "x3_summed"), 1)

        @block.scalar
        def _(act):
            chain = [0]

            def link(ins):
                chain[0] += 1
                ins.then_inc(sem("act_chain"), 1)
                act.wait_ge(sem("act_chain"), chain[0])

            def high(g):
                act.wait_ge(sem(f"w_arrived{g % 2}"), 16 * (g // 2 + 1))
                if g >= 2:
                    act.wait_ge(sem("gemm_done"), g - 1)
                act.activation(whi[g % 2][:], wraw[g % 2][:], ACT.Copy).then_inc(sem("w_high"), 1)

            act.dma_start(vec[:], vec_d).then_inc(sem("vec_arrived"), 16)
            for k in range(KT):
                act.wait_ge(sem(f"x_arrived{k // 2}"), 16)
                act.activation(sqx[:, k, :], xT[:, k, :], ACT.Square).then_inc(sem("x_squared"), 1)
                if k == 0:
                    high(0)
            high(1)
            act.dma_start(con[:, P:NC_], con_d[:, P:NC_]).then_inc(sem("con_arrived"), 16)
            act.wait_ge(sem("x_summed"), 1)
            act.wait_ge(sem("vec_arrived"), 16)
            act.activation(rx[:, 0:HALF], b4[:, 0:HALF], ACT.Sqrt, scale=1.0 / D, bias=vec[:, V_EPS:V_EPS + 1])
            act.activation(rx[:, HALF:T], b5[:, 0:HALF], ACT.Sqrt, scale=1.0 / D,
                           bias=vec[:, V_EPS:V_EPS + 1]).then_inc(sem("x_root"), 1)
            act.wait_ge(sem("x_split"), 2 * KT)
            act.wait_ge(sem("x_squared"), KT)
            act.dma_start(h0T[:], h0_d).then_inc(sem("h0_arrived"), 16)
            act.dma_start(scv[:], sc_d).then_inc(sem("sc_arrived"), 16)
            act.dma_start(wuq[:], wuq_d).then_inc(sem("small_weights"), 16)
            act.dma_start(wukT[:], wukT_d).then_inc(sem("small_weights"), 16)
            act.dma_start(wuk[:], wuk_d).then_inc(sem("small_weights"), 16)
            act.dma_start(wuv[:], wuv_d).then_inc(sem("small_weights"), 16)
            act.dma_start(ptb[:], pt_d).then_inc(sem("pt_arrived"), 16)
            for g in range(2, N_IN + 2):
                if g < N_IN:
                    high(g)
                if g == 4:
                    act.wait_ge(sem("evac"), 3)
                    act.wait_ge(sem("x_summed"), 1)
                    for i in range(3):
                        act.activation(sqq[:, i, :], qlat[:, i, :], ACT.Square).then_inc(sem("q_squared"), 1)
                if g == 6:
                    act.wait_ge(sem("evac"), 5)
                    for i in range(2):
                        act.activation(sqq[:, 3 + i, :], cT[:, i, :], ACT.Square).then_inc(sem("q_squared"), 1)
                if g == 7:
                    act.wait_ge(sem("q_summed"), 1)
                    act.activation(rq[:, 0:HALF], b4[:, 0:HALF], ACT.Sqrt, scale=1.0 / QL,
                                   bias=vec[:, V_EPS:V_EPS + 1])
                    act.activation(rq[:, HALF:T], b5[:, 0:HALF], ACT.Sqrt, scale=1.0 / QL,
                                   bias=vec[:, V_EPS:V_EPS + 1]).then_inc(sem("q_root"), 1)
                    act.wait_ge(sem("q_summed"), 2)
                    act.activation(rk[:, 0:HALF], b6[:, 0:HALF], ACT.Sqrt, scale=1.0 / CL,
                                   bias=vec[:, V_EPS:V_EPS + 1])
                    act.activation(rk[:, HALF:T], b7[:, 0:HALF], ACT.Sqrt, scale=1.0 / CL,
                                   bias=vec[:, V_EPS:V_EPS + 1]).then_inc(sem("q_root"), 1)
                    act.wait_ge(sem("evac"), B_SP + 1)
                    link(act.activation(dw[0][32:40, :], krw[32:40, :], ACT.Abs, bias=vec[32:40, V_DTB:V_DTB + 1]))
                    link(act.activation(dw[1][32:40, :], dw[0][32:40, :], ACT.Exp, scale=-1.0))
                    act.activation(dw[1][32:40, :], dw[1][32:40, :], ACT.Ln, bias=1.0).then_inc(sem("dt_ln"), 1)
                    act.activation(vec[32:40, V_AL:V_AL + 1], vec[32:40, V_AL:V_AL + 1], ACT.Exp
                                   ).then_inc(sem("dt_ln"), 1)
                if g == 9:
                    act.wait_ge(sem("dt_end"), 2)
                    act.activation(dw[1][32:40, :], dw[0][32:40, :], ACT.Exp).then_inc(sem("dt_decay"), 1)
                if g >= 9 and g - 9 < KT:
                    c = g - 9
                    act.wait_ge(sem("conv_done"), c + 1)
                    act.activation(xc[:, c, 0:TP], cacc[c % 2][:, 0:TP], ACT.Silu)
                    act.activation(xc[:, c, TP:T].rearrange("p (b w) -> p b w", w=TS),
                                   samp(cacc[c % 2])[:, :, 0:TS], ACT.Silu).then_inc(sem("silu_done"), 1)
            act.wait_ge(sem("acs_ready"), 1)
            act.activation(pack[96:104, :], acs[32:40, :], ACT.Exp).then_inc(sem("dt_decay"), 1)
            act.wait_ge(sem("pn_ready"), 1)
            act.wait_ge(sem("conv_done"), KT)
            for h in range(H):
                act.wait_ge(sem("diag_ready"), h + 1)
                if h >= 3:
                    act.wait_ge(sem("y_mm"), h - 2)
                e = ex[h % 3]
                for i in range(4):
                    m = act.activation(e[:, GOFF[i]:GOFF[i] + P], dgn[h % 2][:, i, :], ACT.Exp,
                                       bias=pn[:, i, h:h + 1])
                    if i < 3:
                        m = act.activation(e[:, GOFF[i] + P:GOFF[i + 1]], rows_bank[h % 4][:, P * i + P:TP], ACT.Exp,
                                           bias=pn[:, i, h:h + 1])
                m.then_inc(sem("ex_done"), 1)
            act.wait_ge(sem("sdiag_ready"), 1)
            act.activation(gs[:], gs[:], ACT.Exp).then_inc(sem("sex_done"), 1)
            act.wait_ge(sem("evac"), N_IN)
            act.activation(z[:], z[:], ACT.Silu).then_inc(sem("z_silu"), 1)
            for j in range(4):
                act.wait_ge(sem("gated"), j + 1)
                act.activation(z[:, j, :], xc[:, j, :], ACT.Square).then_inc(sem("g_squared"), 1)
            for c in range(2):
                act.wait_ge(sem("g_summed"), c + 1)
                for h in range(2):
                    bk = ((b4, b5), (b6, b7))[c][h]
                    m = act.activation(rg[:, c, h * HALF:(h + 1) * HALF], bk[:, 0:HALF], ACT.Sqrt,
                                       scale=1.0 / 256, bias=vec[:, V_EPS:V_EPS + 1])
                m.then_inc(sem("g_root"), 1)
            act.dma_start(c_o, cT[:]).then_inc(sem("out_c"), 16)
            act.dma_start(kr_o, krR[0:RP, :]).then_inc(sem("out_kr"), 16)
            act.wait_ge(sem("cn_copied"), 2 * KT)
            act.dma_start(cn_o, cn[:]).then_inc(sem("out_cn"), 16)
            act.wait_ge(sem("spo_ready"), 1)
            act.dma_start(sp_o, spo[:]).then_inc(sem("out_sp"), 16)
            act.wait_ge(sem("hn_ready"), NB)
            act.dma_start(ss_o, h0T[:]).then_inc(sem("out_ss"), 16)
            act.wait_ge(sem("hn_mm"), NB)
            act.wait_ge(sem("c_ready"), 2)
            for step in ("kv 0", "high 0", "kv 1", "high 1", "kv 2", "kv 3", "kv 4", "kv 5", "high 2", "high 3",
                         "kv 6", "kv 7"):
                what, u = step.split()
                u = int(u)
                if what == "high":
                    act.wait_ge(sem("o_ready"), u + 1)
                    act.activation(catH[:, 4 + u, :], xc[:, u, :], ACT.Copy).then_inc(sem("oh_ready"), 1)
                    continue
                act.wait_ge(sem("kv_mm"), u + 1)
                src = acc[u % 2][:, 0, :]
                if u < 4:
                    act.activation(KTt[0:64, 2 * u, :], src[0:64], ACT.Copy)
                    m = act.activation(KTt[0:64, 2 * u + 1, :], src[64:128], ACT.Copy)
                else:
                    m = act.activation(V[:, u - 4, :], src, ACT.Copy)
                m.then_inc(sem("kv_evac"), 1)
            def by_sequence(ap):
                return ap.rearrange("p (b h t) -> p h b t", b=NB, h=H)

            def by_head(ap):
                return ap.rearrange("p (h b t) -> p h b t", b=NB, h=H)

            act.wait_ge(sem("qabs_mm"), 1)
            for k in range(2):
                act.activation(by_sequence(qabs[:, k, :]), by_head(acc[0][:, k, :]), ACT.Copy
                               ).then_inc(sem("qabs_ready"), 1)
            act.wait_ge(sem("qps_mm"), 1)
            act.activation(by_sequence(qps[:]), by_head(b7[:]), ACT.Copy).then_inc(sem("qps_ready"), 1)
            act.wait_ge(sem("c64_mm"), 1)
            act.activation(c64[:], b6[0:SA, 0:256], ACT.Copy).then_inc(sem("c64_ready"), 1)

            sbank = [acc[1][:, 1, 384:512], b7[:, 0:256], acc[1][:, 1, 0:384], acc[1][:, 0, :]]
            off = [0, 128, 384, 768, 1280]

            def turned(b, quads):
                for q in quads:
                    act.wait_ge(sem("ct_mm"), b * 9 + q + 1)
                    bk = (b4, b5)[(b + q) % 2]
                    if q < 8:
                        act.activation(CTr[:, :, 256 * q:256 * q + 256].rearrange("p k (t n) -> p t k n", n=P),
                                       bk[:].rearrange("p (t k n) -> p t k n", k=2, n=P), ACT.Copy
                                       ).then_inc(sem("ct_evac"), 1)
                    else:
                        act.activation(KRr[:].rearrange("p a n -> p (a n)"), bk[:], ACT.Copy
                                       ).then_inc(sem("ct_evac"), 1)

            turned(0, range(9))
            for s in range(H):
                act.wait_ge(sem("nm_ready"), s + 1)
                for i in range(QT_N):
                    m = act.activation(Pm[:, off[i]:off[i + 1]], sbank[i], ACT.Exp, bias=mx[:, 4 + i:5 + i],
                                       scale=SCALE, accum_out=mx[:, 8 + i:9 + i])
                m.then_inc(sem("p_exp"), 1)
                if s + 1 < NB:
                    act.wait_ge(sem("s_mm"), s + 1)
                    turned(s + 1, range(8))
                else:
                    act.wait_ge(sem("s_mm"), NB)
                    for g in range(B_OUT, B_OUT + 2):
                        high(g)
                act.wait_ge(sem("shift_ready"), s + 1)
                act.activation(pS[:, 0:1024], sS[:, 0:1024], ACT.Exp, scale=SCALE)
                act.activation(pS[0:SA, 1024:1088], sS[0:SA, 1024:1088], ACT.Exp, scale=SCALE
                               ).then_inc(sem("sp_exp"), 1)
                act.wait_ge(sem("pt_mm"), s + 1)
                act.activation(PTm[:, 0:512], acc[1][:, 0, :], ACT.Copy)
                act.activation(PTm[:, 1024:1280], b7[:, 0:256], ACT.Copy).then_inc(sem("pt_act"), 1)
                if s + 1 < NB:
                    turned(s + 1, [8])
                rows = slice(DH * (s % 2), DH * (s % 2) + DH)
                act.wait_ge(sem("o_mm"), s + 1)
                act.activation(catH[rows, s // 2, 0:TP], acc[1][rows, 0, :], ACT.Copy).then_inc(sem("attn_high"), 1)
            act.wait_ge(sem("os_mm"), 1)
            act.activation(catH[:, 0:4, TP:T], b5[:, 0:256].rearrange("p (a n) -> p a n", a=4), ACT.Copy
                           ).then_inc(sem("osh_ready"), 1)

            for d in range(KT):
                high(B_OUT + 2 + d)
                act.wait_ge(sem("evac"), B_OUT + d + 1)
                act.activation(sq2[:, d, :], xT[:, d, :], ACT.Square).then_inc(sem("x2_squared"), 1)
            act.wait_ge(sem("x2_sum_mm"), 1)
            act.activation(r3[:, 0:HALF], b4[:, 0:HALF], ACT.Sqrt, scale=1.0 / D, bias=vec[:, V_EPS:V_EPS + 1])
            act.activation(r3[:, HALF:T], b5[:, 0:HALF], ACT.Sqrt, scale=1.0 / D,
                           bias=vec[:, V_EPS:V_EPS + 1]).then_inc(sem("x2_root"), 1)
            act.activation(ru[0][:, 0:1], vec[:, V_EPS:V_EPS + 1], ACT.Copy).then_inc(sem("ru_free"), 2)

            def high_at(g, u, pair):
                act.wait_ge(sem(f"w_arrived{u}"), pair * 16 + 16)
                act.wait_ge(sem("gemm_done"), g - 1)
                act.activation(whi[u][:], wraw[u][:], ACT.Copy).then_inc(sem("w_high"), 1)

            def square(n, u, g):
                act.wait_ge(sem("evac"), g + 1)
                act.wait_ge(sem("ul_ready"), n + 1)
                act.activation(us[u][:], ru[u][:], ACT.Square).then_inc(sem("ru_free"), 1)

            def act_quarter(q, last):
                g0 = q * 16 + B_MLP
                with act.Fori(0, 4) as j:
                    for u in range(2):
                        high_at(g0 + 2 * j + 2 + u, u, q * 8 + j + B_MLP // 2 + 1)
                        square(q * 8 + 2 * j + u, u, g0 + 2 * j + u)
                with act.Fori(0, 3 if last else 4) as j:
                    for u in range(2):
                        high_at(g0 + 2 * j + 10 + u, u, q * 8 + j + B_MLP // 2 + 5)

            with act.Fori(0, QUARTERS - 1) as q:
                act_quarter(q, False)
            act_quarter(QUARTERS - 1, True)
            for d in range(KT):
                act.wait_ge(sem("evac"), N_BLK - 8 + d + 1)
                act.activation(sq2[:, d, :], xT[:, d, :], ACT.Square).then_inc(sem("x3_squared"), 1)
            act.wait_ge(sem("x3_sum_mm"), 1)
            act.activation(r3[:, 0:HALF], b4[:, 0:HALF], ACT.Sqrt, scale=1.0 / D, bias=vec[:, V_EPS:V_EPS + 1])
            act.activation(r3[:, HALF:T], b5[:, 0:HALF], ACT.Sqrt, scale=1.0 / D,
                           bias=vec[:, V_EPS:V_EPS + 1]).then_inc(sem("x3_root"), 1)

        @block.vector
        def _(dve):
            chain = [0]

            def link(ins):
                chain[0] += 1
                ins.then_inc(sem("dve_chain"), 1)
                dve.wait_ge(sem("dve_chain"), chain[0])

            dve.wait_ge(sem("vec_arrived"), 16)
            for k in range(KT):
                dve.wait_ge(sem(f"x_arrived{k // 2}"), 16)
                g = vec[:, V_GATT + k:V_GATT + k + 1]
                dve.tensor_scalar(catH[:, k, :], xT[:, k, :], g, None, ALU.mult).then_inc(sem("x_split"), 1)
                dve.wait_ge(sem("x_split"), 2 * k + 1)
                dve.scalar_tensor_tensor(catL[:, k, :], xT[:, k, :], g, catH[:, k, :].bitcast(f32),
                                         ALU.mult, ALU.subtract).then_inc(sem("x_split"), 1)
            dve.wait_ge(sem("x_root"), 1)
            dve.reciprocal(rx[:], rx[:]).then_inc(sem("rx_ready"), 1)
            dve.wait_ge(sem("rx_ready"), 1)

            def evac(g, out):
                dve.wait_ge(sem("gemm_done"), g + 1)
                return dve.tensor_tensor(out, acc[g % 2][:, :, 0:HALF], halves(rx[:]), ALU.mult)

            def causal(c):
                dve.wait_ge(sem("cb_mm"), c + 1)
                for i, (bk, off) in enumerate(((b4, 0), (b5, 0), (b6, 0), (b5, 384))):
                    dve.tensor_tensor(cbm[:, c, GOFF[i]:GOFF[i] + P], bk[:, off:off + P], tri, ALU.mult)
                    if i < 3:
                        dve.tensor_copy(cbm[:, c, GOFF[i] + P:GOFF[i + 1]], bk[:, off + P:off + TP - P * i])
                dve.tensor_copy(cbs[:, c, :], b6[0:SA, 256:256 + SA]).then_inc(sem("cb_ready"), 1)

            for g in range(N_IN):
                if g == 17:
                    causal(0)
                if g == 12:
                    dve.wait_ge(sem("pack_tr"), 1)
                    dve.tensor_copy(pn[:, 0:4, :].rearrange("p a b -> p (a b)"), b4[:, 0:288])
                    dve.tensor_copy(pn[0:SA, 4, :], b4[0:SA, 288:360]).then_inc(sem("pn_ready"), 1)
                if g >= 11 and g - 11 < 6:
                    c = g - 11
                    dve.wait_ge(sem("x_tr"), c + 1)
                    dst = xnat[:, :, c * P:(c + 1) * P] if c < 4 else bnat[:, :, (c - 4) * P:(c - 3) * P]
                    bk = b5 if c % 2 == 0 else b6
                    dve.tensor_copy(dst[:, 0:4, :], bk[:].rearrange("p (a n) -> p a n", a=4))
                    dve.tensor_copy(dst[0:SA, 4, :], b7[0:SA, 0:P]).then_inc(sem("xnat_ready"), 1)
                if g == 15:
                    dve.wait_ge(sem("q_root"), 1)
                    dve.reciprocal(rq[:], rq[:]).then_inc(sem("rq_ready"), 1)
                if g < B_KV:
                    evac(g, halves(qlat[:, g, :])).then_inc(sem("evac"), 1)
                elif g < B_SP:
                    evac(g, halves(cT[:, g - B_KV, :])).then_inc(sem("evac"), 1)
                elif g == B_SP:
                    dve.wait_ge(sem("gemm_done"), g + 1)
                    dve.tensor_tensor(halves(krw[0:64, :]), acc[g % 2][0:64, :, 0:HALF], halves(rx[0:64, :]),
                                      ALU.mult).then_inc(sem("evac"), 1)
                    dve.wait_ge(sem("evac"), g + 1)
                    dve.wait_ge(sem("vec_arrived"), 16)
                    b = vec[32:40, V_DTB:V_DTB + 1]
                    dve.tensor_scalar(acs[32:40, :], krw[32:40, :], b, 0.0, ALU.add, ALU.max
                                      ).then_inc(sem("dt_pos"), 1)
                elif g < B_Z:
                    c = g - B_X
                    p_, q_ = pad[c % 2], cacc[c % 2]
                    dve.wait_ge(sem("gemm_done"), g + 1)
                    if c >= 2:
                        dve.wait_ge(sem("cn_copied"), 2 * (c - 1))
                        dve.wait_ge(sem("silu_done"), c - 1)
                    else:
                        dve.wait_ge(sem("pad_zero"), 2)
                    A = acc[g % 2]
                    dve.tensor_tensor(p_[:, 3:3 + HALF], A[:, 0, 0:HALF], rx[:, 0:HALF], ALU.mult)
                    dve.tensor_tensor(p_[:, 3 + HALF:3 + TP], A[:, 1, 0:TP - HALF], rx[:, HALF:TP], ALU.mult)
                    dve.tensor_tensor(samp(p_)[:, :, 3:3 + TS],
                                      A[:, 1, TP - HALF:HALF].rearrange("p (b w) -> p b w", w=TS),
                                      rx[:, TP:T].rearrange("p (b w) -> p b w", w=TS),
                                      ALU.mult).then_inc(sem("pad_filled"), 1)
                    dve.wait_ge(sem("pad_filled"), c + 1)
                    dve.wait_ge(sem("pad_state"), c + 1)
                    w = [vec[:, V_CW + CONV_K * c + k:V_CW + CONV_K * c + k + 1] for k in range(CONV_K)]
                    ins = dve.tensor_scalar(q_[:, 0:CW], p_[:, 0:CW], w[0], vec[:, V_CB + c:V_CB + c + 1],
                                            ALU.mult, ALU.add)
                    ins.then_inc(sem("evac"), 1)
                    dve.wait_ge(sem("evac"), g + 1)
                    for k in (1, 2):
                        link(dve.scalar_tensor_tensor(q_[:, 0:CW], p_[:, k:k + CW], w[k], q_[:, 0:CW],
                                                      ALU.mult, ALU.add))
                    dve.scalar_tensor_tensor(q_[:, 0:CW], p_[:, 3:3 + CW], w[3], q_[:, 0:CW],
                                             ALU.mult, ALU.add).then_inc(sem("conv_done"), 1)
                else:
                    evac(g, halves(z[:, g - B_Z, :])).then_inc(sem("evac"), 1)
                if g == 6:
                    dve.wait_ge(sem("q_squared"), 3)
                    for i in range(3):
                        dve.tensor_scalar(qlat[:, i, :], qlat[:, i, :], vec[:, V_GQ + i:V_GQ + i + 1], None,
                                          ALU.mult).then_inc(sem("qg_ready"), 1)
                    dve.wait_ge(sem("dt_ln"), 2)
                    dve.wait_ge(sem("dt_pos"), 1)
                    dve.wait_ge(sem("pack_zero"), 1)
                    link(dve.tensor_tensor(pack[32:40, :], acs[32:40, :], dw[1][32:40, :], ALU.add))
                    link(dve.tensor_scalar(dw[0][32:40, :], pack[32:40, :], vec[32:40, V_AL:V_AL + 1], -1.0,
                                           ALU.mult, ALU.mult))
                    dve.wait_ge(sem("con_arrived"), 16)
                    dve.tensor_tensor_scan(acs[32:40, :], con[32:40, C_RST:C_RST + T], dw[0][32:40, :], 0.0,
                                           ALU.mult, ALU.add).then_inc(sem("acs_ready"), 1)
                    dve.wait_ge(sem("acs_ready"), 1)
                    dve.tensor_scalar(pack[0:8, :], acs[32:40, :], -1.0, None, ALU.mult)
                    dve.tensor_scalar(dw[0][32:40, 0:TP], acs[32:40, 0:TP], -1.0, acs[32:40, TP - 1:TP],
                                      ALU.mult, ALU.add).then_inc(sem("dt_end"), 1)
                    sa = acs[32:40, TP:T].rearrange("p (b w) -> p b w", w=TS)
                    dve.tensor_tensor(dw[0][32:40, TP:T].rearrange("p (b w) -> p b w", w=TS),
                                      sa[:, :, TS - 1:TS].to_broadcast([8, NB, TS]), sa,
                                      ALU.subtract).then_inc(sem("dt_end"), 1)
                if g == 7:
                    dve.wait_ge(sem("q_root"), 2)
                    dve.wait_ge(sem("q_squared"), 5)
                    link(dve.reciprocal(rk[:], rk[:]))
                    for i in range(2):
                        dve.scalar_tensor_tensor(cT[:, i, :], cT[:, i, :], vec[:, V_GKV + i:V_GKV + i + 1],
                                                 rk[:], ALU.mult, ALU.mult).then_inc(sem("c_ready"), 1)
                if g == 8:
                    dve.wait_ge(sem("dt_decay"), 1)
                    dve.tensor_tensor(pack[64:72, :], pack[32:40, :], dw[1][32:40, :], ALU.mult
                                      ).then_inc(sem("pack_ready"), 1)
                    dve.wait_ge(sem("kr_mm"), 1)
                    dve.tensor_tensor(t1[:, 0:HALF], b4[:, 0:HALF], cosT[:, 0:HALF], ALU.mult)
                    link(dve.tensor_tensor(t1[:, HALF:T], b5[:, 0:HALF], cosT[:, HALF:T], ALU.mult))
                    dve.tensor_tensor(krR[:, 0:HALF], b6[:, 0:HALF], sinT[:, 0:HALF], ALU.mult)
                    link(dve.tensor_tensor(krR[:, HALF:T], b7[:, 0:HALF], sinT[:, HALF:T], ALU.mult))
                    dve.tensor_tensor(krR[:], krR[:], t1[:], ALU.add).then_inc(sem("kr_ready"), 1)
            causal(1)

            def diag_rows(h):
                dve.wait_ge(sem("rows_done"), h + 1)
                if h >= 2:
                    dve.wait_ge(sem("ex_done"), h - 1)
                dve.tensor_tensor(dgn[h % 2][:], rows_bank[h % 4].rearrange("p (a n) -> p a n", a=4),
                                  neg.rearrange("p (a n) -> p a n", a=1).to_broadcast([P, 4, P]),
                                  ALU.add).then_inc(sem("diag_ready"), 1)

            def take_y(j):
                dve.wait_ge(sem("y_mm"), 2 * j + 2)
                dve.scalar_tensor_tensor(xc[:, j, 0:TP], xc[:, j, 0:TP], vec[:, V_D + j:V_D + j + 1],
                                         acc[1][:, j % 2, :], ALU.mult, ALU.add).then_inc(sem("y_taken"), 1)

            dve.wait_ge(sem("cb_ready"), 2)
            dve.wait_ge(sem("pn_ready"), 1)
            diag_rows(0)
            for h in range(H):
                if h + 1 < H:
                    diag_rows(h + 1)
                dve.wait_ge(sem("ex_done"), h + 1)
                e = ex[h % 3]
                for i in range(4):
                    sl = slice(GOFF[i], GOFF[i + 1])
                    m = dve.scalar_tensor_tensor(e[:, sl], e[:, sl], pn[:, i, 32 + h:33 + h],
                                                 cbm[:, h // 4, sl], ALU.mult, ALU.mult)
                m.then_inc(sem("mix_ready"), 1)
                if h >= 3 and h % 2 == 1:
                    take_y(h // 2 - 1)
            dve.wait_ge(sem("srows_done"), 1)

            def heads(ap):
                return ap.rearrange("p (h n) -> p h n", n=1).to_broadcast([SA, H, SA])

            link(dve.tensor_tensor(gs[:], b4[0:SA, :].rearrange("p (h n) -> p h n", h=H),
                                   con[0:SA, C_SNEG:C_SNEG + SA].rearrange("p (a n) -> p a n", a=1)
                                   .to_broadcast([SA, H, SA]), ALU.add))
            dve.tensor_tensor(gs[:], gs[:], heads(pn[0:SA, 4, 0:8]), ALU.add).then_inc(sem("sdiag_ready"), 1)
            take_y(3)
            dve.wait_ge(sem("se_mm"), 1)
            dve.wait_ge(sem("mix_ready"), H)
            link(dve.tensor_copy(se[:], b7[:, 0:320]))
            dve.wait_ge(sem("sex_done"), 1)
            link(dve.tensor_tensor(gs[:], gs[:], heads(pn[0:SA, 4, 32:40]), ALU.mult))
            dve.tensor_tensor(gs[:].rearrange("p (g e) n -> p g e n", g=2),
                              gs[:].rearrange("p (g e) n -> p g e n", g=2),
                              cbs[:].rearrange("p g (a n) -> p g a n", a=1).to_broadcast([SA, 2, 4, SA]),
                              ALU.mult).then_inc(sem("smix_ready"), 1)
            dve.wait_ge(sem("yo_mm"), 1)
            link(dve.tensor_tensor(ysm[:].rearrange("p a n -> p (a n)"), b6[:, 0:256], se[:, 0:256], ALU.mult))
            dve.wait_ge(sem("ys_mm"), 1)
            dve.tensor_tensor(xnat[:, 0:4, :].rearrange("p a (h n) -> p a h n", h=H),
                              xnat[:, 0:4, :].rearrange("p a (h n) -> p a h n", h=H),
                              pn[:, 0:4, 64:72].rearrange("p a (h n) -> p a h n", n=1)
                              .to_broadcast([P, 4, H, DH]), ALU.mult).then_inc(sem("xdd_ready"), 1)
            dve.tensor_tensor(xnat[0:SA, 4, :].rearrange("p (h n) -> p h n", h=H),
                              xnat[0:SA, 4, :].rearrange("p (h n) -> p h n", h=H),
                              pn[0:SA, 4, 64:72].rearrange("p (h n) -> p h n", n=1)
                              .to_broadcast([SA, H, DH]), ALU.mult).then_inc(sem("xdd_ready"), 1)
            link(dve.tensor_tensor(ysm[:].rearrange("p a n -> p (a n)"), b5[:, 0:256],
                                   ysm[:].rearrange("p a n -> p (a n)"), ALU.add))
            for j in range(4):
                m = dve.scalar_tensor_tensor(xc[:, j, TP:T], xc[:, j, TP:T], vec[:, V_D + j:V_D + j + 1],
                                             ysm[:, j, :], ALU.mult, ALU.add)
            m.then_inc(sem("ys_taken"), 1)
            dve.wait_ge(sem("ys_taken"), 1)
            dve.wait_ge(sem("y_taken"), 4)
            dve.wait_ge(sem("z_silu"), 1)
            for j in range(4):
                dve.tensor_tensor(xc[:, j, :], xc[:, j, :], z[:, j, :], ALU.mult).then_inc(sem("gated"), 1)
            for b in range(NB):
                hb = h0T[:, b, :].rearrange("p (h n) -> p h n", h=H)
                if b == 0:
                    dve.wait_ge(sem("h0_arrived"), 16)
                link(dve.tensor_tensor(hb, hb, se[:, 256 + b:320:NB].rearrange("p (h n) -> p h n", n=1)
                                       .to_broadcast([P, H, DH]), ALU.mult))
                dve.wait_ge(sem("hn_mm"), b + 1)
                dve.tensor_tensor(h0T[:, b, :], h0T[:, b, :], acc[1][:, b % 2, :], ALU.add
                                  ).then_inc(sem("hn_ready"), 1)
                if b == 0:
                    dve.wait_ge(sem("sp_mm"), 1)
                    dve.tensor_copy(spo[:], acc[0][:, 0, :]).then_inc(sem("spo_ready"), 1)
            for c in range(2):
                dve.wait_ge(sem("g_root"), c + 1)
                link(dve.reciprocal(rg[:, c, :], rg[:, c, :]))
                for i in range(2):
                    j = 2 * c + i
                    dve.scalar_tensor_tensor(xc[:, j, :], xc[:, j, :], vec[:, V_GS + j:V_GS + j + 1],
                                             rg[:, c, :], ALU.mult, ALU.mult).then_inc(sem("o_ready"), 1)
            dve.wait_ge(sem("oh_ready"), 4)
            dve.wait_ge(sem("ol_ready"), 4)
            dve.wait_ge(sem("rq_ready"), 1)
            for n, u in enumerate(Q_ORDER):
                dve.wait_ge(sem("q_mm"), n + 1)
                pr, sa = acc[n % 2][:, 0, :], acc[n % 2][:, 1, 0:SA]
                if u < 4:
                    for e in range(2):
                        rows = slice(64 * e, 64 * e + 64)
                        dve.tensor_tensor(QT[0:64, 2 * u + e, :], pr[rows], rq[rows, 0:TP], ALU.mult)
                        m = dve.tensor_tensor(qs[:, 2 * u + e, :], sa[rows], rq[rows, TP:T], ALU.mult)
                else:
                    dve.tensor_tensor(qp[:, u - 4, 0:TP], pr, rq[:, 0:TP], ALU.mult)
                    m = dve.tensor_tensor(qp[:, u - 4, TP:T], sa, rq[:, TP:T], ALU.mult)
                m.then_inc(sem("q_evac"), 1)
            dve.wait_ge(sem("q_evac"), 6)

            def both(ap):
                return ap.rearrange("p (a n) -> p a n", a=1).to_broadcast([P, 2, ap.shape[1]])

            dve.tensor_tensor(tq[0][:], qp[:], both(cosT), ALU.mult)
            dve.wait_ge(sem("rot_mm"), 1)
            for i in range(2):
                dve.tensor_tensor(tq[1][:, i, 0:TP], (b4, b5)[i][:], sinT[:, 0:TP], ALU.mult)
            link(dve.tensor_tensor(tq[1][:, :, TP:T], b6[:, 0:2 * SA].rearrange("p (a n) -> p a n", a=2),
                                   both(sinT[:, TP:T]), ALU.mult))
            dve.wait_ge(sem("out_cn"), 16)
            dve.tensor_tensor(qrs[:], tq[0][:, :, TP:T], tq[1][:, :, TP:T], ALU.add).then_inc(sem("qrs_ready"), 1)
            for h in range(H):
                rows = slice(RP * (h % 4), RP * (h % 4) + RP)
                dve.tensor_tensor(QT[64:96, h, :], tq[0][rows, h // 4, 0:TP], tq[1][rows, h // 4, 0:TP],
                                  ALU.add).then_inc(sem("qrope_ready"), 1)
            dve.wait_ge(sem("snew_mm"), 1)
            dve.tensor_tensor(snew[:], acc[1][0:SA, 0, :], con[0:SA, C_SM:C_SM + 512], ALU.add
                              ).then_inc(sem("snew_ready"), 1)

            sbank = [acc[1][:, 1, 384:512], b7[:, 0:256], acc[1][:, 1, 0:384], acc[1][:, 0, :]]
            am = con[:, C_AM:C_AM + P]
            off = [0, 128, 384, 768, 1280]
            sscore = acc[0][:].rearrange("p a (t q) -> p (a t) q", q=SA)
            dve.memset(mxs[:, SA:P], 0.0)
            dve.wait_ge(sem("out_c"), 16)
            dve.wait_ge(sem("out_sp"), 16)
            for s in range(H):
                dve.wait_ge(sem("score_mm"), s + 1)
                for i in range(QT_N):
                    dve.tensor_tensor(sbank[i][:, P * i:P * i + P], sbank[i][:, P * i:P * i + P], am, ALU.add
                                      ).then_inc(sem("score_masked"), 1)
                for i in range(QT_N):
                    dve.wait_ge(sem("score_masked"), 4 * s + i + 1)
                    m = dve.reduce_max(mx[:, i:i + 1], sbank[i], AX.X, negate=True)
                link(m)
                dve.tensor_scalar(mx[:, 4:8], mx[:, 0:4], SCALE, None, ALU.mult).then_inc(sem("nm_ready"), 1)
                dve.wait_ge(sem("p_exp"), s + 1)
                link(dve.reciprocal(mx[:, 8:12], mx[:, 8:12]))
                for i in range(QT_N):
                    sl = Pm[:, off[i]:off[i + 1]]
                    m = dve.tensor_scalar(sl, sl, mx[:, 8 + i:9 + i], None, ALU.mult)
                m.then_inc(sem("p_norm"), 1)
                sn = snew[:, s * SA:s * SA + SA]
                dve.wait_ge(sem("s_mm"), s + 1)
                link(dve.reduce_max(mxs[:, 0:SA], sscore.rearrange("p t q -> p q t"), AX.X))
                dve.tensor_tensor(mxs[0:SA, 0:SA], mxs[0:SA, 0:SA], sn, ALU.max).then_inc(sem("smax_ready"), 1)
                dve.wait_ge(sem("smax_tr"), s + 1)
                link(dve.reduce_max(rm[:], b6[0:SA, 128:256], AX.X))
                dve.tensor_scalar(dgm[:], ident[0:SA, 0:SA], rm[:], None, ALU.mult).then_inc(sem("sdiag2_ready"), 1)
                dve.wait_ge(sem("smax_mm"), s + 1)
                link(dve.tensor_copy(mxs[:, 0:SA], b6[:, 256:256 + SA]))
                dve.tensor_tensor(sS[:, 0:1024].rearrange("p (t q) -> p t q", q=SA), sscore,
                                  mxs[:, 0:SA].rearrange("p (a q) -> p a q", a=1).to_broadcast([P, NPG, SA]),
                                  ALU.subtract)
                dve.tensor_tensor(sS[0:SA, 1024:1088], sn, mxs[0:SA, 0:SA], ALU.subtract
                                  ).then_inc(sem("shift_ready"), 1)
                dve.wait_ge(sem("pt_mm"), s + 1)
                dve.tensor_copy(PTm[:, 512:1024], acc[1][:, 1, :]).then_inc(sem("pt_dve"), 1)
                dve.wait_ge(sem("sp_exp"), s + 1)
                link(dve.reduce_sum(psm[:], pS[:, 0:1024].rearrange("p (t q) -> p q t", q=SA), AX.X))
                dve.tensor_tensor(psm[0:SA, :], psm[0:SA, :], pS[0:SA, 1024:1088], ALU.add
                                  ).then_inc(sem("psum_ready"), 1)
                rows = slice(DH * (s % 2), DH * (s % 2) + DH)
                dve.wait_ge(sem("attn_high"), s + 1)
                dve.tensor_tensor(catL[rows, s // 2, 0:TP], acc[1][rows, 0, :],
                                  catH[rows, s // 2, 0:TP].bitcast(f32), ALU.subtract).then_inc(sem("attn_low"), 1)
                dve.wait_ge(sem("den_mm"), s + 1)
                link(dve.reciprocal(rsm[:], b6[:, 320:320 + SA]))
                dve.wait_ge(sem("pv_mm"), s + 1)
                dve.tensor_tensor(olat[:, :, s * SA:s * SA + SA],
                                  b6[:, 0:2 * SA].rearrange("p (a n) -> p a n", a=2), both(rsm[:]), ALU.mult
                                  ).then_inc(sem("olat_ready"), 1)
            dve.wait_ge(sem("osh_ready"), 1)
            dve.tensor_tensor(catL[:, 0:4, TP:T], b5[:, 0:256].rearrange("p (a n) -> p a n", a=4),
                              catH[:, 0:4, TP:T].bitcast(f32), ALU.subtract).then_inc(sem("osl_ready"), 1)

            dve.wait_ge(sem("out_kr"), 16)
            dve.wait_ge(sem("x_again"), 16)
            for d in range(KT):
                g = B_OUT + d
                dve.wait_ge(sem("gemm_done"), g + 1)
                dve.tensor_tensor(halves(xT[:, d, :]), acc[g % 2][:, :, 0:HALF], halves(xT[:, d, :]), ALU.add
                                  ).then_inc(sem("evac"), 1)
                dve.wait_ge(sem("evac"), g + 1)
                gm = vec[:, V_GM + d:V_GM + d + 1]
                dve.tensor_scalar(x2H[:, d, :], xT[:, d, :], gm, None, ALU.mult).then_inc(sem("x2_split"), 1)
                dve.wait_ge(sem("x2_split"), 2 * d + 1)
                dve.scalar_tensor_tensor(x2L[:, d, :], xT[:, d, :], gm, x2H[:, d, :].bitcast(f32),
                                         ALU.mult, ALU.subtract).then_inc(sem("x2_split"), 1)

            def up_out(n, g, u):
                dve.wait_ge(sem("gemm_done"), g + 1)
                dve.wait_ge(sem("ru_free"), n + 1)
                dve.scalar_tensor_tensor(halves(ru[u][:]), acc[u][:, :, 0:HALF], 0.0, halves(r3[:]),
                                         ALU.max, ALU.mult).then_inc(sem("evac"), 1)
                dve.wait_ge(sem("evac"), g + 1)

            def up_high(n, u, slot):
                dve.tensor_tensor(uH[:, slot, :] if isinstance(slot, int) else
                                  uH[:, bass.ds(slot, 1), :].rearrange("p a n -> p (a n)"),
                                  ru[u][:], ru[u][:], ALU.mult).then_inc(sem("uh_ready"), 1)

            def down_out(g, u, d):
                x_ = xT[:, bass.ds(d, 1), :].rearrange("p a (h n) -> p (a h) n", h=2)
                dve.wait_ge(sem("gemm_done"), g + 1)
                dve.tensor_tensor(x_, acc[u][:, :, 0:HALF], x_, ALU.add).then_inc(sem("evac"), 1)

            dve.wait_ge(sem("x2_root"), 1)
            dve.reciprocal(r3[:], r3[:]).then_inc(sem("r3_ready"), 1)
            dve.wait_ge(sem("r3_ready"), 1)
            with dve.Fori(0, QUARTERS) as q:
                with dve.Fori(0, 4) as j:
                    for u in range(2):
                        up_out(q * 8 + 2 * j + u, q * 16 + 2 * j + B_MLP + u, u)
                        up_high(None, u, 2 * j + u)
                with dve.Fori(0, 4) as j:
                    for u in range(2):
                        down_out(q * 16 + 2 * j + B_MLP + 8 + u, u, 2 * j + u)
            dve.wait_ge(sem("x3_root"), 1)
            link(dve.reciprocal(r3[:], r3[:]))
            for d in range(KT):
                dve.scalar_tensor_tensor(sq2[:, d, :], xT[:, d, :], vec[:, V_GF + d:V_GF + d + 1], r3[:],
                                         ALU.mult, ALU.mult).then_inc(sem("y_ready"), 1)

        @block.tensor
        def _(pe):
            def gemm(u, xh, xl, order=range(KT), before=None):
                n = 0
                for k in order:
                    if before:
                        before(k)
                    for h in range(2):
                        cols = slice(h * HALF, (h + 1) * HALF)
                        for q, (a, b) in enumerate(((whi, xh), (whi, xl), (wlo, xh))):
                            m = pe.matmul(acc[u][:, h, 0:HALF], a[u][:, k, :], b[:, k, cols],
                                          start=n == 0 and q == 0, stop=n == KT - 1 and q == 2)
                    n += 1
                m.then_inc(sem("gemm_done"), 1)

            def block_ready(g):
                pe.wait_ge(sem("w_split"), g + 1)
                if isinstance(g, int) and g < 2:
                    return
                pe.wait_ge(sem("evac"), g - 1)

            for g in range(N_IN):
                block_ready(g)
                gemm(g % 2, catH, catL,
                     before=(lambda k: pe.wait_ge(sem("x_split"), 2 * k + 2)) if g == 0 else None)
                if g == 0:
                    pe.wait_ge(sem("ones_ready"), 1)
                    pe.wait_ge(sem("x_added"), 1)
                    for h in range(2):
                        m = pe.matmul((b4, b5)[h][:, 0:HALF], ones, rk[:, h * HALF:(h + 1) * HALF],
                                      start=True, stop=True)
                    m.then_inc(sem("x_summed"), 1)
                if g == 5:
                    pe.wait_ge(sem("x_root"), 1)
                    pe.wait_ge(sem("q_squared"), 3)
                    for h, bk in ((0, b4), (1, b5)):
                        for i in range(3):
                            m = pe.matmul(bk[:, 0:HALF], ones, sqq[:, i, h * HALF:(h + 1) * HALF],
                                          start=i == 0, stop=i == 2)
                    m.then_inc(sem("q_summed"), 1)
                    pe.wait_ge(sem("q_squared"), 5)
                    for h, bk in ((0, b6), (1, b7)):
                        for i in range(2):
                            m = pe.matmul(bk[:, 0:HALF], ones, sqq[:, 3 + i, h * HALF:(h + 1) * HALF],
                                          start=i == 0, stop=i == 1)
                    m.then_inc(sem("q_summed"), 1)
                if g == 7:
                    pe.wait_ge(sem("q_root"), 2)
                    for lhs, (ba, bb) in ((con[0:RP, C_REP:C_REP + P], (b4, b5)),
                                          (con[0:RP, C_RREP:C_RREP + P], (b6, b7))):
                        for h, bk in ((0, ba), (1, bb)):
                            m = pe.matmul(bk[:, 0:HALF], lhs, krw[0:RP, h * HALF:(h + 1) * HALF],
                                          start=True, stop=True)
                    m.then_inc(sem("kr_mm"), 1)
                if g == 10:
                    pe.wait_ge(sem("kr_ready"), 1)
                if g == 11:
                    pe.wait_ge(sem("pack_ready"), 1)
                    for i in range(5):
                        n = P if i < 4 else SA
                        m = pe.transpose(b4[0:n, 72 * i:72 * i + 72], pack[0:72, P * i:P * i + n],
                                         ident[0:72, 0:72])
                    m.then_inc(sem("pack_tr"), 1)
                if g >= 10 and g - 10 < 6:
                    c = g - 10
                    pe.wait_ge(sem("silu_done"), c + 1)
                    if c >= 1:
                        pe.wait_ge(sem("xnat_ready"), c)
                    bk = b5 if c % 2 == 0 else b6
                    for i in range(5):
                        n = P if i < 4 else SA
                        m = pe.transpose(bk[:, P * i:P * i + P] if i < 4 else b7[0:SA, 0:P],
                                         xc[:, c, P * i:P * i + n], ident)
                    m.then_inc(sem("x_tr"), 1)
                if g >= 16:
                    c = g - 16
                    pe.wait_ge(sem("silu_done"), KT)
                    pe.wait_ge(sem("xnat_ready"), 6)
                    if c:
                        pe.wait_ge(sem("cb_ready"), 1)
                    for i, (bk, off) in enumerate(((b4, 0), (b5, 0), (b6, 0), (b5, 384))):
                        m = pe.matmul(bk[:, off:off + TP - P * i], xc[:, 4 + c, P * i:P * i + P],
                                      xc[:, 6 + c, P * i:TP], start=True, stop=True)
                    m = pe.matmul(b6[0:SA, 256:256 + SA], xc[:, 4 + c, TP:T], xc[:, 6 + c, TP:T],
                                  start=True, stop=True)
                    m.then_inc(sem("cb_mm"), 1)

            def decay_rows(h):
                if h >= 4:
                    pe.wait_ge(sem("ex_done"), h - 3)
                elif h >= 2:
                    pe.wait_ge(sem("cb_ready"), 2)
                else:
                    pe.wait_ge(sem("evac"), N_IN)
                pe.matmul(rows_bank[h % 4], ident[32:40, 32 + h:33 + h].to_broadcast([8, P]),
                          acs[32:40, 0:TP], start=True, stop=True).then_inc(sem("rows_done"), 1)

            for h in range(3):
                decay_rows(h)
            for h in range(H):
                if h + 3 < H:
                    decay_rows(h + 3)
                j = h // 2
                pe.wait_ge(sem("mix_ready"), h + 1)
                if j >= 2:
                    pe.wait_ge(sem("y_taken"), j - 1)
                for i in range(4):
                    m = pe.matmul(acc[1][64 * (h % 2):64 * (h % 2) + 64, j % 2, P * i:TP],
                                  xnat[:, i, 64 * h:64 * h + 64], ex[h % 3][:, GOFF[i]:GOFF[i + 1]],
                                  start=i == 0, stop=i == 3)
                m.then_inc(sem("y_mm"), 1)
            pe.wait_ge(sem("cb_ready"), 2)
            for h in range(H):
                m = pe.matmul(b4[0:SA, SA * h:SA * h + SA], ident[32:40, 32 + h:33 + h].to_broadcast([8, SA]),
                              acs[32:40, TP:T], start=True, stop=True)
            m.then_inc(sem("srows_done"), 1)
            e8 = pack[96:104, :]
            for h in range(H):
                sel = ident[96:104, 96 + h:97 + h]
                pe.matmul(b7[64 * (h % 2):64 * (h % 2) + 64, SA * (h // 2):SA * (h // 2) + SA],
                          sel.to_broadcast([8, 64]), e8[:, TP:T], start=True, stop=True)
            for h in range(H):
                sel = ident[96:104, 96 + h:97 + h]
                m = pe.matmul(b7[:, 256 + NB * h:256 + NB * h + NB], sel.to_broadcast([8, P]),
                              e8[:, TP + TS - 1:T:TS], start=True, stop=True)
            m.then_inc(sem("se_mm"), 1)
            pe.wait_ge(sem("h0_arrived"), 16)
            for b in range(NB):
                for j in range(4):
                    m = pe.matmul(b6[:, SA * j + TS * b:SA * j + TS * b + TS], h0T[:, b, P * j:P * j + P],
                                  xc[:, 6 + j // 2, TP + TS * b:TP + TS * b + TS], start=True, stop=True)
            m.then_inc(sem("yo_mm"), 1)
            pe.wait_ge(sem("smix_ready"), 1)
            for h in range(H):
                m = pe.matmul(b5[64 * (h % 2):64 * (h % 2) + 64, SA * (h // 2):SA * (h // 2) + SA],
                              xnat[0:SA, 4, 64 * h:64 * h + 64], gs[:, h, :], start=True, stop=True)
            m.then_inc(sem("ys_mm"), 1)
            pe.wait_ge(sem("xdd_ready"), 1)
            for c in range(2):
                for i in range(4):
                    m = pe.matmul(acc[0][:, 0, 256 * c:256 * c + 256], bnat[:, i, P * c:P * c + P],
                                  xnat[:, i, 256 * c:256 * c + 256], start=i == 0, stop=i == 3)
            m.then_inc(sem("sp_mm"), 1)
            pe.wait_ge(sem("bms_ready"), NB)
            pe.wait_ge(sem("xdd_ready"), 2)
            pe.wait_ge(sem("y_taken"), 4)
            for b in range(NB):
                if b >= 2:
                    pe.wait_ge(sem("hn_ready"), b - 1)
                for c in range(2):
                    m = pe.matmul(acc[1][:, b % 2, 256 * c:256 * c + 256], bms[:, b, P * c:P * c + P],
                                  xnat[0:SA, 4, 256 * c:256 * c + 256], start=True, stop=True)
                m.then_inc(sem("hn_mm"), 1)
            pe.wait_ge(sem("ys_taken"), 1)
            for c in range(2):
                for h, bk in ((0, (b4, b6)[c]), (1, (b5, b7)[c])):
                    for i in range(2):
                        if h == 0:
                            pe.wait_ge(sem("g_squared"), 2 * c + i + 1)
                        m = pe.matmul(bk[:, 0:HALF], ones, z[:, 2 * c + i, h * HALF:(h + 1) * HALF],
                                      start=i == 0, stop=i == 1)
                m.then_inc(sem("g_summed"), 1)
            pe.wait_ge(sem("hn_ready"), NB)
            pe.wait_ge(sem("spo_ready"), 1)
            pe.wait_ge(sem("small_weights"), 64)
            for u in range(8):
                if u >= 2:
                    pe.wait_ge(sem("kv_evac"), u - 1)
                for k in range(2):
                    if u < 4:
                        lhs, rhs = wukT[:, k, P * u:P * u + P], cT[:, k, 0:TP]
                    else:
                        lhs, rhs = cT[:, k, P * (u - 4):P * (u - 3)], wuv[:, k, :]
                    m = pe.matmul(acc[u % 2][:, 0, :], lhs, rhs, start=k == 0, stop=k == 1)
                m.then_inc(sem("kv_mm"), 1)
            pe.wait_ge(sem("qg_ready"), 3)
            for n, u in enumerate(Q_ORDER):
                if n == 4:
                    pe.wait_ge(sem("g_root"), 2)
                    pe.wait_ge(sem("q_evac"), 2)
                    for i in range(2):
                        pe.matmul((b4, b5)[i][:], rot, qp[:, i, 0:TP], start=True, stop=True)
                        m = pe.matmul(b6[:, SA * i:SA * i + SA], rot, qp[:, i, TP:T], start=True, stop=True)
                    m.then_inc(sem("rot_mm"), 1)
                if n < 2:
                    pe.wait_ge(sem("kv_evac"), 7 + n)
                else:
                    pe.wait_ge(sem("q_evac"), n - 1)
                for k in range(3):
                    w = wuq[:, k, P * u:P * u + P]
                    pe.matmul(acc[n % 2][:, 0, :], w, qlat[:, k, 0:TP], start=k == 0, stop=k == 2)
                    m = pe.matmul(acc[n % 2][:, 1, 0:SA], w, qlat[:, k, TP:T], start=k == 0, stop=k == 2)
                m.then_inc(sem("q_mm"), 1)
            pe.wait_ge(sem("q_evac"), 6)
            for h in range(H):
                for k in range(2):
                    m = pe.matmul(acc[0][:, k, SA * h:SA * h + SA], wuk[:, h, P * k:P * k + P], qs[:, h, :],
                                  start=True, stop=True)
            m.then_inc(sem("qabs_mm"), 1)
            pe.wait_ge(sem("qrs_ready"), 1)
            for h in range(H):
                m = pe.matmul(b7[:, SA * h:SA * h + SA], con[:, C_REP + P * (h % 4):C_REP + P * (h % 4) + P],
                              qrs[:, h // 4, :], start=True, stop=True)
            m.then_inc(sem("qps_mm"), 1)
            for k in range(2):
                m = pe.transpose(b6[0:SA, P * k:P * k + P], cT[:, k, TP:T], ident)
            m.then_inc(sem("c64_mm"), 1)

            def turns(b, quads):
                u = b % 2
                for q in quads:
                    if q in (0, 4):
                        pe.wait_ge(sem(f"cache{u}_half{q // 4}"), NPG // 2 * 16 * (b // 2 + 1))
                    if q == 8:
                        pe.wait_ge(sem(f"cache{u}_rotary"), NPG * 16 * (b // 2 + 1))
                    if b * 9 + q >= 2:
                        pe.wait_ge(sem("ct_evac"), b * 9 + q - 1)
                    for j in range(4):
                        if q < 8:
                            src = ckv[u][:, 2 * q + j // 2, P * (j % 2):P * (j % 2) + P]
                        else:
                            src = ckr[u][:, 4 * j:4 * j + 4, :].rearrange("p a n -> p (a n)")
                        m = pe.transpose((b4, b5)[(b + q) % 2][:, P * j:P * j + P], src, ident)
                    m.then_inc(sem("ct_mm"), 1)

            sbank = [acc[1][:, 1, 384:512], b7[:, 0:256], acc[1][:, 1, 0:384], acc[1][:, 0, :]]
            off = [0, 128, 384, 768]
            turns(0, range(0, 4))
            pe.wait_ge(sem("qabs_ready"), 2)
            pe.wait_ge(sem("qps_ready"), 1)
            for k in range(2):
                pe.matmul(acc[1][0:SA, 0, :], cT[:, k, TP:T], qabs[:, k, :], start=k == 0, stop=False)
            pe.matmul(acc[1][0:SA, 0, :], krR[0:RP, TP:T], qps[0:RP, :], start=False, stop=True
                      ).then_inc(sem("snew_mm"), 1)
            turns(0, range(4, 9))
            pe.wait_ge(sem("qrope_ready"), H)
            pe.wait_ge(sem("krope_ready"), 1)
            for s in range(H):
                for i in range(QT_N):
                    if s == 0 and i == QT_N - 1:
                        pe.wait_ge(sem("snew_ready"), 1)
                    if s and i == QT_N - 1:
                        pe.wait_ge(sem("attn_low"), s)
                    m = pe.matmul(sbank[i], QT[:, s, P * i:P * i + P], KTt[:, s, 0:P * (i + 1)],
                                  start=True, stop=True)
                m.then_inc(sem("score_mm"), 1)
                pe.wait_ge(sem("ct_evac"), s * 9 + 9)
                pe.wait_ge(sem("qb_ready"), s + 1)
                for a in range(NPG // 4):
                    pe.matmul(acc[0][:, a // 2, 256 * (a % 2):256 * (a % 2) + 256], KRr[:, a, :],
                              qpb[:].rearrange("p a n -> p (a n)"), start=True, stop=False)
                    for t in range(4 * a, 4 * a + 4):
                        for k in range(2):
                            m = pe.matmul(acc[0][:, t // 8, SA * (t % 8):SA * (t % 8) + SA],
                                          CTr[:, k, P * t:P * t + P], qabs[:, k, s * SA:s * SA + SA],
                                          start=False, stop=k == 1 and t % 4 == 3)
                m.then_inc(sem("s_mm"), 1)
                if s + 1 < NB:
                    turns(s + 1, range(0, 4))
                if s == 0:
                    pe.wait_ge(sem("c64_ready"), 1)
                pe.wait_ge(sem("smax_ready"), s + 1)
                pe.transpose(b6[:, 128:256], mxs[:], ident).then_inc(sem("smax_tr"), 1)
                if s + 1 < NB:
                    turns(s + 1, range(4, 6))
                pe.wait_ge(sem("sdiag2_ready"), s + 1)
                pe.matmul(b6[:, 256:256 + SA], ones[0:SA, :], dgm[:], start=True, stop=True
                          ).then_inc(sem("smax_mm"), 1)
                if s + 1 < NB:
                    turns(s + 1, range(6, 8))
                pe.wait_ge(sem("p_norm"), s + 1)
                for k in range(QT_N):
                    for i in range(k, QT_N):
                        c = GOFF[k] + P * (i - k)
                        m = pe.transpose((acc[1][:, 0, :], acc[1][:, 1, :], b7)[c // 512][:, c % 512:c % 512 + P],
                                         Pm[:, off[i] + P * k:off[i] + P * k + P], ident)
                m.then_inc(sem("pt_mm"), 1)
                pe.wait_ge(sem("sp_exp"), s + 1)
                for k in range(2):
                    for t in range(NPG):
                        pe.matmul(b6[:, SA * k:SA * k + SA], ckv[s % 2][:, t, P * k:P * k + P],
                                  pS[:, SA * t:SA * t + SA], start=t == 0, stop=False)
                    m = pe.matmul(b6[:, SA * k:SA * k + SA], c64[:, P * k:P * k + P], pS[0:SA, 1024:1088],
                                  start=False, stop=True)
                m.then_inc(sem("pv_mm"), 1)
                if s + 1 < NB:
                    turns(s + 1, [8])
                pe.wait_ge(sem("pt_act"), s + 1)
                pe.wait_ge(sem("pt_dve"), s + 1)
                for k in range(QT_N):
                    m = pe.matmul(acc[1][DH * (s % 2):DH * (s % 2) + DH, 0, P * k:TP], V[:, k, DH * s:DH * s + DH],
                                  PTm[:, GOFF[k]:GOFF[k + 1]], start=k == 0, stop=k == 3)
                m.then_inc(sem("o_mm"), 1)
                pe.wait_ge(sem("psum_ready"), s + 1)
                pe.matmul(b6[:, 320:320 + SA], ones, psm[:], start=True, stop=True).then_inc(sem("den_mm"), 1)

            pe.wait_ge(sem("olat_ready"), NB)
            for h in range(H):
                for k in range(2):
                    rhs = olat[:, k, :].rearrange("p (b h t) -> p h b t", b=NB, h=H)[:, h, :, :]
                    m = pe.matmul(b5[64 * (h % 2):64 * (h % 2) + 64, SA * (h // 2):SA * (h // 2) + SA],
                                  wuv[:, k, 64 * h:64 * h + 64], rhs, start=k == 0, stop=k == 1)
            m.then_inc(sem("os_mm"), 1)

            pe.wait_ge(sem("oh_ready"), 4)
            pe.wait_ge(sem("ol_ready"), 4)

            def heads_ready(k):
                if k < 4:
                    pe.wait_ge(sem("osl_ready"), 1)

            for g in range(B_OUT, B_MLP):
                block_ready(g)
                gemm(g % 2, catH, catL, order=[4, 5, 6, 7, 0, 1, 2, 3], before=heads_ready if g == B_OUT else None)

            def up(g, u, before=None):
                block_ready(g)
                gemm(u, x2H, x2L, before=before)

            def down(g, u, q, first):
                block_ready(g)
                gemm(u, uH, uL, before=(lambda k: pe.wait_ge(sem("ul_ready"), q * 8 + k + 3)) if first else None)

            def quarter(q, peel):
                g0 = q * 16 + B_MLP
                if peel:
                    up(g0, 0, before=lambda k: pe.wait_ge(sem("x2_split"), 2 * k + 2))
                    pe.wait_ge(sem("x2_summed"), 1)
                    for h in range(2):
                        m = pe.matmul((b4, b5)[h][:, 0:HALF], ones, r2[:, h * HALF:(h + 1) * HALF],
                                      start=True, stop=True)
                    m.then_inc(sem("x2_sum_mm"), 1)
                    up(g0 + 1, 1)
                else:
                    up(g0, 0)
                    up(g0 + 1, 1)
                with pe.Fori(1, 4) as j:
                    up(g0 + 2 * j, 0)
                    up(g0 + 2 * j + 1, 1)
                down(g0 + 8, 0, q, True)
                down(g0 + 9, 1, q, False)
                with pe.Fori(1, 4) as j:
                    down(g0 + 2 * j + 8, 0, q, False)
                    down(g0 + 2 * j + 9, 1, q, False)

            quarter(0, True)
            with pe.Fori(1, QUARTERS) as q:
                quarter(q, False)
            pe.wait_ge(sem("x3_summed"), 1)
            for h in range(2):
                m = pe.matmul((b4, b5)[h][:, 0:HALF], ones, r2[:, h * HALF:(h + 1) * HALF], start=True, stop=True)
            m.then_inc(sem("x3_sum_mm"), 1)


_SHAPES = [((P, KT, T), "y"), ((P, 2, T), "c"), ((RP, T), "kr"), ((P, 512), "ssm_p"),
           ((P, NB, 512), "ssm_s"), ((P, KT, 27), "conv")]


def layouts(i):
    import numpy as np
    c = np.ascontiguousarray

    def blocks(w):
        k, n = w.shape[0] // P, w.shape[1] // P
        return w.reshape(k, P, n, P).transpose(2, 1, 0, 3).reshape(n, P, k * P)

    def columns(v):
        return v.reshape(-1, P).T

    w_in, w_up, w_down = i["w_in"][0], i["w_up"][0], i["w_down"][0]
    e = np.cumsum([QL, CL, RP, 512, 1024, 8])
    q, kv, kpe, zz, xbc, dt = np.split(w_in, e[:-1], axis=1)
    special = np.concatenate([kpe, dt, np.zeros((D, P - RP - 8), w_in.dtype)], axis=1)
    parts = [blocks(a) for a in (q, kv, special, xbc, zz)] + [blocks(i["w_out"][0])]
    fq = w_up.shape[1] // QUARTERS
    for n in range(QUARTERS):
        parts += [blocks(w_up[:, n * fq:(n + 1) * fq]), blocks(w_down[n * fq:(n + 1) * fq])]
    x = np.concatenate([i["x_prompt"].reshape(TP, D), i["x_sample"].reshape(SA, D)], axis=0)
    wuq = i["w_uq"][0].reshape(QL, H, 96)
    wuq = np.concatenate([wuq[:, :, :64].reshape(QL, 512), wuq[:, :, 64:].reshape(QL, 256)], axis=1)
    vec = np.zeros((P, NV), np.float32)
    vec[:, V_GATT:V_GATT + 8] = columns(i["norm_attn"][0])
    vec[:, V_GQ:V_GQ + 3] = columns(i["q_norm"][0])
    vec[:, V_GKV:V_GKV + 2] = columns(i["kv_norm"][0])
    vec[:, V_CW:V_CW + 32] = i["conv_w"][0].reshape(CONV_K, KT, P).transpose(2, 1, 0).reshape(P, 32)
    vec[:, V_CB:V_CB + 8] = columns(i["conv_b"][0])
    vec[:, V_GS:V_GS + 4] = columns(i["ssm_norm"][0])
    vec[:, V_GM:V_GM + 8] = columns(i["norm_mlp"][0])
    vec[:, V_GF:V_GF + 8] = columns(i["norm_final"])
    vec[:, V_D:V_D + 4] = columns(np.repeat(i["d_skip"][0], DH))
    vec[32:40, V_DTB] = i["dt_bias"][0]
    vec[32:40, V_AL] = i["a_log"][0]
    vec[:, V_EPS] = EPS
    s = np.arange(P)
    for b in range(NB):
        vec[:SA, V_BM + b] = (s[:SA] // TS == b)
    for a in range(4):
        vec[:, V_QM + a] = (s // RP == a)
    return {
        "wst": c(np.concatenate(parts, axis=0)),
        "x": c(x.T.reshape(KT, P, T).transpose(1, 0, 2)),
        "kv": c(i["cache_kv_latent"][0]), "kr": c(i["cache_k_rope"][0]),
        "h0": c(i["state_ssm"][0].reshape(NB, 512, NST).transpose(2, 0, 1)),
        "sc": c(i["state_conv"][0].reshape(NB, 3, KT, P).transpose(3, 2, 0, 1)),
        "wuq": c(wuq.reshape(3, P, 768).transpose(1, 0, 2)),
        "wukT": c(i["w_uk"][0].transpose(2, 0, 1).reshape(2, P, 512).transpose(1, 0, 2)),
        "wuk": c(i["w_uk"][0].transpose(1, 0, 2)),
        "wuv": c(i["w_uv"][0].transpose(1, 0, 2).reshape(2, P, 512).transpose(1, 0, 2)),
        "vec": vec, "con": constants(), "pt": c(i["page_table"].reshape(1, NB * NPG)),
    }


def constants():
    import numpy as np
    con = np.zeros((P, NC_), np.float32)
    p = np.arange(P)
    con[:, C_ID:C_ID + P] = np.eye(P)
    con[:, C_ONE:C_ONE + P] = 1.0
    swap = (p // RP) * RP + (p % RP + RP // 2) % RP
    con[p, C_ROT + swap] = 1.0
    for a in range(4):
        con[RP * a + p % RP, C_REP + P * a + p] = 1.0
    con[(p % RP + RP // 2) % RP, C_RREP + p] = 1.0
    con[:, C_AM:C_AM + P] = np.where(p[None, :] <= p[:, None], 0, NEG)
    con[:, C_TRI:C_TRI + P] = p[None, :] >= p[:, None]
    con[:, C_NEG:C_NEG + P] = np.where(p[None, :] >= p[:, None], 0, NEG)
    s = np.arange(SA)
    same = (s[:, None] // TS == s[None, :] // TS) & (s[None, :] >= s[:, None])
    con[:SA, C_SNEG:C_SNEG + SA] = np.where(same, 0, NEG)
    pos = np.concatenate([np.arange(TP), np.tile(PAST + np.arange(TS), NB)]).astype(np.float32)
    inv = (np.float32(10000.0) ** (-(np.arange(0, RP, 2, dtype=np.float32) / RP))).astype(np.float32)
    ang = (pos[:, None] * inv[None, :]).astype(np.float32)
    con[:, C_COS:C_COS + T] = np.cos(ang)[:, p % 16].T
    con[:, C_SIN:C_SIN + T] = np.sin(ang)[:, p % 16].T * np.where(p % RP < 16, -1, 1)[:, None]
    m = same.reshape(SA, NB, 1, TS)
    con[:SA, C_SM:C_SM + 512] = np.broadcast_to(np.where(m, 0, NEG), (SA, NB, H, TS)).reshape(SA, 512)
    rst = np.ones(T)
    rst[0] = 0
    rst[TP::TS] = 0
    con[:, C_RST:C_RST + T] = rst
    return con


def kernel(**inputs):
    import numpy as np
    import concourse.bacc as bacc
    from concourse.bass_utils import run_bass_kernel_spmd as run

    nc = bacc.Bacc("TRN2", target_bir_lowering=False, num_devices=1)
    arrays, args = {}, []
    for name, a in layouts({k: np.asarray(v) for k, v in inputs.items()}).items():
        arrays["in_" + name] = a
        args.append(nc.dram_tensor("in_" + name, a.shape, mybir.dt.from_np(a.dtype), kind="ExternalInput").ap())
    for shape, name in _SHAPES:
        args.append(nc.dram_tensor("out_" + name, shape, mybir.dt.float32, kind="ExternalOutput").ap())
    build(nc, *args)
    r = run(nc, [arrays], core_ids=[0]).results[0]
    y = r["out_y"].transpose(2, 1, 0).reshape(T, D)
    c = r["out_c"].transpose(2, 1, 0).reshape(T, CL)
    kr = r["out_kr"].T
    sp = r["out_ssm_p"].T
    ss = r["out_ssm_s"].transpose(1, 2, 0)
    cn = r["out_conv"].transpose(2, 1, 0).reshape(27, D)
    return (y[:TP].reshape(1, TP, D), y[TP:].reshape(NB, TS, D),
            c[:TP].reshape(1, 1, TP, CL), kr[:TP].reshape(1, 1, TP, RP),
            sp.reshape(1, 1, H, DH, NST), cn[:3].reshape(1, 1, 3, D),
            c[TP:].reshape(1, NB, TS, CL), kr[TP:].reshape(1, NB, TS, RP),
            ss.reshape(1, NB, H, DH, NST), cn[3:].reshape(1, NB, 3, D))
```

```python
import concourse.bass as bass
from concourse import mybir
from contextlib import ExitStack

P = 128
D = 1024
KT = D // P
TP, NB, TS = 512, 8, 8
SA = NB * TS
T = TP + SA
HALF = T // 2
QL, CL, RP = 384, 256, 32
H, DH = 8, 64
NST = 128
PAST, PAGE = 2048, 128
NPG = PAST // PAGE
POOL = 160
QT_N = TP // P
CONV_K = 4
EPS = 1e-6
SCALE = float(64 + RP) ** -0.5
NEG = -1e30

B_Q, B_KV, B_SP, B_X, B_Z, N_IN = 0, 3, 5, 6, 14, 18
B_OUT = N_IN
B_MLP = B_OUT + 8
N_BLK = B_MLP + 64
QUARTERS = 4
POOL_SUMS = 5
Q_ORDER = (4, 5, 0, 1, 2, 3)

V_GATT, V_GQ, V_GKV, V_CW, V_CB, V_GS, V_GM, V_GF, V_D, V_DTB, V_AL, V_EPS, V_BM, V_QM = (
    0, 8, 11, 13, 45, 53, 57, 65, 73, 77, 78, 79, 80, 88)
NV = 92
C_ONE, C_ID, C_ROT, C_AM, C_TRI, C_NEG, C_SNEG, C_COS, C_SIN, C_SM, C_RST, C_REP, C_RREP = (
    0, 128, 256, 384, 512, 640, 768, 832, 1408, 1984, 2496, 3072, 3584)
NC_ = 3712

PADW = 3 + TP + NB * (3 + TS)
CW = PADW - 3
SB0 = 3 + TP
GOFF = [0, 512, 896, 1152, 1280]


def build(nc, wst, x_d, kv_d, kr_d, h0_d, sc_d, wuq_d, wukT_d, wuk_d, wuv_d, vec_d, con_d, pt_d,
          y_o, c_o, kr_o, sp_o, ss_o, cn_o):
    f32, f32r, i32 = mybir.dt.float32, mybir.dt.float32r, mybir.dt.int32
    ALU, ACT, AX = mybir.AluOpType, mybir.ActivationFunctionType, mybir.AxisListType
    ctx = ExitStack()
    with ctx:
        base = (nc.sbuf_base + 31) // 32 * 32
        room = nc.sbuf_usable_end - base

        def at(name, shape, off, dt=f32):
            size = 4
            for s in shape[1:]:
                size *= s
            assert off + size <= room, (name, off + size, room)
            return nc.alloc_sbuf_tensor_at(name, shape, dt, offset=base + off)

        made = {}

        def sem(name):
            if name not in made:
                made[name] = ctx.enter_context(nc.semaphore(name))
            return made[name]

        xT = at("xT", [P, KT, T], 0)
        h0T = at("h0T", [P, NB, 512], 0)
        catH = at("catH", [P, KT, T], 18432, f32r)
        catL = at("catL", [P, KT, T], 36864, f32r)
        wraw = [at(f"wraw{i}", [P, KT, P], 55296 + 4096 * i) for i in range(2)]
        whi = [at(f"whi{i}", [P, KT, P], 63488 + 4096 * i, f32r) for i in range(2)]
        wlo = [at(f"wlo{i}", [P, KT, P], 71680 + 4096 * i, f32r) for i in range(2)]
        con = at("con", [P, NC_], 79872)
        vec = at("vec", [P, NV], 94720)
        o = 95104
        qlat = at("qlat", [P, 3, T], o)
        cT = at("cT", [P, 2, T], o + 6912)
        wuq = at("wuq", [P, 3, 768], o + 11520)
        wukT = at("wukT", [P, 2, 512], o + 20736)
        wuk = at("wuk", [64, H, CL], o + 24832)
        wuv = at("wuv", [P, 2, 512], o + 33024)
        qH, wuqH = at("qH", [P, 3, T], 63488, f32r), at("wuqH", [P, 3, 768], 70400, f32r)
        qL, wuqL = at("qL", [P, 3, T], o, f32r), at("wuqL", [P, 3, 768], o + 11520, f32r)
        rx_o = o + 37120
        rx = at("rx", [P, T], rx_o)
        rq = at("rq", [P, T], o + 39424)
        rk = at("rk", [P, T], o + 41728)
        krR = at("krR", [P, T], o + 44032)
        pack = at("pack", [P, T], o + 46336)
        acs = at("acs", [P, T], o + 48640)
        acsH = at("acsH", [8, T], o + 48640, f32r)
        acsL = at("acsL", [8, T], o + 46336, f32r)
        pn = at("pn", [P, 5, 72], o + 50944)
        ptb = at("ptb", [1, NB * NPG], o + 52384, i32)
        r = o + 52896
        xc = at("xc", [P, KT, T], r)
        sqx = at("sqx", [P, KT, T], r)
        z = at("z", [P, 4, T], r + 18432)
        xnat = at("xnat", [P, 5, 512], r + 27648)
        bnat = at("bnat", [P, 5, 256], r + 37888)
        cbm = at("cbm", [P, 2, 1280], r + 43008)
        sqq = at("sqq", [P, 5, T], r + 37888)
        cbs = at("cbs", [64, 2, SA], r + 53248)
        pad = [at(f"pad{i}", [P, PADW], r + 53760 + 2432 * i) for i in range(2)]
        cacc = [at(f"cacc{i}", [P, PADW], r + 53760 + 4864 + 2432 * i) for i in range(2)]
        krw = at("krw", [P, T], r + 27648)
        t1 = at("t1", [P, T], r + 27648 + 2304)
        dw = [at(f"dw{i}", [P, T], r + 27648 + 4608 + 2304 * i) for i in range(2)]
        cn = at("cn", [P, KT, 27], r + 63488)
        scv = at("scv", [P, KT, NB, 3], 16384)
        pick = at("pick", [8, H], r + 64352, f32r)
        ex = [at("ex0", [P, 1280], r + 53760), at("ex1", [P, 1280], 36864), at("ex2", [P, 1280], 18432),
              at("ex3", [P, 1280], 27648)]
        dgn = [at("dgn0", [P, 4, P], r + 61184), at("dgn1", [P, 4, P], 18432 + 5120)]
        gs = at("gs", [64, H, SA], 36864 + 5120)
        se = at("se", [P, 320], r + 53760 + 5120)
        ysm = at("ysm", [P, 4, SA], r + 53760 + 6400)
        bms = at("bms", [64, NB, 256], 18432)
        spo = at("spo", [P, 512], 36864)
        rg = at("rg", [P, 2, T], r + 43008)
        QT = at("QT", [96, H, TP], r)
        KTt = at("KTt", [96, H, TP], r + 16384)
        V = at("V", [P, QT_N, 512], r + 32768)
        Pm = at("Pm", [P, 1280], r + 40960)
        PTm = at("PTm", [P, 1280], r + 46080)
        qp = at("qp", [P, 2, T], r + 40960)
        tq = [at(f"tq{i}", [P, 2, T], r + 51200 + 4608 * i) for i in range(2)]
        qs = at("qs", [64, H, SA], r + 61440)
        qrs = at("qrs", [P, 2, SA], r + 63488)
        mx = at("mx", [P, 12], rx_o)
        qabs = at("qabs", [P, 2, 512], o)
        qps = at("qps", [P, 512], o + 4096)
        snew = at("snew", [64, 512], o + 46336)
        c64 = at("c64", [64, 256], o + 50944)
        ckv = [at("ckv0", [P, NPG, CL], 0), at("ckv1", [P, NPG, CL], o + 11520)]
        ckr = [at("ckr0", [P, NPG, RP], 16384), at("ckr1", [P, NPG, RP], o + 27904)]
        CTr = at("CTr", [P, 2, PAST], 63488)
        KRr = at("KRr", [P, 4, P], o + 39424)
        sS = at("sS", [P, 1088], r + 51200)
        pS = at("pS", [P, 1088], r + 55552)
        rm = at("rm", [SA, 1], r + 59904)
        dgm = at("dgm", [SA, SA], r + 59936)
        psm = at("psm", [P, SA], r + 60192)
        rsm = at("rsm", [P, SA], r + 60448)
        mxs = at("mxs", [P, P], r + 60704)
        qpb = at("qpb", [P, 4, SA], r + 61216)
        olat = at("olat", [P, 2, 512], o + 6912)
        x2H = at("x2H", [P, KT, T], o, f32r)
        x2L = at("x2L", [P, KT, T], o + 18432, f32r)
        uH = at("uH", [P, KT, T], o + 36864, f32r)
        uL = at("uL", [P, KT, T], o + 55296, f32r)
        ru = [at(f"ru{i}", [P, T], o + 73728 + 2304 * i) for i in range(2)]
        us = [at(f"us{i}", [P, T], o + 78336 + 2304 * i) for i in range(2)]
        r2 = at("r2", [P, T], o + 82944)
        r3 = at("r3", [P, T], o + 85248)
        sq2 = at("sq2", [P, KT, T], o + 87552)

        B = [ctx.enter_context(nc.psum_tensor(f"bank{i}", [P, 2, 512], f32)) for i in range(2)] + \
            [ctx.enter_context(nc.psum_tensor(f"bank{i}", [P, 512], f32)) for i in range(4, 8)]
        acc = [B[0], B[1]]
        b4, b5, b6, b7 = B[2:]

        ident = con[:, C_ID:C_ID + P]
        ones = con[:, C_ONE:C_ONE + P]
        rot = con[:, C_ROT:C_ROT + P]
        tri = con[:, C_TRI:C_TRI + P]
        neg = con[:, C_NEG:C_NEG + P]
        cosT = con[:, C_COS:C_COS + T]
        sinT = con[:, C_SIN:C_SIN + T]

        rows_bank = [b7[:]] + [(acc[0][:, 0, :], acc[0][:, 1, :], b4[:], b5[:])[h % 4] for h in range(H - 1)]

        def halves(ap):
            return ap.rearrange("p (a n) -> p a n", a=2)

        def samp(ap, w=TS):
            return ap[:, SB0:SB0 + NB * (3 + TS)].rearrange("p (b w) -> p b w", w=3 + TS)

        block = ctx.enter_context(nc.Block())

        @block.sync
        def _(sp):
            def ring(g):
                if g >= 2:
                    sp.wait_ge(sem("w_split"), g - 1)
                sp.dma_start(wraw[g % 2][:], wst[g, :, :].rearrange("p (k n) -> p k n", k=KT)
                             ).then_inc(sem(f"w_arrived{g % 2}"), 16)

            for k in range(KT):
                if k % 2 == 0:
                    sp.dma_start(xT[:, k:k + 2, :], x_d[:, k:k + 2, :]).then_inc(sem(f"x_arrived{k // 2}"), 16)
                if k == 0:
                    ring(0)
            for g in range(1, N_IN + 2):
                ring(g)

            def pages(b, u, free, count):
                numbers = [sp.value_load(ptb[0:1, b * NPG + j:b * NPG + j + 1] if isinstance(b, int)
                                         else ptb[0:1, bass.ds(b * NPG + j, 1)], min_val=0, max_val=POOL - 1)
                           for j in range(NPG)]
                sp.wait_ge(sem(free), count)
                for j, page in enumerate(numbers):
                    sp.dma_start(ckv[u][:, j, :], kv_d[bass.ds(page, 1), :, :].rearrange("a p n -> (a p) n")
                                 ).then_inc(sem(f"cache{u}_half{j // (NPG // 2)}"), 16)
                for j, page in enumerate(numbers):
                    sp.dma_start(ckr[u][:, j, :], kr_d[bass.ds(page, 1), :, :].rearrange("a p n -> (a p) n")
                                 ).then_inc(sem(f"cache{u}_rotary"), 16)

            sp.wait_ge(sem("pt_arrived"), 16)
            pages(0, 0, "out_ss", 16)
            pages(1, 1, "qabs_mm", 1)
            with sp.Fori(1, NB // 2) as i:
                for u in range(2):
                    pages(i * 2 + u, u, "pv_mm", i * 2 + u - 1)
            sp.wait_ge(sem("pv_mm"), 7)
            sp.dma_start(xT[:], x_d).then_inc(sem("x_again"), 16)
            with sp.Fori((N_IN + 2) // 2, N_BLK // 2) as i:
                for u in range(2):
                    sp.wait_ge(sem("w_split"), i * 2 + u - 1)
                    sp.dma_start(wraw[u][:], wst[bass.ds(i * 2 + u, 1), :, :].rearrange("a p (k n) -> (a p) k n", k=KT)
                                 ).then_inc(sem(f"w_arrived{u}"), 16)
            for h in range(2):
                cols = slice(h * HALF, (h + 1) * HALF)
                for c in range(2):
                    sp.wait_ge(sem("y_ready"), KT * h + 4 * c + 4)
                    sp.dma_start(y_o[:, 4 * c:4 * c + 4, cols], sq2[:, 4 * c:4 * c + 4, cols]).then_inc(sem("out_y"), 16)
            for name in ("out_c", "out_kr", "out_cn", "out_sp", "out_ss"):
                sp.wait_ge(sem(name), 16)
            sp.wait_ge(sem("out_y"), 64)

        @block.gpsimd
        def _(pool):
            def low(g):
                pool.wait_ge(sem("w_high"), g + 1)
                pool.tensor_tensor(wlo[g % 2][:], wraw[g % 2][:], whi[g % 2][:].bitcast(f32),
                                   ALU.subtract).then_inc(sem("w_split"), 1)

            pool.memset(ones, 1.0).then_inc(sem("filled"), 1)
            pool.memset(pack[:], 0.0).then_inc(sem("filled"), 1)
            for i in range(2):
                pool.memset(pad[i][:], 0.0).then_inc(sem("filled"), 1)
            for g in range(N_IN):
                if g != 1:
                    low(g)
                if g == 0:
                    for k in range(1, POOL_SUMS):
                        pool.wait_ge(sem("x_squared"), k + 1)
                        if k > 1:
                            pool.wait_ge(sem("pool_sum"), k - 1)
                        pool.tensor_tensor(rk[:], sqx[:, 0, :] if k == 1 else rk[:], sqx[:, k, :], ALU.add
                                           ).then_inc(sem("pool_sum" if k < POOL_SUMS - 1 else "x_added"), 1)
                    low(1)
                if g == 5:
                    pool.wait_ge(sem("q_squared"), 3)
                    pool.tensor_tensor(sqq[:, 0, :], sqq[:, 0, :], sqq[:, 1, :], ALU.add).then_inc(sem("latent_sum"), 1)
                    pool.wait_ge(sem("latent_sum"), 1)
                    pool.tensor_tensor(sqq[:, 0, :], sqq[:, 0, :], sqq[:, 2, :], ALU.add).then_inc(sem("latent_sum"), 1)
                if g == 6:
                    pool.wait_ge(sem("q_squared"), 5)
                    pool.tensor_tensor(sqq[:, 3, :], sqq[:, 3, :], sqq[:, 4, :], ALU.add).then_inc(sem("latent_sum"), 1)
                if B_X <= g < B_X + KT:
                    c = g - B_X
                    if c == 0:
                        pool.wait_ge(sem("sc_arrived"), 16)
                        pool.wait_ge(sem("filled"), 4)
                    if c >= 2:
                        pool.wait_ge(sem("conv_done"), c - 1)
                        pool.wait_ge(sem("cn_copied"), 2 * (c - 1))
                    pool.tensor_copy(samp(pad[c % 2])[:, :, 0:3], scv[:, c, :, :]).then_inc(sem("pad_state"), 1)
                if B_X <= g - 1 < B_X + KT:
                    c = g - 1 - B_X
                    pool.wait_ge(sem("pad_filled"), c + 1)
                    pool.tensor_copy(cn[:, c, 0:3], pad[c % 2][:, TP:TP + 3]).then_inc(sem("cn_copied"), 1)
                    pool.tensor_copy(cn[:, c, 3:27].rearrange("p (b w) -> p b w", w=3),
                                     samp(pad[c % 2])[:, :, TS:TS + 3]).then_inc(sem("cn_copied"), 1)

            pool.wait_ge(sem("xnat_ready"), 6)
            pool.wait_ge(sem("pn_ready"), 1)
            pool.tensor_tensor(xnat[:, 0:4, :].rearrange("p a (h n) -> p a h n", h=H),
                               xnat[:, 0:4, :].rearrange("p a (h n) -> p a h n", h=H),
                               pn[:, 0:4, 32:40].rearrange("p a (h n) -> p a h n", n=1)
                               .to_broadcast([P, 4, H, DH]), ALU.mult)
            pool.tensor_tensor(xnat[0:SA, 4, :].rearrange("p (h n) -> p h n", h=H),
                               xnat[0:SA, 4, :].rearrange("p (h n) -> p h n", h=H),
                               pn[0:SA, 4, 32:40].rearrange("p (h n) -> p h n", n=1)
                               .to_broadcast([SA, H, DH]), ALU.mult).then_inc(sem("xdt_ready"), 1)
            pool.wait_ge(sem("cb_ready"), 2)
            pool.wait_ge(sem("sex_done"), 1)
            pool.wait_ge(sem("xdt_ready"), 1)
            pool.tensor_tensor(gs[:].rearrange("p (g e) n -> p g e n", g=2),
                               gs[:].rearrange("p (g e) n -> p g e n", g=2),
                               cbs[:].rearrange("p g (a n) -> p g a n", a=1).to_broadcast([SA, 2, 4, SA]),
                               ALU.mult).then_inc(sem("smix_ready"), 1)
            pool.wait_ge(sem("y_mm"), H)
            pool.wait_ge(sem("vec_arrived"), 16)
            for b in range(NB):
                pool.tensor_scalar(bms[:, b, :], bnat[0:SA, 4, :], vec[0:SA, V_BM + b:V_BM + b + 1], 1.0,
                                   ALU.mult, ALU.mult).then_inc(sem("bms_ready"), 1)
            pool.wait_ge(sem("wuq_high"), 1)
            pool.tensor_tensor(wuqL[:], wuq[:], wuqH[:].bitcast(f32), ALU.subtract).then_inc(sem("wuq_split"), 1)
            for j in range(4):
                pool.wait_ge(sem("oh_ready"), j + 1)
                pool.tensor_tensor(catL[:, 4 + j, :], xc[:, j, :], catH[:, 4 + j, :].bitcast(f32), ALU.subtract
                                   ).then_inc(sem("ol_ready"), 1)
            pool.wait_ge(sem("kr_ready"), 1)
            pool.wait_ge(sem("hn_mm"), NB)
            pool.wait_ge(sem("g_summed"), 2)
            pool.wait_ge(sem("ol_ready"), 4)
            for h in range(H):
                m = pool.tensor_copy(KTt[64:96, h, :], krR[64:96, 0:TP])
            m.then_inc(sem("krope_ready"), 1)

            def spread(q):
                return pool.tensor_tensor(qpb[:], q.rearrange("p (a n) -> p a n", a=1).to_broadcast([P, 4, SA]),
                                          vec[:, V_QM:V_QM + 4].rearrange("p (a n) -> p a n", n=1)
                                          .to_broadcast([P, 4, SA]), ALU.mult)

            pool.wait_ge(sem("qabs_ready"), 2)
            pool.wait_ge(sem("qps_ready"), 1)
            pool.wait_ge(sem("qabs_mm"), 1)
            pool.wait_ge(sem("qrope_ready"), H)
            pool.wait_ge(sem("krope_ready"), 1)
            spread(qps[:, 0:SA]).then_inc(sem("qb_ready"), 1)
            with pool.Fori(1, NB) as b:
                pool.wait_ge(sem("s_mm"), b * 4)
                spread(qps[:, bass.ds(b * SA, SA)]).then_inc(sem("qb_ready"), 1)
            pool.wait_ge(sem("s_mm"), 4 * NB)
            for g in range(B_OUT, B_OUT + 2):
                low(g)
            for d in range(KT):
                low(B_OUT + 2 + d)
                pool.wait_ge(sem("res_squared"), d + 1)
                if d == 1:
                    pool.tensor_tensor(r2[:], sq2[:, 0, :], sq2[:, 1, :], ALU.add).then_inc(sem("pool_sum"), 1)
                elif d > 1:
                    pool.wait_ge(sem("pool_sum"), POOL_SUMS - 2 + d - 1)
                    pool.tensor_tensor(r2[:], r2[:], sq2[:, d, :], ALU.add
                                       ).then_inc(sem("pool_sum" if d < KT - 1 else "res_summed"), 1)
            pool.wait_ge(sem("res_root"), 1)
            pool.tensor_copy(us[0][:, 0:1], vec[:, V_EPS:V_EPS + 1]).then_inc(sem("ul_ready"), 2)

            def low_at(g, u):
                pool.wait_ge(sem("w_high"), g + 1)
                pool.tensor_tensor(wlo[u][:], wraw[u][:], whi[u][:].bitcast(f32), ALU.subtract
                                   ).then_inc(sem("w_split"), 1)

            def low_hidden(n, u, slot):
                dst = uL[:, bass.ds(slot, 1), :].rearrange("p a n -> p (a n)")
                hi_ = uH[:, bass.ds(slot, 1), :].rearrange("p a n -> p (a n)").bitcast(f32)
                pool.wait_ge(sem("ru_free"), n + 3)
                pool.wait_ge(sem("uh_ready"), n + 1)
                pool.tensor_tensor(dst, us[u][:], hi_, ALU.subtract).then_inc(sem("ul_ready"), 1)

            def pool_up(q):
                g0 = q * 16 + B_MLP
                with pool.Fori(0, 4) as j:
                    for u in range(2):
                        low_at(g0 + 2 * j + 2 + u, u)
                        low_hidden(q * 8 + 2 * j + u, u, 2 * j + u)

            with pool.Fori(0, QUARTERS - 1) as q:
                pool_up(q)
                with pool.Fori(0, 4) as j:
                    for u in range(2):
                        low_at(q * 16 + 2 * j + B_MLP + 10 + u, u)
            pool_up(QUARTERS - 1)
            for d in range(KT - 1):
                if d < KT - 2:
                    low(N_BLK - KT + 2 + d)
                if d:
                    pool.wait_ge(sem("res_squared"), KT + d + 1)
                    if d > 1:
                        pool.wait_ge(sem("pool_sum"), POOL_SUMS - 2 + KT - 2 + d - 1)
                    pool.tensor_tensor(r2[:], sq2[:, 0, :] if d == 1 else r2[:], sq2[:, d, :], ALU.add
                                       ).then_inc(sem("pool_sum" if d < KT - 2 else "res_summed"), 1)

        @block.scalar
        def _(act):
            chain = [0]

            def link(ins):
                chain[0] += 1
                ins.then_inc(sem("act_chain"), 1)
                act.wait_ge(sem("act_chain"), chain[0])

            def high(g):
                act.wait_ge(sem(f"w_arrived{g % 2}"), 16 * (g // 2 + 1))
                if g >= 2:
                    act.wait_ge(sem("gemm_done"), g - 1)
                act.activation(whi[g % 2][:], wraw[g % 2][:], ACT.Copy).then_inc(sem("w_high"), 1)

            act.dma_start(vec[:], vec_d).then_inc(sem("vec_arrived"), 16)
            for k in range(KT):
                act.wait_ge(sem(f"x_arrived{k // 2}"), 16)
                act.activation(sqx[:, k, :], xT[:, k, :], ACT.Square).then_inc(sem("x_squared"), 1)
                if k == 0:
                    high(0)
            high(1)
            act.wait_ge(sem("x_summed"), 1)
            act.wait_ge(sem("vec_arrived"), 16)
            act.activation(rx[:, 0:HALF], b4[:, 0:HALF], ACT.Sqrt, scale=1.0 / D, bias=vec[:, V_EPS:V_EPS + 1])
            act.activation(rx[:, HALF:T], b5[:, 0:HALF], ACT.Sqrt, scale=1.0 / D,
                           bias=vec[:, V_EPS:V_EPS + 1]).then_inc(sem("x_root"), 1)
            act.wait_ge(sem("x_split"), 2 * KT)
            act.wait_ge(sem("x_squared"), KT)
            act.dma_start(scv[:], sc_d).then_inc(sem("sc_arrived"), 16)
            for g in range(2, N_IN + 2):
                if g < N_IN:
                    high(g)
                if g == 2:
                    act.dma_start(con[:, P:C_COS], con_d[:, P:C_COS]).then_inc(sem("con_arrived"), 16)
                if g == 3:
                    act.dma_start(con[:, C_COS:NC_], con_d[:, C_COS:NC_]).then_inc(sem("con_arrived"), 16)
                if g in (7, 8):
                    b = 4 * (g - 7)
                    act.dma_start(h0T[:, b:b + 4, :], h0_d[:, b:b + 4, :]).then_inc(sem("h0_arrived"), 16)
                if g == 10:
                    act.dma_start(wuq[:], wuq_d).then_inc(sem("small_weights"), 16)
                if g == 11:
                    act.dma_start(wukT[:], wukT_d).then_inc(sem("small_weights"), 16)
                    act.dma_start(wuk[:], wuk_d).then_inc(sem("small_weights"), 16)
                if g == 12:
                    act.dma_start(wuv[:], wuv_d).then_inc(sem("small_weights"), 16)
                    act.dma_start(ptb[:], pt_d).then_inc(sem("pt_arrived"), 16)
                if g == 4:
                    act.wait_ge(sem("evac"), 3)
                    act.wait_ge(sem("x_summed"), 1)
                    for i in range(3):
                        act.activation(sqq[:, i, :], qlat[:, i, :], ACT.Square).then_inc(sem("q_squared"), 1)
                if g == 6:
                    act.wait_ge(sem("evac"), 5)
                    for i in range(2):
                        act.activation(sqq[:, 3 + i, :], cT[:, i, :], ACT.Square).then_inc(sem("q_squared"), 1)
                if g == 7:
                    act.wait_ge(sem("q_summed"), 1)
                    act.activation(rq[:, 0:HALF], b4[:, 0:HALF], ACT.Sqrt, scale=1.0 / QL,
                                   bias=vec[:, V_EPS:V_EPS + 1])
                    act.activation(rq[:, HALF:T], b5[:, 0:HALF], ACT.Sqrt, scale=1.0 / QL,
                                   bias=vec[:, V_EPS:V_EPS + 1]).then_inc(sem("q_root"), 1)
                    act.wait_ge(sem("q_summed"), 2)
                    act.activation(rk[:, 0:HALF], b6[:, 0:HALF], ACT.Sqrt, scale=1.0 / CL,
                                   bias=vec[:, V_EPS:V_EPS + 1])
                    act.activation(rk[:, HALF:T], b7[:, 0:HALF], ACT.Sqrt, scale=1.0 / CL,
                                   bias=vec[:, V_EPS:V_EPS + 1]).then_inc(sem("q_root"), 1)
                    act.wait_ge(sem("evac"), B_SP + 1)
                    link(act.activation(dw[0][32:40, :], krw[32:40, :], ACT.Abs, bias=vec[32:40, V_DTB:V_DTB + 1]))
                    link(act.activation(dw[1][32:40, :], dw[0][32:40, :], ACT.Exp, scale=-1.0))
                    act.activation(dw[1][32:40, :], dw[1][32:40, :], ACT.Ln, bias=1.0).then_inc(sem("dt_ln"), 1)
                    act.activation(vec[32:40, V_AL:V_AL + 1], vec[32:40, V_AL:V_AL + 1], ACT.Exp
                                   ).then_inc(sem("dt_ln"), 1)
                if g == 9:
                    act.wait_ge(sem("dt_end"), 2)
                    act.activation(dw[1][32:40, :], dw[0][32:40, :], ACT.Exp).then_inc(sem("dt_decay"), 1)
                if g >= 9 and g - 9 < KT:
                    c = g - 9
                    act.wait_ge(sem("conv_done"), c + 1)
                    act.activation(xc[:, c, 0:TP], cacc[c % 2][:, 0:TP], ACT.Silu)
                    act.activation(xc[:, c, TP:T].rearrange("p (b w) -> p b w", w=TS),
                                   samp(cacc[c % 2])[:, :, 0:TS], ACT.Silu).then_inc(sem("silu_done"), 1)
            act.wait_ge(sem("acs_ready"), 1)
            act.activation(pack[96:104, :], acs[32:40, :], ACT.Exp).then_inc(sem("dt_decay"), 1)
            act.wait_ge(sem("pn_ready"), 1)
            act.wait_ge(sem("cn_copied"), 2 * KT)
            for h in range(H):
                act.wait_ge(sem("diag_ready"), h + 1)
                if h >= 4:
                    act.wait_ge(sem("y_mm"), h - 3)
                e = ex[h % 4]
                for i in range(4):
                    m = act.activation(e[:, GOFF[i]:GOFF[i] + P], dgn[h % 2][:, i, :], ACT.Exp,
                                       bias=pn[:, i, h:h + 1])
                    if i < 3:
                        m = act.activation(e[:, GOFF[i] + P:GOFF[i + 1]], rows_bank[h][:, P * i + P:TP], ACT.Exp,
                                           bias=pn[:, i, h:h + 1])
                m.then_inc(sem("ex_done"), 1)
                if h == 5:
                    act.wait_ge(sem("sdiag_ready"), 1)
                    act.activation(gs[:], gs[:], ACT.Exp).then_inc(sem("sex_done"), 1)
            act.wait_ge(sem("evac"), N_IN)
            act.activation(z[:], z[:], ACT.Silu).then_inc(sem("z_silu"), 1)
            act.wait_ge(sem("small_weights"), 64)
            act.activation(wuqH[:], wuq[:], ACT.Copy).then_inc(sem("wuq_high"), 1)
            for j in range(4):
                act.wait_ge(sem("gated"), j + 1)
                act.activation(z[:, j, 0:TP], xc[:, j, 0:TP], ACT.Square)
            act.wait_ge(sem("gated_sample"), 1)
            act.activation(z[:, :, TP:T], xc[:, 0:4, TP:T], ACT.Square).then_inc(sem("g_squared"), 1)
            for c in range(2):
                act.wait_ge(sem("g_summed"), c + 1)
                for h in range(2):
                    bk = ((b4, b5), (b6, b7))[c][h]
                    m = act.activation(rg[:, c, h * HALF:(h + 1) * HALF], bk[:, 0:HALF], ACT.Sqrt,
                                       scale=1.0 / 256, bias=vec[:, V_EPS:V_EPS + 1])
                m.then_inc(sem("g_root"), 1)
            act.dma_start(c_o, cT[:]).then_inc(sem("out_c"), 16)
            act.dma_start(kr_o, krR[0:RP, :]).then_inc(sem("out_kr"), 16)
            act.wait_ge(sem("cn_copied"), 2 * KT)
            act.dma_start(cn_o, cn[:]).then_inc(sem("out_cn"), 16)
            act.wait_ge(sem("spo_ready"), 1)
            act.dma_start(sp_o, spo[:]).then_inc(sem("out_sp"), 16)
            act.wait_ge(sem("hn_ready"), NB)
            act.dma_start(ss_o, h0T[:]).then_inc(sem("out_ss"), 16)
            act.wait_ge(sem("hn_mm"), NB)
            act.wait_ge(sem("c_ready"), 2)
            def head_high(j):
                act.wait_ge(sem("o_ready"), j + 1)
                act.activation(catH[:, 4 + j, :], xc[:, j, :], ACT.Copy).then_inc(sem("oh_ready"), 1)

            def kv_out(u):
                act.wait_ge(sem("kv_mm"), u + 1)
                src = acc[u % 2][:, 0, :]
                if u < 4:
                    act.activation(KTt[0:64, 2 * u, :], src[0:64], ACT.Copy)
                    m = act.activation(KTt[0:64, 2 * u + 1, :], src[64:128], ACT.Copy)
                else:
                    m = act.activation(V[:, u - 4, :], src, ACT.Copy)
                m.then_inc(sem("kv_evac"), 1)

            kv_out(0)
            head_high(0)
            kv_out(1)
            head_high(1)
            for u in range(2, 6):
                kv_out(u)
            head_high(2)
            head_high(3)
            kv_out(6)
            kv_out(7)

            def by_sequence(ap):
                return ap.rearrange("p (b h t) -> p h b t", b=NB, h=H)

            def by_head(ap):
                return ap.rearrange("p (h b t) -> p h b t", b=NB, h=H)

            act.wait_ge(sem("qabs_mm"), 1)
            for k in range(2):
                act.activation(by_sequence(qabs[:, k, :]), by_head(acc[0][:, k, :]), ACT.Copy
                               ).then_inc(sem("qabs_ready"), 1)
            act.wait_ge(sem("qps_mm"), 1)
            act.activation(by_sequence(qps[:]), by_head(b7[:]), ACT.Copy).then_inc(sem("qps_ready"), 1)
            act.wait_ge(sem("c64_mm"), 1)
            act.activation(c64[:], b6[0:SA, 0:256], ACT.Copy).then_inc(sem("c64_ready"), 1)

            sbank = [acc[1][:, 1, 384:512], b7[:, 0:256], acc[1][:, 1, 0:384], acc[1][:, 0, :]]
            off = [0, 128, 384, 768, 1280]

            def turned(b, quads):
                for q in quads:
                    if b and q < 8:
                        act.wait_ge(sem("s_mm"), 4 * b - 3 + q // 2)
                    act.wait_ge(sem("ct_mm"), b * 9 + q + 1)
                    bk = (b4, b5)[(b + q) % 2]
                    if q < 8:
                        act.activation(CTr[:, :, 256 * q:256 * q + 256].rearrange("p k (t n) -> p t k n", n=P),
                                       bk[:].rearrange("p (t k n) -> p t k n", k=2, n=P), ACT.Copy
                                       ).then_inc(sem("ct_evac"), 1)
                    else:
                        act.activation(KRr[:].rearrange("p a n -> p (a n)"), bk[:], ACT.Copy
                                       ).then_inc(sem("ct_evac"), 1)

            turned(0, range(9))
            for s in range(H):
                act.wait_ge(sem("nm_ready"), s + 1)
                for i in range(QT_N):
                    m = act.activation(Pm[:, off[i]:off[i + 1]], sbank[i], ACT.Exp, bias=mx[:, 4 + i:5 + i],
                                       scale=SCALE, accum_out=mx[:, 8 + i:9 + i])
                m.then_inc(sem("p_exp"), 1)
                if s + 1 < NB:
                    turned(s + 1, range(8))
                else:
                    act.wait_ge(sem("s_mm"), 4 * NB)
                    for g in range(B_OUT, B_OUT + 2):
                        high(g)
                for e in range(2):
                    act.wait_ge(sem("shift_ready"), 2 * s + e + 1)
                    m = act.activation(pS[:, 512 * e:512 * e + 512], sS[:, 512 * e:512 * e + 512], ACT.Exp, scale=SCALE)
                    if e:
                        m = act.activation(pS[0:SA, 1024:1088], sS[0:SA, 1024:1088], ACT.Exp, scale=SCALE)
                    m.then_inc(sem("sp_exp"), 1)
                act.wait_ge(sem("pt_mm"), s + 1)
                act.activation(PTm[:, 0:512], acc[1][:, 0, :], ACT.Copy)
                act.activation(PTm[:, 1024:1280], b7[:, 0:256], ACT.Copy).then_inc(sem("pt_act"), 1)
                if s + 1 < NB:
                    turned(s + 1, [8])
                rows = slice(DH * (s % 2), DH * (s % 2) + DH)
                act.wait_ge(sem("o_mm"), s + 1)
                act.activation(catH[rows, s // 2, 0:TP], acc[1][rows, 0, :], ACT.Copy).then_inc(sem("attn_high"), 1)
            act.wait_ge(sem("os_mm"), 1)
            act.activation(catH[:, 0:4, TP:T], b5[:, 0:256].rearrange("p (a n) -> p a n", a=4), ACT.Copy
                           ).then_inc(sem("osh_ready"), 1)

            for d in range(KT):
                high(B_OUT + 2 + d)
                act.wait_ge(sem("evac"), B_OUT + d + 1)
                act.activation(sq2[:, d, :], xT[:, d, :], ACT.Square).then_inc(sem("res_squared"), 1)
            act.wait_ge(sem("res_sum_mm"), 1)
            act.activation(r3[:, 0:HALF], b4[:, 0:HALF], ACT.Sqrt, scale=1.0 / D, bias=vec[:, V_EPS:V_EPS + 1])
            act.activation(r3[:, HALF:T], b5[:, 0:HALF], ACT.Sqrt, scale=1.0 / D,
                           bias=vec[:, V_EPS:V_EPS + 1]).then_inc(sem("res_root"), 1)
            act.activation(ru[0][:, 0:1], vec[:, V_EPS:V_EPS + 1], ACT.Copy).then_inc(sem("ru_free"), 2)

            def high_at(g, u, pair):
                act.wait_ge(sem(f"w_arrived{u}"), pair * 16 + 16)
                act.wait_ge(sem("gemm_done"), g - 1)
                act.activation(whi[u][:], wraw[u][:], ACT.Copy).then_inc(sem("w_high"), 1)

            def square(n, u, g):
                act.wait_ge(sem("evac"), g + 1)
                act.wait_ge(sem("ul_ready"), n + 1)
                act.activation(us[u][:], ru[u][:], ACT.Square).then_inc(sem("ru_free"), 1)

            def act_quarter(q, last):
                g0 = q * 16 + B_MLP
                with act.Fori(0, 4) as j:
                    for u in range(2):
                        high_at(g0 + 2 * j + 2 + u, u, q * 8 + j + B_MLP // 2 + 1)
                        square(q * 8 + 2 * j + u, u, g0 + 2 * j + u)
                if last:
                    for d in range(KT - 1):
                        if d < KT - 2:
                            high(N_BLK - KT + 2 + d)
                        act.wait_ge(sem("evac"), N_BLK - KT + d + 1)
                        act.activation(sq2[:, d, :], xT[:, d, :], ACT.Square).then_inc(sem("res_squared"), 1)
                    return
                with act.Fori(0, 4) as j:
                    for u in range(2):
                        high_at(g0 + 2 * j + 10 + u, u, q * 8 + j + B_MLP // 2 + 5)

            with act.Fori(0, QUARTERS - 1) as q:
                act_quarter(q, False)
            act_quarter(QUARTERS - 1, True)
            for h in range(2):
                cols = slice(h * HALF, (h + 1) * HALF)
                act.wait_ge(sem("last_evac"), h + 1)
                act.activation(sq2[:, KT - 1, cols], xT[:, KT - 1, cols], ACT.Square).then_inc(sem("last_squared"), 1)
                act.wait_ge(sem("res_sum_mm"), h + 2)
                act.activation(r3[:, cols], (b4, b5)[h][:, 0:HALF], ACT.Sqrt, scale=1.0 / D,
                               bias=vec[:, V_EPS:V_EPS + 1]).then_inc(sem("res_root"), 1)

        @block.vector
        def _(dve):
            chain = [0]

            def link(ins):
                chain[0] += 1
                ins.then_inc(sem("dve_chain"), 1)
                dve.wait_ge(sem("dve_chain"), chain[0])

            dve.wait_ge(sem("vec_arrived"), 16)
            for k in range(KT):
                dve.wait_ge(sem(f"x_arrived{k // 2}"), 16)
                g = vec[:, V_GATT + k:V_GATT + k + 1]
                dve.tensor_scalar(catH[:, k, :], xT[:, k, :], g, None, ALU.mult).then_inc(sem("x_split"), 1)
                dve.wait_ge(sem("x_split"), 2 * k + 1)
                dve.scalar_tensor_tensor(catL[:, k, :], xT[:, k, :], g, catH[:, k, :].bitcast(f32),
                                         ALU.mult, ALU.subtract).then_inc(sem("x_split"), 1)
            dve.wait_ge(sem("x_squared"), KT)
            for k in range(POOL_SUMS + 1, KT):
                m = dve.tensor_tensor(rq[:], sqx[:, POOL_SUMS, :] if k == POOL_SUMS + 1 else rq[:], sqx[:, k, :],
                                      ALU.add)
                if k < KT - 1:
                    link(m)
            m.then_inc(sem("x_added"), 1)
            dve.wait_ge(sem("x_root"), 1)
            dve.reciprocal(rx[:], rx[:]).then_inc(sem("rx_ready"), 1)
            dve.wait_ge(sem("rx_ready"), 1)

            def evac(g, out):
                dve.wait_ge(sem("gemm_done"), g + 1)
                return dve.tensor_tensor(out, acc[g % 2][:, :, 0:HALF], halves(rx[:]), ALU.mult)

            def diag_rows(h):
                dve.wait_ge(sem("rows_done"), h + 1)
                if h >= 2:
                    dve.wait_ge(sem("ex_done"), h - 1)
                dve.tensor_tensor(dgn[h % 2][:], rows_bank[h].rearrange("p (a n) -> p a n", a=4),
                                  neg.rearrange("p (a n) -> p a n", a=1).to_broadcast([P, 4, P]),
                                  ALU.add).then_inc(sem("diag_ready"), 1)

            def causal(c):
                dve.wait_ge(sem("cb_mm"), c + 1)
                for i, (bk, off) in enumerate(((b4, 0), (b5, 0), (b6, 0), (b5, 384))):
                    dve.tensor_tensor(cbm[:, c, GOFF[i]:GOFF[i] + P], bk[:, off:off + P], tri, ALU.mult)
                    if i < 3:
                        dve.tensor_copy(cbm[:, c, GOFF[i] + P:GOFF[i + 1]], bk[:, off + P:off + TP - P * i])
                dve.tensor_copy(cbs[:, c, :], b6[0:SA, 256:256 + SA]).then_inc(sem("cb_ready"), 1)

            for g in range(N_IN):
                if g == N_IN - 1:
                    causal(0)
                    dve.wait_ge(sem("silu_done"), KT)
                    diag_rows(0)
                if g == 12:
                    dve.wait_ge(sem("pack_tr"), 1)
                    dve.tensor_copy(pn[:, 0:4, :].rearrange("p a b -> p (a b)"), b4[:, 0:288])
                    dve.tensor_copy(pn[0:SA, 4, :], b4[0:SA, 288:360]).then_inc(sem("pn_ready"), 1)
                if g >= 11 and g - 11 < 6:
                    c = g - 11
                    dve.wait_ge(sem("x_tr"), c + 1)
                    dst = xnat[:, :, c * P:(c + 1) * P] if c < 4 else bnat[:, :, (c - 4) * P:(c - 3) * P]
                    bk = b5 if c % 2 == 0 else b6
                    dve.tensor_copy(dst[:, 0:4, :], bk[:].rearrange("p (a n) -> p a n", a=4))
                    dve.tensor_copy(dst[0:SA, 4, :], b7[0:SA, 0:P]).then_inc(sem("xnat_ready"), 1)
                if g == 13:
                    dve.wait_ge(sem("pack_tr"), 1)
                    link(dve.tensor_copy(acsH[:], acs[32:40, :]))
                    dve.tensor_copy(pick[:], ident[0:8, 0:H])
                    dve.scalar_tensor_tensor(acsL[:], pack[0:8, :], -1.0, acsH[:].bitcast(f32), ALU.mult, ALU.subtract
                                             ).then_inc(sem("acs_split"), 1)
                if g == 15:
                    dve.wait_ge(sem("q_root"), 1)
                    dve.reciprocal(rq[:], rq[:]).then_inc(sem("rq_ready"), 1)
                if g < B_KV:
                    evac(g, halves(qlat[:, g, :])).then_inc(sem("evac"), 1)
                elif g < B_SP:
                    evac(g, halves(cT[:, g - B_KV, :])).then_inc(sem("evac"), 1)
                elif g == B_SP:
                    dve.wait_ge(sem("gemm_done"), g + 1)
                    dve.tensor_tensor(halves(krw[0:64, :]), acc[g % 2][0:64, :, 0:HALF], halves(rx[0:64, :]),
                                      ALU.mult).then_inc(sem("evac"), 1)
                    dve.wait_ge(sem("evac"), g + 1)
                    dve.wait_ge(sem("vec_arrived"), 16)
                    b = vec[32:40, V_DTB:V_DTB + 1]
                    dve.tensor_scalar(acs[32:40, :], krw[32:40, :], b, 0.0, ALU.add, ALU.max
                                      ).then_inc(sem("dt_pos"), 1)
                elif g < B_Z:
                    c = g - B_X
                    p_, q_ = pad[c % 2], cacc[c % 2]
                    dve.wait_ge(sem("gemm_done"), g + 1)
                    if c >= 2:
                        dve.wait_ge(sem("cn_copied"), 2 * (c - 1))
                        dve.wait_ge(sem("silu_done"), c - 1)
                    else:
                        dve.wait_ge(sem("filled"), 4)
                    A = acc[g % 2]
                    dve.tensor_tensor(p_[:, 3:3 + HALF], A[:, 0, 0:HALF], rx[:, 0:HALF], ALU.mult)
                    dve.tensor_tensor(p_[:, 3 + HALF:3 + TP], A[:, 1, 0:TP - HALF], rx[:, HALF:TP], ALU.mult)
                    dve.tensor_tensor(samp(p_)[:, :, 3:3 + TS],
                                      A[:, 1, TP - HALF:HALF].rearrange("p (b w) -> p b w", w=TS),
                                      rx[:, TP:T].rearrange("p (b w) -> p b w", w=TS),
                                      ALU.mult).then_inc(sem("pad_filled"), 1)
                    dve.wait_ge(sem("pad_filled"), c + 1)
                    dve.wait_ge(sem("pad_state"), c + 1)
                    w = [vec[:, V_CW + CONV_K * c + k:V_CW + CONV_K * c + k + 1] for k in range(CONV_K)]
                    ins = dve.tensor_scalar(q_[:, 0:CW], p_[:, 0:CW], w[0], vec[:, V_CB + c:V_CB + c + 1],
                                            ALU.mult, ALU.add)
                    ins.then_inc(sem("evac"), 1)
                    dve.wait_ge(sem("evac"), g + 1)
                    for k in (1, 2):
                        link(dve.scalar_tensor_tensor(q_[:, 0:CW], p_[:, k:k + CW], w[k], q_[:, 0:CW],
                                                      ALU.mult, ALU.add))
                    dve.scalar_tensor_tensor(q_[:, 0:CW], p_[:, 3:3 + CW], w[3], q_[:, 0:CW],
                                             ALU.mult, ALU.add).then_inc(sem("conv_done"), 1)
                else:
                    evac(g, halves(z[:, g - B_Z, :])).then_inc(sem("evac"), 1)
                if g == 6:
                    dve.wait_ge(sem("q_squared"), 3)
                    dve.wait_ge(sem("dt_ln"), 2)
                    dve.wait_ge(sem("dt_pos"), 1)
                    dve.wait_ge(sem("filled"), 2)
                    link(dve.tensor_tensor(pack[32:40, :], acs[32:40, :], dw[1][32:40, :], ALU.add))
                    link(dve.tensor_scalar(dw[0][32:40, :], pack[32:40, :], vec[32:40, V_AL:V_AL + 1], -1.0,
                                           ALU.mult, ALU.mult))
                    dve.wait_ge(sem("con_arrived"), 32)
                    dve.tensor_tensor_scan(acs[32:40, :], con[32:40, C_RST:C_RST + T], dw[0][32:40, :], 0.0,
                                           ALU.mult, ALU.add).then_inc(sem("acs_ready"), 1)
                    dve.wait_ge(sem("acs_ready"), 1)
                    dve.tensor_scalar(pack[0:8, :], acs[32:40, :], -1.0, None, ALU.mult)
                    dve.tensor_scalar(dw[0][32:40, 0:TP], acs[32:40, 0:TP], -1.0, acs[32:40, TP - 1:TP],
                                      ALU.mult, ALU.add).then_inc(sem("dt_end"), 1)
                    sa = acs[32:40, TP:T].rearrange("p (b w) -> p b w", w=TS)
                    dve.tensor_tensor(dw[0][32:40, TP:T].rearrange("p (b w) -> p b w", w=TS),
                                      sa[:, :, TS - 1:TS].to_broadcast([8, NB, TS]), sa,
                                      ALU.subtract).then_inc(sem("dt_end"), 1)
                if g == 7:
                    dve.wait_ge(sem("q_root"), 2)
                    dve.wait_ge(sem("q_squared"), 5)
                    link(dve.reciprocal(rk[:], rk[:]))
                    for i in range(2):
                        dve.scalar_tensor_tensor(cT[:, i, :], cT[:, i, :], vec[:, V_GKV + i:V_GKV + i + 1],
                                                 rk[:], ALU.mult, ALU.mult).then_inc(sem("c_ready"), 1)
                if g == 8:
                    dve.wait_ge(sem("dt_decay"), 1)
                    dve.tensor_copy(pack[64:72, :], dw[1][32:40, :]).then_inc(sem("pack_ready"), 1)
                    dve.wait_ge(sem("kr_mm"), 1)
                    dve.tensor_tensor(t1[:, 0:HALF], b4[:, 0:HALF], cosT[:, 0:HALF], ALU.mult)
                    link(dve.tensor_tensor(t1[:, HALF:T], b5[:, 0:HALF], cosT[:, HALF:T], ALU.mult))
                    dve.tensor_tensor(krR[:, 0:HALF], b6[:, 0:HALF], sinT[:, 0:HALF], ALU.mult)
                    link(dve.tensor_tensor(krR[:, HALF:T], b7[:, 0:HALF], sinT[:, HALF:T], ALU.mult))
                    dve.tensor_tensor(krR[:], krR[:], t1[:], ALU.add).then_inc(sem("kr_ready"), 1)

            def take_y(j):
                dve.wait_ge(sem("y_mm"), 2 * j + 2)
                dve.scalar_tensor_tensor(xc[:, j, 0:TP], xc[:, j, 0:TP], vec[:, V_D + j:V_D + j + 1],
                                         acc[1][:, j % 2, :], ALU.mult, ALU.add).then_inc(sem("y_taken"), 1)

            dve.wait_ge(sem("pn_ready"), 1)

            def heads(ap):
                return ap.rearrange("p (h n) -> p h n", n=1).to_broadcast([SA, H, SA])

            for h in range(H):
                if h + 1 < H:
                    diag_rows(h + 1)
                dve.wait_ge(sem("ex_done"), h + 1)
                dve.wait_ge(sem("cb_ready"), h // 4 + 1)
                e = ex[h % 4]
                dve.tensor_tensor(e[:], e[:], cbm[:, h // 4, :], ALU.mult).then_inc(sem("mix_ready"), 1)
                if h == 0:
                    causal(1)
                if h >= 3 and h % 2 == 1:
                    take_y(h // 2 - 1)
                if h == 4:
                    dve.wait_ge(sem("srows_done"), 1)
                    link(dve.tensor_tensor(gs[:], b6[0:SA, :].rearrange("p (h n) -> p h n", h=H),
                                           con[0:SA, C_SNEG:C_SNEG + SA].rearrange("p (a n) -> p a n", a=1)
                                           .to_broadcast([SA, H, SA]), ALU.add))
                    dve.tensor_tensor(gs[:], gs[:], heads(pn[0:SA, 4, 0:8]), ALU.add).then_inc(sem("sdiag_ready"), 1)
            take_y(3)
            dve.tensor_tensor(xnat[:, 0:4, :].rearrange("p a (h n) -> p a h n", h=H),
                              xnat[:, 0:4, :].rearrange("p a (h n) -> p a h n", h=H),
                              pn[:, 0:4, 64:72].rearrange("p a (h n) -> p a h n", n=1)
                              .to_broadcast([P, 4, H, DH]), ALU.mult).then_inc(sem("xdd_ready"), 1)
            dve.wait_ge(sem("y_taken"), 4)
            dve.wait_ge(sem("z_silu"), 1)
            for j in range(4):
                dve.tensor_tensor(xc[:, j, 0:TP], xc[:, j, 0:TP], z[:, j, 0:TP], ALU.mult).then_inc(sem("gated"), 1)
            dve.wait_ge(sem("q_squared"), 3)
            for i in range(3):
                gain = vec[:, V_GQ + i:V_GQ + i + 1]
                dve.tensor_scalar(qH[:, i, :], qlat[:, i, :], gain, None, ALU.mult).then_inc(sem("q_split"), 1)
                dve.wait_ge(sem("q_split"), 2 * i + 1)
                dve.scalar_tensor_tensor(qL[:, i, :], qlat[:, i, :], gain, qH[:, i, :].bitcast(f32),
                                         ALU.mult, ALU.subtract).then_inc(sem("q_split"), 1)
            dve.wait_ge(sem("se_mm"), 1)
            dve.wait_ge(sem("mix_ready"), H)
            link(dve.tensor_copy(se[:], b7[:, 0:320]))
            dve.wait_ge(sem("yo_mm"), 1)
            link(dve.tensor_tensor(ysm[:].rearrange("p a n -> p (a n)"), b4[:, 0:256], se[:, 0:256], ALU.mult))
            dve.wait_ge(sem("ys_mm"), 1)
            dve.tensor_tensor(xnat[0:SA, 4, :].rearrange("p (h n) -> p h n", h=H),
                              xnat[0:SA, 4, :].rearrange("p (h n) -> p h n", h=H),
                              pn[0:SA, 4, 64:72].rearrange("p (h n) -> p h n", n=1)
                              .to_broadcast([SA, H, DH]), ALU.mult).then_inc(sem("xdd_ready"), 1)
            link(dve.tensor_tensor(ysm[:].rearrange("p a n -> p (a n)"), b5[:, 0:256],
                                   ysm[:].rearrange("p a n -> p (a n)"), ALU.add))
            for j in range(4):
                m = dve.scalar_tensor_tensor(xc[:, j, TP:T], xc[:, j, TP:T], vec[:, V_D + j:V_D + j + 1],
                                             ysm[:, j, :], ALU.mult, ALU.add)
            m.then_inc(sem("ys_taken"), 1)
            dve.wait_ge(sem("ys_taken"), 1)
            dve.tensor_tensor(xc[:, 0:4, TP:T], xc[:, 0:4, TP:T], z[:, :, TP:T], ALU.mult
                              ).then_inc(sem("gated_sample"), 1)
            dve.wait_ge(sem("h0_arrived"), 32)
            for b in range(NB):
                hb = h0T[:, b, :].rearrange("p (h n) -> p h n", h=H)
                m = dve.tensor_tensor(hb, hb, se[:, 256 + b:320:NB].rearrange("p (h n) -> p h n", n=1)
                                      .to_broadcast([P, H, DH]), ALU.mult)
            link(m)
            for b in range(NB):
                dve.wait_ge(sem("hn_mm"), b + 1)
                dve.tensor_tensor(h0T[:, b, :], h0T[:, b, :], acc[1][:, b % 2, :], ALU.add
                                  ).then_inc(sem("hn_ready"), 1)
                if b == 0:
                    dve.wait_ge(sem("sp_mm"), 1)
                    dve.tensor_copy(spo[:], acc[0][:, 0, :]).then_inc(sem("spo_ready"), 1)
            for c in range(2):
                dve.wait_ge(sem("g_root"), c + 1)
                link(dve.reciprocal(rg[:, c, :], rg[:, c, :]))
                for i in range(2):
                    j = 2 * c + i
                    dve.scalar_tensor_tensor(xc[:, j, :], xc[:, j, :], vec[:, V_GS + j:V_GS + j + 1],
                                             rg[:, c, :], ALU.mult, ALU.mult).then_inc(sem("o_ready"), 1)
            dve.wait_ge(sem("oh_ready"), 4)
            dve.wait_ge(sem("ol_ready"), 4)
            dve.wait_ge(sem("rq_ready"), 1)
            for n, u in enumerate(Q_ORDER):
                dve.wait_ge(sem("q_mm"), n + 1)
                A = acc[n % 2]
                if u < 4:
                    for e in range(2):
                        rows = slice(64 * e, 64 * e + 64)
                        dve.tensor_tensor(QT[0:64, 2 * u + e, 0:HALF], A[rows, 0, 0:HALF], rq[rows, 0:HALF], ALU.mult)
                        dve.tensor_tensor(QT[0:64, 2 * u + e, HALF:TP], A[rows, 1, 0:TP - HALF], rq[rows, HALF:TP],
                                          ALU.mult)
                        m = dve.tensor_tensor(qs[:, 2 * u + e, :], A[rows, 1, TP - HALF:HALF], rq[rows, TP:T],
                                              ALU.mult)
                else:
                    m = dve.tensor_tensor(halves(qp[:, u - 4, :]), A[:, :, 0:HALF], halves(rq[:]), ALU.mult)
                m.then_inc(sem("q_evac"), 1)
            dve.wait_ge(sem("q_evac"), 6)

            def both(ap):
                return ap.rearrange("p (a n) -> p a n", a=1).to_broadcast([P, 2, ap.shape[1]])

            dve.tensor_tensor(tq[0][:], qp[:], both(cosT), ALU.mult)
            dve.wait_ge(sem("rot_mm"), 1)
            for i in range(2):
                dve.tensor_tensor(tq[1][:, i, 0:TP], (b4, b5)[i][:], sinT[:, 0:TP], ALU.mult)
            link(dve.tensor_tensor(tq[1][:, :, TP:T], b6[:, 0:2 * SA].rearrange("p (a n) -> p a n", a=2),
                                   both(sinT[:, TP:T]), ALU.mult))
            dve.wait_ge(sem("out_cn"), 16)
            dve.tensor_tensor(qrs[:], tq[0][:, :, TP:T], tq[1][:, :, TP:T], ALU.add).then_inc(sem("qrs_ready"), 1)
            for h in range(H):
                rows = slice(RP * (h % 4), RP * (h % 4) + RP)
                dve.tensor_tensor(QT[64:96, h, :], tq[0][rows, h // 4, 0:TP], tq[1][rows, h // 4, 0:TP],
                                  ALU.add).then_inc(sem("qrope_ready"), 1)
            dve.wait_ge(sem("snew_mm"), 1)
            dve.tensor_tensor(snew[:], acc[1][0:SA, 0, :], con[0:SA, C_SM:C_SM + 512], ALU.add
                              ).then_inc(sem("snew_ready"), 1)

            sbank = [acc[1][:, 1, 384:512], b7[:, 0:256], acc[1][:, 1, 0:384], acc[1][:, 0, :]]
            am = con[:, C_AM:C_AM + P]
            off = [0, 128, 384, 768, 1280]
            sscore = acc[0][:].rearrange("p a (t q) -> p (a t) q", q=SA)
            dve.wait_ge(sem("out_c"), 16)
            dve.wait_ge(sem("out_sp"), 16)
            for s in range(H):
                dve.wait_ge(sem("score_mm"), s + 1)
                for i in range(QT_N):
                    dve.tensor_tensor(sbank[i][:, P * i:P * i + P], sbank[i][:, P * i:P * i + P], am, ALU.add
                                      ).then_inc(sem("score_masked"), 1)
                for i in range(QT_N):
                    dve.wait_ge(sem("score_masked"), 4 * s + i + 1)
                    m = dve.reduce_max(mx[:, i:i + 1], sbank[i], AX.X, negate=True)
                link(m)
                dve.tensor_scalar(mx[:, 4:8], mx[:, 0:4], SCALE, None, ALU.mult).then_inc(sem("nm_ready"), 1)
                dve.wait_ge(sem("p_exp"), s + 1)
                link(dve.reciprocal(mx[:, 8:12], mx[:, 8:12]))
                for i in range(QT_N):
                    sl = Pm[:, off[i]:off[i + 1]]
                    m = dve.tensor_scalar(sl, sl, mx[:, 8 + i:9 + i], None, ALU.mult)
                m.then_inc(sem("p_norm"), 1)
                sn = snew[:, s * SA:s * SA + SA]
                dve.wait_ge(sem("s_mm"), 4 * s + 2)
                link(dve.reduce_max(mxs[:, SA:P], sscore[:, 0:8, :].rearrange("p t q -> p q t"), AX.X))
                link(dve.tensor_tensor(mxs[0:SA, SA:P], mxs[0:SA, SA:P], sn, ALU.max))
                dve.wait_ge(sem("s_mm"), 4 * s + 4)
                link(dve.reduce_max(mxs[:, 0:SA], sscore[:, 8:16, :].rearrange("p t q -> p q t"), AX.X))
                dve.tensor_tensor(mxs[:, 0:SA], mxs[:, 0:SA], mxs[:, SA:P], ALU.max).then_inc(sem("smax_ready"), 1)
                dve.wait_ge(sem("smax_tr"), s + 1)
                link(dve.reduce_max(rm[:], b6[0:SA, 128:256], AX.X))
                dve.tensor_scalar(dgm[:], ident[0:SA, 0:SA], rm[:], None, ALU.mult).then_inc(sem("sdiag2_ready"), 1)
                dve.wait_ge(sem("smax_mm"), s + 1)
                link(dve.tensor_copy(mxs[:, 0:SA], b6[:, 256:256 + SA]))
                for e in range(2):
                    if e:
                        dve.tensor_tensor(sS[0:SA, 1024:1088], sn, mxs[0:SA, 0:SA], ALU.subtract)
                    dve.tensor_tensor(sS[:, 512 * e:512 * e + 512].rearrange("p (t q) -> p t q", q=SA),
                                      sscore[:, 8 * e:8 * e + 8, :],
                                      mxs[:, 0:SA].rearrange("p (a q) -> p a q", a=1)
                                      .to_broadcast([P, NPG // 2, SA]), ALU.subtract
                                      ).then_inc(sem("shift_ready"), 1)
                dve.wait_ge(sem("pt_mm"), s + 1)
                dve.tensor_copy(PTm[:, 512:1024], acc[1][:, 1, :]).then_inc(sem("pt_dve"), 1)
                dve.wait_ge(sem("sp_exp"), 2 * s + 2)
                link(dve.reduce_sum(psm[:], pS[:, 0:1024].rearrange("p (t q) -> p q t", q=SA), AX.X))
                dve.tensor_tensor(psm[0:SA, :], psm[0:SA, :], pS[0:SA, 1024:1088], ALU.add
                                  ).then_inc(sem("psum_ready"), 1)
                rows = slice(DH * (s % 2), DH * (s % 2) + DH)
                dve.wait_ge(sem("attn_high"), s + 1)
                dve.tensor_tensor(catL[rows, s // 2, 0:TP], acc[1][rows, 0, :],
                                  catH[rows, s // 2, 0:TP].bitcast(f32), ALU.subtract).then_inc(sem("attn_low"), 1)
                dve.wait_ge(sem("den_mm"), s + 1)
                link(dve.reciprocal(rsm[:], b6[:, 320:320 + SA]))
                dve.wait_ge(sem("pv_mm"), s + 1)
                dve.tensor_tensor(olat[:, :, s * SA:s * SA + SA],
                                  b6[:, 0:2 * SA].rearrange("p (a n) -> p a n", a=2), both(rsm[:]), ALU.mult
                                  ).then_inc(sem("olat_ready"), 1)
            dve.wait_ge(sem("osh_ready"), 1)
            dve.tensor_tensor(catL[:, 0:4, TP:T], b5[:, 0:256].rearrange("p (a n) -> p a n", a=4),
                              catH[:, 0:4, TP:T].bitcast(f32), ALU.subtract).then_inc(sem("osl_ready"), 1)

            dve.wait_ge(sem("out_kr"), 16)
            dve.wait_ge(sem("x_again"), 16)
            for d in range(KT):
                g = B_OUT + d
                dve.wait_ge(sem("gemm_done"), g + 1)
                dve.tensor_tensor(halves(xT[:, d, :]), acc[g % 2][:, :, 0:HALF], halves(xT[:, d, :]), ALU.add
                                  ).then_inc(sem("evac"), 1)
                dve.wait_ge(sem("evac"), g + 1)
                gm = vec[:, V_GM + d:V_GM + d + 1]
                dve.tensor_scalar(x2H[:, d, :], xT[:, d, :], gm, None, ALU.mult).then_inc(sem("x2_split"), 1)
                dve.wait_ge(sem("x2_split"), 2 * d + 1)
                dve.scalar_tensor_tensor(x2L[:, d, :], xT[:, d, :], gm, x2H[:, d, :].bitcast(f32),
                                         ALU.mult, ALU.subtract).then_inc(sem("x2_split"), 1)

            def up_out(n, g, u):
                dve.wait_ge(sem("gemm_done"), g + 1)
                dve.wait_ge(sem("ru_free"), n + 1)
                dve.scalar_tensor_tensor(halves(ru[u][:]), acc[u][:, :, 0:HALF], 0.0, halves(r3[:]),
                                         ALU.max, ALU.mult).then_inc(sem("evac"), 1)
                dve.wait_ge(sem("evac"), g + 1)

            def up_high(u, slot):
                dve.tensor_tensor(uH[:, bass.ds(slot, 1), :].rearrange("p a n -> p (a n)"),
                                  ru[u][:], ru[u][:], ALU.mult).then_inc(sem("uh_ready"), 1)

            def down_out(g, u, d):
                x_ = xT[:, bass.ds(d, 1), :].rearrange("p a (h n) -> p (a h) n", h=2)
                dve.wait_ge(sem("gemm_done"), g + 1)
                dve.tensor_tensor(x_, acc[u][:, :, 0:HALF], x_, ALU.add).then_inc(sem("evac"), 1)

            dve.wait_ge(sem("res_root"), 1)
            dve.reciprocal(r3[:], r3[:]).then_inc(sem("r3_ready"), 1)
            dve.wait_ge(sem("r3_ready"), 1)
            def dve_quarter(q, last):
                g0 = q * 16 + B_MLP
                with dve.Fori(0, 4) as j:
                    for u in range(2):
                        up_out(q * 8 + 2 * j + u, g0 + 2 * j + u, u)
                        up_high(u, 2 * j + u)
                with dve.Fori(0, 3 if last else 4) as j:
                    for u in range(2):
                        down_out(g0 + 2 * j + 8 + u, u, 2 * j + u)

            with dve.Fori(0, QUARTERS - 1) as q:
                dve_quarter(q, False)
            dve_quarter(QUARTERS - 1, True)
            dve.wait_ge(sem("gemm_done"), N_BLK - 1)
            dve.tensor_tensor(halves(xT[:, KT - 2, :]), acc[0][:, :, 0:HALF], halves(xT[:, KT - 2, :]), ALU.add
                              ).then_inc(sem("evac"), 1)
            for h in range(2):
                cols = slice(h * HALF, (h + 1) * HALF)
                dve.wait_ge(sem("last_half"), h + 1)
                dve.tensor_tensor(xT[:, KT - 1, cols], (acc[1][:, 0, :], b6)[h][:, 0:HALF], xT[:, KT - 1, cols], ALU.add
                                  ).then_inc(sem("last_evac"), 1)
                if h == 0:
                    dve.wait_ge(sem("res_root"), 2)
                    link(dve.reciprocal(r3[:, cols], r3[:, cols]))
                    dve.wait_ge(sem("last_evac"), 1)
            for h in range(2):
                cols = slice(h * HALF, (h + 1) * HALF)
                if h == 1:
                    dve.wait_ge(sem("res_root"), 3)
                    link(dve.reciprocal(r3[:, cols], r3[:, cols]))
                    dve.wait_ge(sem("last_evac"), 2)
                for d in range(KT):
                    dve.scalar_tensor_tensor(sq2[:, d, cols], xT[:, d, cols], vec[:, V_GF + d:V_GF + d + 1],
                                             r3[:, cols], ALU.mult, ALU.mult).then_inc(sem("y_ready"), 1)

        @block.tensor
        def _(pe):
            def gemm(u, xh, xl, order=range(KT), before=None, part=None):
                n = KT // 2 if part == 1 else 0
                for k in order[:KT // 2] if part == 0 else order[KT // 2:] if part == 1 else order:
                    if before:
                        before(k)
                    for h in range(2):
                        cols = slice(h * HALF, (h + 1) * HALF)
                        for q, (a, b) in enumerate(((whi, xh), (whi, xl), (wlo, xh))):
                            m = pe.matmul(acc[u][:, h, 0:HALF], a[u][:, k, :], b[:, k, cols],
                                          start=n == 0 and q == 0, stop=n == KT - 1 and q == 2)
                    n += 1
                if part != 0:
                    m.then_inc(sem("gemm_done"), 1)

            def block_ready(g):
                pe.wait_ge(sem("w_split"), g + 1)
                if isinstance(g, int) and g < 2:
                    return
                pe.wait_ge(sem("evac"), g - 1)

            def decay_rows(h):
                if h >= 5:
                    pe.wait_ge(sem("ex_done"), h - 3)
                elif h >= 3:
                    pe.wait_ge(sem("cb_ready"), 2)
                elif h >= 1:
                    pe.wait_ge(sem("evac"), N_IN)
                one_head = pick[:, h:h + 1].to_broadcast([8, P])
                pe.matmul(rows_bank[h], one_head, acsH[:, 0:TP], start=True, stop=False)
                pe.matmul(rows_bank[h], one_head, acsL[:, 0:TP], start=False, stop=True
                          ).then_inc(sem("rows_done"), 1)

            for g in range(N_IN):
                if g == N_IN - 1:
                    pe.wait_ge(sem("acs_split"), 1)
                    pe.wait_ge(sem("xnat_ready"), 6)
                    decay_rows(0)
                block_ready(g)
                gemm(g % 2, catH, catL,
                     before=(lambda k: pe.wait_ge(sem("x_split"), 2 * k + 2)) if g == 0 else None)
                if g == 0:
                    pe.wait_ge(sem("filled"), 1)
                    pe.wait_ge(sem("x_added"), 2)
                    for h in range(2):
                        for part, r_ in enumerate((rk, rq)):
                            m = pe.matmul((b4, b5)[h][:, 0:HALF], ones, r_[:, h * HALF:(h + 1) * HALF],
                                          start=part == 0, stop=part == 1)
                    m.then_inc(sem("x_summed"), 1)
                if g == 5:
                    pe.wait_ge(sem("x_root"), 1)
                    for count, src, banks in ((2, sqq[:, 0, :], (b4, b5)), (3, sqq[:, 3, :], (b6, b7))):
                        pe.wait_ge(sem("latent_sum"), count)
                        for h in range(2):
                            m = pe.matmul(banks[h][:, 0:HALF], ones, src[:, h * HALF:(h + 1) * HALF],
                                          start=True, stop=True)
                        m.then_inc(sem("q_summed"), 1)
                if g == 7:
                    pe.wait_ge(sem("con_arrived"), 32)
                    pe.wait_ge(sem("q_root"), 2)
                    for lhs, (ba, bb) in ((con[0:RP, C_REP:C_REP + P], (b4, b5)),
                                          (con[0:RP, C_RREP:C_RREP + P], (b6, b7))):
                        for h, bk in ((0, ba), (1, bb)):
                            m = pe.matmul(bk[:, 0:HALF], lhs, krw[0:RP, h * HALF:(h + 1) * HALF],
                                          start=True, stop=True)
                    m.then_inc(sem("kr_mm"), 1)
                if g == 10:
                    pe.wait_ge(sem("kr_ready"), 1)
                if g == 11:
                    pe.wait_ge(sem("pack_ready"), 1)
                    for i in range(5):
                        n = P if i < 4 else SA
                        m = pe.transpose(b4[0:n, 72 * i:72 * i + 72], pack[0:72, P * i:P * i + n],
                                         ident[0:72, 0:72])
                    m.then_inc(sem("pack_tr"), 1)
                if g >= 10 and g - 10 < 6:
                    c = g - 10
                    pe.wait_ge(sem("silu_done"), c + 1)
                    if c >= 1:
                        pe.wait_ge(sem("xnat_ready"), c)
                    bk = b5 if c % 2 == 0 else b6
                    for i in range(5):
                        n = P if i < 4 else SA
                        m = pe.transpose(bk[:, P * i:P * i + P] if i < 4 else b7[0:SA, 0:P],
                                         xc[:, c, P * i:P * i + n], ident)
                    m.then_inc(sem("x_tr"), 1)
                if g >= 16:
                    c = g - 16
                    pe.wait_ge(sem("silu_done"), KT)
                    pe.wait_ge(sem("xnat_ready"), 6)
                    if c:
                        pe.wait_ge(sem("cb_ready"), 1)
                    for i, (bk, off) in enumerate(((b4, 0), (b5, 0), (b6, 0), (b5, 384))):
                        m = pe.matmul(bk[:, off:off + TP - P * i], xc[:, 4 + c, P * i:P * i + P],
                                      xc[:, 6 + c, P * i:TP], start=True, stop=True)
                    m = pe.matmul(b6[0:SA, 256:256 + SA], xc[:, 4 + c, TP:T], xc[:, 6 + c, TP:T],
                                  start=True, stop=True)
                    m.then_inc(sem("cb_mm"), 1)

            for h in range(1, 3):
                decay_rows(h)
            for h in range(H):
                if h == 1:
                    decay_rows(3)
                if 1 <= h and h + 3 < H:
                    decay_rows(h + 3)
                j = h // 2
                pe.wait_ge(sem("mix_ready"), h + 1)
                if h == 0:
                    pe.wait_ge(sem("xdt_ready"), 1)
                if j >= 2:
                    pe.wait_ge(sem("y_taken"), j - 1)
                for i in range(4):
                    m = pe.matmul(acc[1][64 * (h % 2):64 * (h % 2) + 64, j % 2, P * i:TP],
                                  xnat[:, i, 64 * h:64 * h + 64], ex[h % 4][:, GOFF[i]:GOFF[i + 1]],
                                  start=i == 0, stop=i == 3)
                m.then_inc(sem("y_mm"), 1)
                if h == 1:
                    pe.wait_ge(sem("dt_decay"), 2)
                    for e in range(H):
                        m = pe.matmul(b6[0:SA, SA * e:SA * e + SA], ident[32:40, 32 + e:33 + e].to_broadcast([8, SA]),
                                      acs[32:40, TP:T], start=True, stop=True)
                    m.then_inc(sem("srows_done"), 1)
                    e8 = pack[96:104, :]
                    for e in range(H):
                        sel = ident[96:104, 96 + e:97 + e]
                        pe.matmul(b7[64 * (e % 2):64 * (e % 2) + 64, SA * (e // 2):SA * (e // 2) + SA],
                                  sel.to_broadcast([8, 64]), e8[:, TP:T], start=True, stop=True)
                    for e in range(H):
                        sel = ident[96:104, 96 + e:97 + e]
                        m = pe.matmul(b7[:, 256 + NB * e:256 + NB * e + NB], sel.to_broadcast([8, P]),
                                      e8[:, TP + TS - 1:T:TS], start=True, stop=True)
                    m.then_inc(sem("se_mm"), 1)
            pe.wait_ge(sem("h0_arrived"), 32)
            for b in range(NB):
                for j in range(4):
                    m = pe.matmul(b4[:, SA * j + TS * b:SA * j + TS * b + TS], h0T[:, b, P * j:P * j + P],
                                  xc[:, 6 + j // 2, TP + TS * b:TP + TS * b + TS], start=True, stop=True)
            m.then_inc(sem("yo_mm"), 1)
            pe.wait_ge(sem("smix_ready"), 1)
            for h in range(H):
                m = pe.matmul(b5[64 * (h % 2):64 * (h % 2) + 64, SA * (h // 2):SA * (h // 2) + SA],
                              xnat[0:SA, 4, 64 * h:64 * h + 64], gs[:, h, :], start=True, stop=True)
            m.then_inc(sem("ys_mm"), 1)
            pe.wait_ge(sem("xdd_ready"), 1)
            for c in range(2):
                for i in range(4):
                    m = pe.matmul(acc[0][:, 0, 256 * c:256 * c + 256], bnat[:, i, P * c:P * c + P],
                                  xnat[:, i, 256 * c:256 * c + 256], start=i == 0, stop=i == 3)
            m.then_inc(sem("sp_mm"), 1)
            pe.wait_ge(sem("bms_ready"), NB)
            pe.wait_ge(sem("xdd_ready"), 2)
            pe.wait_ge(sem("y_taken"), 4)
            for b in range(NB):
                if b >= 2:
                    pe.wait_ge(sem("hn_ready"), b - 1)
                for c in range(2):
                    m = pe.matmul(acc[1][:, b % 2, 256 * c:256 * c + 256], bms[:, b, P * c:P * c + P],
                                  xnat[0:SA, 4, 256 * c:256 * c + 256], start=True, stop=True)
                m.then_inc(sem("hn_mm"), 1)
            pe.wait_ge(sem("ys_taken"), 1)
            pe.wait_ge(sem("g_squared"), 1)
            for c in range(2):
                for h, bk in ((0, (b4, b6)[c]), (1, (b5, b7)[c])):
                    for i in range(2):
                        m = pe.matmul(bk[:, 0:HALF], ones, z[:, 2 * c + i, h * HALF:(h + 1) * HALF],
                                      start=i == 0, stop=i == 1)
                m.then_inc(sem("g_summed"), 1)
            pe.wait_ge(sem("hn_ready"), NB)
            pe.wait_ge(sem("spo_ready"), 1)
            pe.wait_ge(sem("small_weights"), 64)
            for u in range(8):
                if u >= 2:
                    pe.wait_ge(sem("kv_evac"), u - 1)
                for k in range(2):
                    if u < 4:
                        lhs, rhs = wukT[:, k, P * u:P * u + P], cT[:, k, 0:TP]
                    else:
                        lhs, rhs = cT[:, k, P * (u - 4):P * (u - 3)], wuv[:, k, :]
                    m = pe.matmul(acc[u % 2][:, 0, :], lhs, rhs, start=k == 0, stop=k == 1)
                m.then_inc(sem("kv_mm"), 1)
            pe.wait_ge(sem("q_split"), 6)
            pe.wait_ge(sem("wuq_split"), 1)
            for n, u in enumerate(Q_ORDER):
                if n == 4:
                    pe.wait_ge(sem("g_root"), 2)
                    pe.wait_ge(sem("q_evac"), 2)
                    for i in range(2):
                        pe.matmul((b4, b5)[i][:], rot, qp[:, i, 0:TP], start=True, stop=True)
                        m = pe.matmul(b6[:, SA * i:SA * i + SA], rot, qp[:, i, TP:T], start=True, stop=True)
                    m.then_inc(sem("rot_mm"), 1)
                if n < 2:
                    pe.wait_ge(sem("kv_evac"), 7 + n)
                else:
                    pe.wait_ge(sem("q_evac"), n - 1)
                cols = slice(P * u, P * u + P)
                for k in range(3):
                    for h in range(2):
                        for q, (a, b) in enumerate(((wuqH, qH), (wuqH, qL), (wuqL, qH))):
                            m = pe.matmul(acc[n % 2][:, h, 0:HALF], a[:, k, cols], b[:, k, h * HALF:(h + 1) * HALF],
                                          start=k == 0 and q == 0, stop=k == 2 and q == 2)
                m.then_inc(sem("q_mm"), 1)
            pe.wait_ge(sem("q_evac"), 6)
            for h in range(H):
                for k in range(2):
                    m = pe.matmul(acc[0][:, k, SA * h:SA * h + SA], wuk[:, h, P * k:P * k + P], qs[:, h, :],
                                  start=True, stop=True)
            m.then_inc(sem("qabs_mm"), 1)
            pe.wait_ge(sem("qrs_ready"), 1)
            for h in range(H):
                m = pe.matmul(b7[:, SA * h:SA * h + SA], con[:, C_REP + P * (h % 4):C_REP + P * (h % 4) + P],
                              qrs[:, h // 4, :], start=True, stop=True)
            m.then_inc(sem("qps_mm"), 1)
            for k in range(2):
                m = pe.transpose(b6[0:SA, P * k:P * k + P], cT[:, k, TP:T], ident)
            m.then_inc(sem("c64_mm"), 1)

            def turns(b, quads):
                u = b % 2
                for q in quads:
                    if q in (0, 4):
                        pe.wait_ge(sem(f"cache{u}_half{q // 4}"), NPG // 2 * 16 * (b // 2 + 1))
                    if q == 8:
                        pe.wait_ge(sem(f"cache{u}_rotary"), NPG * 16 * (b // 2 + 1))
                    if b * 9 + q >= 2:
                        pe.wait_ge(sem("ct_evac"), b * 9 + q - 1)
                    for j in range(4):
                        if q < 8:
                            src = ckv[u][:, 2 * q + j // 2, P * (j % 2):P * (j % 2) + P]
                        else:
                            src = ckr[u][:, 4 * j:4 * j + 4, :].rearrange("p a n -> p (a n)")
                        m = pe.transpose((b4, b5)[(b + q) % 2][:, P * j:P * j + P], src, ident)
                    m.then_inc(sem("ct_mm"), 1)

            def turn_probs(s):
                pe.wait_ge(sem("p_norm"), s + 1)
                for k in range(QT_N):
                    for i in range(k, QT_N):
                        c = GOFF[k] + P * (i - k)
                        m = pe.transpose((acc[1][:, 0, :], acc[1][:, 1, :], b7)[c // 512][:, c % 512:c % 512 + P],
                                         Pm[:, off[i] + P * k:off[i] + P * k + P], ident)
                m.then_inc(sem("pt_mm"), 1)

            sbank = [acc[1][:, 1, 384:512], b7[:, 0:256], acc[1][:, 1, 0:384], acc[1][:, 0, :]]
            off = [0, 128, 384, 768]
            turns(0, range(0, 4))
            pe.wait_ge(sem("qabs_ready"), 2)
            pe.wait_ge(sem("qps_ready"), 1)
            for k in range(2):
                pe.matmul(acc[1][0:SA, 0, :], cT[:, k, TP:T], qabs[:, k, :], start=k == 0, stop=False)
            pe.matmul(acc[1][0:SA, 0, :], krR[0:RP, TP:T], qps[0:RP, :], start=False, stop=True
                      ).then_inc(sem("snew_mm"), 1)
            turns(0, range(4, 9))
            pe.wait_ge(sem("qrope_ready"), H)
            pe.wait_ge(sem("krope_ready"), 1)
            for s in range(H):
                for i in range(QT_N):
                    if s == 0 and i == QT_N - 1:
                        pe.wait_ge(sem("snew_ready"), 1)
                    if s and i == QT_N - 1:
                        pe.wait_ge(sem("attn_low"), s)
                    m = pe.matmul(sbank[i], QT[:, s, P * i:P * i + P], KTt[:, s, 0:P * (i + 1)],
                                  start=True, stop=True)
                m.then_inc(sem("score_mm"), 1)
                pe.wait_ge(sem("ct_evac"), s * 9 + 9)
                pe.wait_ge(sem("qb_ready"), s + 1)
                for a in range(NPG // 4):
                    pe.matmul(acc[0][:, a // 2, 256 * (a % 2):256 * (a % 2) + 256], KRr[:, a, :],
                              qpb[:].rearrange("p a n -> p (a n)"), start=True, stop=False)
                    for t in range(4 * a, 4 * a + 4):
                        for k in range(2):
                            m = pe.matmul(acc[0][:, t // 8, SA * (t % 8):SA * (t % 8) + SA],
                                          CTr[:, k, P * t:P * t + P], qabs[:, k, s * SA:s * SA + SA],
                                          start=False, stop=k == 1 and t % 4 == 3)
                    m.then_inc(sem("s_mm"), 1)
                    if s + 1 < NB and a in (1, 2):
                        turns(s + 1, range(2 * a - 2, 2 * a))
                if s + 1 < NB:
                    turns(s + 1, range(4, 6))
                else:
                    turn_probs(s)
                if s == 0:
                    pe.wait_ge(sem("c64_ready"), 1)
                pe.wait_ge(sem("smax_ready"), s + 1)
                pe.transpose(b6[:, 128:256], mxs[:], ident).then_inc(sem("smax_tr"), 1)
                if s + 1 < NB:
                    turns(s + 1, range(6, 8))
                pe.wait_ge(sem("sdiag2_ready"), s + 1)
                pe.matmul(b6[:, 256:256 + SA], ones[0:SA, :], dgm[:], start=True, stop=True
                          ).then_inc(sem("smax_mm"), 1)
                if s + 1 < NB:
                    turn_probs(s)
                for k in range(2):
                    for t in range(NPG):
                        if k == 0 and t % (NPG // 2) == 0:
                            pe.wait_ge(sem("sp_exp"), 2 * s + 2 * t // NPG + 1)
                        pe.matmul(b6[:, SA * k:SA * k + SA], ckv[s % 2][:, t, P * k:P * k + P],
                                  pS[:, SA * t:SA * t + SA], start=t == 0, stop=False)
                    m = pe.matmul(b6[:, SA * k:SA * k + SA], c64[:, P * k:P * k + P], pS[0:SA, 1024:1088],
                                  start=False, stop=True)
                m.then_inc(sem("pv_mm"), 1)
                if s + 1 < NB:
                    turns(s + 1, [8])
                pe.wait_ge(sem("pt_act"), s + 1)
                pe.wait_ge(sem("pt_dve"), s + 1)
                for k in range(QT_N):
                    m = pe.matmul(acc[1][DH * (s % 2):DH * (s % 2) + DH, 0, P * k:TP], V[:, k, DH * s:DH * s + DH],
                                  PTm[:, GOFF[k]:GOFF[k + 1]], start=k == 0, stop=k == 3)
                m.then_inc(sem("o_mm"), 1)
                pe.wait_ge(sem("psum_ready"), s + 1)
                pe.matmul(b6[:, 320:320 + SA], ones, psm[:], start=True, stop=True).then_inc(sem("den_mm"), 1)

            order = [4, 5, 6, 7, 0, 1, 2, 3]
            pe.wait_ge(sem("oh_ready"), 4)
            pe.wait_ge(sem("ol_ready"), 4)
            block_ready(B_OUT)
            gemm(0, catH, catL, order, part=0)
            pe.wait_ge(sem("olat_ready"), NB)
            for h in range(H):
                for k in range(2):
                    rhs = olat[:, k, :].rearrange("p (b h t) -> p h b t", b=NB, h=H)[:, h, :, :]
                    m = pe.matmul(b5[64 * (h % 2):64 * (h % 2) + 64, SA * (h // 2):SA * (h // 2) + SA],
                                  wuv[:, k, 64 * h:64 * h + 64], rhs, start=k == 0, stop=k == 1)
            m.then_inc(sem("os_mm"), 1)
            block_ready(B_OUT + 1)
            gemm(1, catH, catL, order, part=0)
            pe.wait_ge(sem("osl_ready"), 1)
            for u in range(2):
                gemm(u, catH, catL, order, part=1)
            for g in range(B_OUT + 2, B_MLP):
                block_ready(g)
                gemm(g % 2, catH, catL, order)

            def up(g, u, before=None):
                block_ready(g)
                gemm(u, x2H, x2L, before=before)

            def down(g, u, q, first):
                block_ready(g)
                gemm(u, uH, uL, before=(lambda k: pe.wait_ge(sem("ul_ready"), q * 8 + k + 3)) if first else None)

            def quarter(q, peel, last=False):
                g0 = q * 16 + B_MLP
                if peel:
                    up(g0, 0, before=lambda k: pe.wait_ge(sem("x2_split"), 2 * k + 2))
                    pe.wait_ge(sem("res_summed"), 1)
                    for h in range(2):
                        m = pe.matmul((b4, b5)[h][:, 0:HALF], ones, r2[:, h * HALF:(h + 1) * HALF],
                                      start=True, stop=True)
                    m.then_inc(sem("res_sum_mm"), 1)
                    up(g0 + 1, 1)
                else:
                    up(g0, 0)
                    up(g0 + 1, 1)
                with pe.Fori(1, 4) as j:
                    up(g0 + 2 * j, 0)
                    up(g0 + 2 * j + 1, 1)
                down(g0 + 8, 0, q, True)
                down(g0 + 9, 1, q, False)
                with pe.Fori(1, 3) as j:
                    down(g0 + 2 * j + 8, 0, q, False)
                    down(g0 + 2 * j + 9, 1, q, False)
                down(g0 + 14, 0, q, False)
                if not last:
                    down(g0 + 15, 1, q, False)

            quarter(0, True)
            with pe.Fori(1, QUARTERS - 1) as q:
                quarter(q, False)
            quarter(QUARTERS - 1, False, last=True)
            def norm_sums(h):
                cols = slice(h * HALF, (h + 1) * HALF)
                pe.wait_ge(sem("res_summed"), 2)
                pe.matmul((b4, b5)[h][:, 0:HALF], ones, r2[:, cols], start=True, stop=False)
                pe.wait_ge(sem("last_squared"), h + 1)
                pe.matmul((b4, b5)[h][:, 0:HALF], ones, sq2[:, KT - 1, cols], start=False, stop=True
                          ).then_inc(sem("res_sum_mm"), 1)

            block_ready(N_BLK - 1)
            for h in range(2):
                for k in range(KT):
                    if h == 1 and k == KT // 2:
                        norm_sums(0)
                    for q, (a, b) in enumerate(((whi, uH), (whi, uL), (wlo, uH))):
                        m = pe.matmul((acc[1][:, 0, :], b6)[h][:, 0:HALF], a[1][:, k, :],
                                      b[:, k, h * HALF:(h + 1) * HALF],
                                      start=k == 0 and q == 0, stop=k == KT - 1 and q == 2)
                m.then_inc(sem("last_half"), 1)
            norm_sums(1)


_SHAPES = [((P, KT, T), "y"), ((P, 2, T), "c"), ((RP, T), "kr"), ((P, 512), "ssm_p"),
           ((P, NB, 512), "ssm_s"), ((P, KT, 27), "conv")]


def layouts(i):
    import numpy as np
    c = np.ascontiguousarray

    def blocks(w):
        k, n = w.shape[0] // P, w.shape[1] // P
        return w.reshape(k, P, n, P).transpose(2, 1, 0, 3).reshape(n, P, k * P)

    def columns(v):
        return v.reshape(-1, P).T

    w_in, w_up, w_down = i["w_in"][0], i["w_up"][0], i["w_down"][0]
    e = np.cumsum([QL, CL, RP, 512, 1024, 8])
    q, kv, kpe, zz, xbc, dt = np.split(w_in, e[:-1], axis=1)
    special = np.concatenate([kpe, dt, np.zeros((D, P - RP - 8), w_in.dtype)], axis=1)
    parts = [blocks(a) for a in (q, kv, special, xbc, zz)] + [blocks(i["w_out"][0])]
    fq = w_up.shape[1] // QUARTERS
    for n in range(QUARTERS):
        parts += [blocks(w_up[:, n * fq:(n + 1) * fq]), blocks(w_down[n * fq:(n + 1) * fq])]
    x = np.concatenate([i["x_prompt"].reshape(TP, D), i["x_sample"].reshape(SA, D)], axis=0)
    wuq = i["w_uq"][0].reshape(QL, H, 96)
    wuq = np.concatenate([wuq[:, :, :64].reshape(QL, 512), wuq[:, :, 64:].reshape(QL, 256)], axis=1)
    vec = np.zeros((P, NV), np.float32)
    vec[:, V_GATT:V_GATT + 8] = columns(i["norm_attn"][0])
    vec[:, V_GQ:V_GQ + 3] = columns(i["q_norm"][0])
    vec[:, V_GKV:V_GKV + 2] = columns(i["kv_norm"][0])
    vec[:, V_CW:V_CW + 32] = i["conv_w"][0].reshape(CONV_K, KT, P).transpose(2, 1, 0).reshape(P, 32)
    vec[:, V_CB:V_CB + 8] = columns(i["conv_b"][0])
    vec[:, V_GS:V_GS + 4] = columns(i["ssm_norm"][0])
    vec[:, V_GM:V_GM + 8] = columns(i["norm_mlp"][0])
    vec[:, V_GF:V_GF + 8] = columns(i["norm_final"])
    vec[:, V_D:V_D + 4] = columns(np.repeat(i["d_skip"][0], DH))
    vec[32:40, V_DTB] = i["dt_bias"][0]
    vec[32:40, V_AL] = i["a_log"][0]
    vec[:, V_EPS] = EPS
    s = np.arange(P)
    for b in range(NB):
        vec[:SA, V_BM + b] = (s[:SA] // TS == b)
    for a in range(4):
        vec[:, V_QM + a] = (s // RP == a)
    return {
        "wst": c(np.concatenate(parts, axis=0)),
        "x": c(x.T.reshape(KT, P, T).transpose(1, 0, 2)),
        "kv": c(i["cache_kv_latent"][0]), "kr": c(i["cache_k_rope"][0]),
        "h0": c(i["state_ssm"][0].reshape(NB, 512, NST).transpose(2, 0, 1)),
        "sc": c(i["state_conv"][0].reshape(NB, 3, KT, P).transpose(3, 2, 0, 1)),
        "wuq": c(wuq.reshape(3, P, 768).transpose(1, 0, 2)),
        "wukT": c(i["w_uk"][0].transpose(2, 0, 1).reshape(2, P, 512).transpose(1, 0, 2)),
        "wuk": c(i["w_uk"][0].transpose(1, 0, 2)),
        "wuv": c(i["w_uv"][0].transpose(1, 0, 2).reshape(2, P, 512).transpose(1, 0, 2)),
        "vec": vec, "con": constants(), "pt": c(i["page_table"].reshape(1, NB * NPG)),
    }


def constants():
    import numpy as np
    con = np.zeros((P, NC_), np.float32)
    p = np.arange(P)
    con[:, C_ID:C_ID + P] = np.eye(P)
    con[:, C_ONE:C_ONE + P] = 1.0
    swap = (p // RP) * RP + (p % RP + RP // 2) % RP
    con[p, C_ROT + swap] = 1.0
    for a in range(4):
        con[RP * a + p % RP, C_REP + P * a + p] = 1.0
    con[(p % RP + RP // 2) % RP, C_RREP + p] = 1.0
    con[:, C_AM:C_AM + P] = np.where(p[None, :] <= p[:, None], 0, NEG)
    con[:, C_TRI:C_TRI + P] = p[None, :] >= p[:, None]
    con[:, C_NEG:C_NEG + P] = np.where(p[None, :] >= p[:, None], 0, NEG)
    s = np.arange(SA)
    same = (s[:, None] // TS == s[None, :] // TS) & (s[None, :] >= s[:, None])
    con[:SA, C_SNEG:C_SNEG + SA] = np.where(same, 0, NEG)
    pos = np.concatenate([np.arange(TP), np.tile(PAST + np.arange(TS), NB)]).astype(np.float32)
    inv = (np.float32(10000.0) ** (-(np.arange(0, RP, 2, dtype=np.float32) / RP))).astype(np.float32)
    ang = (pos[:, None] * inv[None, :]).astype(np.float32)
    con[:, C_COS:C_COS + T] = np.cos(ang)[:, p % 16].T
    con[:, C_SIN:C_SIN + T] = np.sin(ang)[:, p % 16].T * np.where(p % RP < 16, -1, 1)[:, None]
    m = same.reshape(SA, NB, 1, TS)
    con[:SA, C_SM:C_SM + 512] = np.broadcast_to(np.where(m, 0, NEG), (SA, NB, H, TS)).reshape(SA, 512)
    rst = np.ones(T)
    rst[0] = 0
    rst[TP::TS] = 0
    con[:, C_RST:C_RST + T] = rst
    return con


def kernel(**inputs):
    import numpy as np
    import concourse.bacc as bacc
    from concourse.bass_utils import run_bass_kernel_spmd as run

    nc = bacc.Bacc("TRN2", target_bir_lowering=False, num_devices=1)
    arrays, args = {}, []
    for name, a in layouts({k: np.asarray(v) for k, v in inputs.items()}).items():
        arrays["in_" + name] = a
        args.append(nc.dram_tensor("in_" + name, a.shape, mybir.dt.from_np(a.dtype), kind="ExternalInput").ap())
    for shape, name in _SHAPES:
        args.append(nc.dram_tensor("out_" + name, shape, mybir.dt.float32, kind="ExternalOutput").ap())
    build(nc, *args)
    r = run(nc, [arrays], core_ids=[0]).results[0]
    y = r["out_y"].transpose(2, 1, 0).reshape(T, D)
    c = r["out_c"].transpose(2, 1, 0).reshape(T, CL)
    kr = r["out_kr"].T
    sp = r["out_ssm_p"].T
    ss = r["out_ssm_s"].transpose(1, 2, 0)
    cn = r["out_conv"].transpose(2, 1, 0).reshape(27, D)
    return (y[:TP].reshape(1, TP, D), y[TP:].reshape(NB, TS, D),
            c[:TP].reshape(1, 1, TP, CL), kr[:TP].reshape(1, 1, TP, RP),
            sp.reshape(1, 1, H, DH, NST), cn[:3].reshape(1, 1, 3, D),
            c[TP:].reshape(1, NB, TS, CL), kr[TP:].reshape(1, NB, TS, RP),
            ss.reshape(1, NB, H, DH, NST), cn[3:].reshape(1, NB, 3, D))
```
